# Optimizing a Trainium2 kernel written in Bass

```python
import jax, jax.numpy as jnp
from jax import lax
import numpy as np
import math
import jax
import jax.numpy as jnp

D_MODEL = 1024
BATCH = 1
SEQ = 256
DEPTH = 1

PLE_DIM = 256
BRANCH_WIDTH = D_MODEL // 2
N_BRANCH = 3
FOX_HEAD_DIM = 64
FOX_HEADS = BRANCH_WIDTH // FOX_HEAD_DIM
FOX_WIDTH = FOX_HEADS * FOX_HEAD_DIM
FOX_BLOCK = 128
SC_WIDTH = BRANCH_WIDTH
SC_KERNEL = 3
DN_HEAD_DIM = 128
DN_HEADS = BRANCH_WIDTH // DN_HEAD_DIM
DN_WIDTH = DN_HEADS * DN_HEAD_DIM
DN_CONV = 4
DN_CHUNK = 64
D_FF = 128 * ((8 * D_MODEL // 3 + 127) // 128)
FFN_CONV = 3
EPS = 1e-6

IN_SIZES = (3 * FOX_WIDTH, FOX_HEADS, 3 * SC_WIDTH, 3 * DN_WIDTH, DN_HEADS, DN_HEADS, DN_WIDTH, N_BRANCH * D_MODEL)
IN_WIDTH = sum(IN_SIZES)


def split_cols(t, sizes):
    offs = []
    acc = 0
    for s in sizes[:-1]:
        acc += s
        offs.append(acc)
    return jnp.split(t, offs, axis=-1)

def rmsnorm(x, gain):
    xf = x.astype(jnp.float32)
    y = xf * lax.rsqrt(jnp.mean(xf * xf, axis=-1, keepdims=True) + EPS)
    return (y * gain.astype(jnp.float32)).astype(x.dtype)

def l2norm(x):
    xf = x.astype(jnp.float32)
    return xf * lax.rsqrt(jnp.sum(xf * xf, axis=-1, keepdims=True) + EPS)

def causal_dwconv(x, w):
    k_width, chans = w.shape
    return lax.conv_general_dilated(x, w[:, None, :].astype(x.dtype), window_strides=(1,),
                                    padding=[(k_width - 1, 0)],
                                    dimension_numbers=('NWC', 'WIO', 'NWC'),
                                    feature_group_count=chans)

def forgetting_attention(q, k, v, f_logit, b_f, q_gain, k_gain):
    seq = q.shape[1]
    dh = q.shape[-1]
    q = rmsnorm(q, q_gain).transpose(0, 2, 1, 3)
    k = rmsnorm(k, k_gain).transpose(0, 2, 1, 3)
    v = v.transpose(0, 2, 1, 3)
    log_f = jax.nn.log_sigmoid(f_logit.astype(jnp.float32) + b_f.astype(jnp.float32))
    cum_f = jnp.cumsum(log_f, axis=1).transpose(0, 2, 1)
    scale = dh ** -0.5
    outs = []
    for start in range(0, seq, FOX_BLOCK):
        end = start + FOX_BLOCK
        s = jnp.einsum('bhqd,bhkd->bhqk', q[:, :, start:end], k[:, :, :end],
                       preferred_element_type=jnp.float32) * scale
        s = s + cum_f[:, :, start:end, None] - cum_f[:, :, None, :end]
        causal = jnp.arange(start, end)[:, None] >= jnp.arange(end)[None, :]
        s = jnp.where(causal, s, -jnp.inf)
        pr = jax.nn.softmax(s, axis=-1).astype(v.dtype)
        outs.append(jnp.einsum('bhqk,bhkd->bqhd', pr, v[:, :, :end]))
    return jnp.concatenate(outs, axis=1)

def gated_delta_rule(q, k, v, g, beta):
    bsz, seq, heads, dk = q.shape
    dv = v.shape[-1]
    c = DN_CHUNK
    n_chunks = seq // c

    def to_chunks(t):
        return t.astype(jnp.float32).reshape(bsz, n_chunks, c, heads, -1).transpose(1, 0, 3, 2, 4)

    qc = to_chunks(q) * dk ** -0.5
    kc = to_chunks(k)
    vc = to_chunks(v)
    gc = to_chunks(g[..., None])[..., 0]
    bc = to_chunks(beta[..., None])[..., 0]
    gcum = jnp.cumsum(gc, axis=-1)
    incl = jnp.tril(jnp.ones((c, c), dtype=bool))
    strict = jnp.tril(jnp.ones((c, c), dtype=bool), k=-1)
    decay = jnp.exp(jnp.where(incl, gcum[..., :, None] - gcum[..., None, :], -jnp.inf))
    kb = kc * bc[..., None]
    a_mat = jnp.where(strict, jnp.einsum('nbhid,nbhjd->nbhij', kb, kc) * decay, 0.0) \
        + jnp.eye(c, dtype=jnp.float32)
    rhs = jnp.concatenate([vc * bc[..., None], kb * jnp.exp(gcum)[..., None]], axis=-1)
    sol = lax.linalg.triangular_solve(a_mat, rhs, left_side=True, lower=True, unit_diagonal=True)
    u_val, k_cum = sol[..., :dv], sol[..., dv:]
    qk = jnp.where(incl, jnp.einsum('nbhid,nbhjd->nbhij', qc, kc) * decay, 0.0)
    q_dec = qc * jnp.exp(gcum)[..., None]
    k_dec = kc * jnp.exp(gcum[..., -1:] - gcum)[..., None]
    g_tot = jnp.exp(gcum[..., -1])

    def step(state, xs):
        u_i, kcum_i, qk_i, qdec_i, kdec_i, gtot_i = xs
        v_new = u_i - jnp.einsum('bhck,bhkv->bhcv', kcum_i, state)
        out = jnp.einsum('bhck,bhkv->bhcv', qdec_i, state) + jnp.einsum('bhij,bhjv->bhiv', qk_i, v_new)
        state = state * gtot_i[..., None, None] + jnp.einsum('bhck,bhcv->bhkv', kdec_i, v_new)
        return state, out

    state0 = jnp.zeros((bsz, heads, dk, dv), jnp.float32)
    _, out = lax.scan(step, state0, (u_val, k_cum, qk, q_dec, k_dec, g_tot))
    return out.transpose(1, 0, 3, 2, 4).reshape(bsz, seq, heads, dv)

def hybrid_layer(x, p_i, g_mix, w_in, b_fox_f, fox_q_gain, fox_k_gain, sc_conv_w, dn_conv_w,
                 dn_a_log, dn_dt_bias, dn_norm_gain, w_branch, w_o, g_ffn, w_up, ffn_conv_w,
                 w_down, g_ple, w_ple_gate, w_ple):
    bsz, seq, _ = x.shape
    h = rmsnorm(x, g_mix)
    proj = h @ w_in
    fox_qkv, fox_f, sc_bcv, dn_qkv, dn_b, dn_a, dn_z, br_gate = split_cols(proj, IN_SIZES)

    fq, fk, fv = [t.reshape(bsz, seq, FOX_HEADS, FOX_HEAD_DIM) for t in jnp.split(fox_qkv, 3, axis=-1)]
    y_fox = forgetting_attention(fq, fk, fv, fox_f, b_fox_f, fox_q_gain, fox_k_gain)
    y_fox = y_fox.reshape(bsz, seq, FOX_WIDTH)

    sb, sc, sv = jnp.split(sc_bcv, 3, axis=-1)
    y_sc = sb * causal_dwconv(sc * sv, sc_conv_w)

    dn_qkv = jax.nn.silu(causal_dwconv(dn_qkv, dn_conv_w))
    dq, dk_, dv_ = [t.reshape(bsz, seq, DN_HEADS, DN_HEAD_DIM) for t in jnp.split(dn_qkv, 3, axis=-1)]
    beta = jax.nn.sigmoid(dn_b.astype(jnp.float32))
    g = -jnp.exp(dn_a_log.astype(jnp.float32)) * jax.nn.softplus(dn_a.astype(jnp.float32) + dn_dt_bias.astype(jnp.float32))
    o_dn = gated_delta_rule(l2norm(dq), l2norm(dk_), dv_, g, beta).astype(x.dtype)
    z = dn_z.reshape(bsz, seq, DN_HEADS, DN_HEAD_DIM)
    y_dn = (rmsnorm(o_dn, dn_norm_gain) * jax.nn.silu(z)).reshape(bsz, seq, DN_WIDTH)

    ys = jnp.stack([y_fox, y_sc, y_dn], axis=2)
    gates = jax.nn.sigmoid(br_gate).reshape(bsz, seq, N_BRANCH, D_MODEL)
    merged = jnp.sum(jnp.einsum('bsnc,ncd->bsnd', ys, w_branch) * gates, axis=2)
    x = x + merged @ w_o

    u = causal_dwconv(rmsnorm(x, g_ffn) @ w_up, ffn_conv_w)
    u_gate, u_val = jnp.split(u, 2, axis=-1)
    x = x + (jax.nn.silu(u_gate) * u_val) @ w_down

    x = x + jax.nn.sigmoid(rmsnorm(x, g_ple) @ w_ple_gate) * (p_i.astype(x.dtype) @ w_ple)
    return x

def first_inputs(seed: int = 0) -> dict:
    key = jax.random.key(seed)
    ks = jax.random.split(key, 24)
    f32 = jnp.float32

    def nrm(k, shape, scale):
        return jax.random.normal(k, shape, f32) * scale

    def gain(k, shape):
        return 1.0 + 0.02 * jax.random.normal(k, shape, f32)

    x = nrm(ks[0], (BATCH, SEQ, D_MODEL), 1.0)
    p = nrm(ks[1], (DEPTH, BATCH, SEQ, PLE_DIM), 1.0)
    g_mix = gain(ks[2], (DEPTH, D_MODEL))
    w_in = nrm(ks[3], (DEPTH, D_MODEL, IN_WIDTH), D_MODEL ** -0.5)
    b_fox_f = jnp.linspace(1.0, 5.0, FOX_HEADS, dtype=f32)[None, :] + nrm(ks[4], (DEPTH, FOX_HEADS), 0.1)
    fox_q_gain = gain(ks[5], (DEPTH, FOX_HEAD_DIM))
    fox_k_gain = gain(ks[6], (DEPTH, FOX_HEAD_DIM))
    sc_conv_w = nrm(ks[7], (DEPTH, SC_KERNEL, SC_WIDTH), SC_KERNEL ** -0.5)
    dn_conv_w = nrm(ks[8], (DEPTH, DN_CONV, 3 * DN_WIDTH), DN_CONV ** -0.5)
    dn_a_log = jnp.log(jax.random.uniform(ks[9], (DEPTH, DN_HEADS), f32, 1.0, 16.0))
    dt = jnp.exp(jax.random.uniform(ks[10], (DEPTH, DN_HEADS), f32, float(np.log(1e-3)), float(np.log(1e-1))))
    dn_dt_bias = dt + jnp.log(-jnp.expm1(-dt))
    dn_norm_gain = gain(ks[11], (DEPTH, DN_HEAD_DIM))
    w_branch = nrm(ks[12], (DEPTH, N_BRANCH, BRANCH_WIDTH, D_MODEL), BRANCH_WIDTH ** -0.5)
    w_o = nrm(ks[13], (DEPTH, D_MODEL, D_MODEL), D_MODEL ** -0.5)
    g_ffn = gain(ks[14], (DEPTH, D_MODEL))
    w_up = nrm(ks[15], (DEPTH, D_MODEL, 2 * D_FF), D_MODEL ** -0.5)
    ffn_conv_w = nrm(ks[16], (DEPTH, FFN_CONV, 2 * D_FF), FFN_CONV ** -0.5)
    w_down = nrm(ks[17], (DEPTH, D_FF, D_MODEL), D_FF ** -0.5)
    g_ple = gain(ks[18], (DEPTH, D_MODEL))
    w_ple_gate = nrm(ks[19], (DEPTH, D_MODEL, D_MODEL), D_MODEL ** -0.5)
    w_ple = nrm(ks[20], (DEPTH, PLE_DIM, D_MODEL), PLE_DIM ** -0.5)
    return {'x': x, 'p': p, 'g_mix': g_mix, 'w_in': w_in, 'b_fox_f': b_fox_f,
            'fox_q_gain': fox_q_gain, 'fox_k_gain': fox_k_gain, 'sc_conv_w': sc_conv_w,
            'dn_conv_w': dn_conv_w, 'dn_a_log': dn_a_log, 'dn_dt_bias': dn_dt_bias,
            'dn_norm_gain': dn_norm_gain, 'w_branch': w_branch, 'w_o': w_o, 'g_ffn': g_ffn,
            'w_up': w_up, 'ffn_conv_w': ffn_conv_w, 'w_down': w_down, 'g_ple': g_ple,
            'w_ple_gate': w_ple_gate, 'w_ple': w_ple}

def first_block(x, p, g_mix, w_in, b_fox_f, fox_q_gain, fox_k_gain, sc_conv_w, dn_conv_w,
              dn_a_log, dn_dt_bias, dn_norm_gain, w_branch, w_o, g_ffn, w_up, ffn_conv_w,
              w_down, g_ple, w_ple_gate, w_ple):
    for i in range(DEPTH):
        x = hybrid_layer(x, p[i], g_mix[i], w_in[i], b_fox_f[i], fox_q_gain[i], fox_k_gain[i],
                         sc_conv_w[i], dn_conv_w[i], dn_a_log[i], dn_dt_bias[i], dn_norm_gain[i],
                         w_branch[i], w_o[i], g_ffn[i], w_up[i], ffn_conv_w[i], w_down[i],
                         g_ple[i], w_ple_gate[i], w_ple[i])
    return x


DEPTH_2 = 2

CHUNK = 64
N_EVEN = (DEPTH_2 + 1) // 2
N_ODD = DEPTH_2 // 2
RMS_EPS = 1e-6

DIFF_HEADS = 4
DIFF_HEAD_DIM = 64
DIFF_V_DIM = 2 * DIFF_HEAD_DIM
DIFF_WIDTH = DIFF_HEADS * DIFF_V_DIM
Q_BLOCK = 128

POOL_WINDOWS = (2, 4, 8, 16)
POOL_GROUPS = len(POOL_WINDOWS)
POOL_WIDTH = D_MODEL // 2
POOL_GROUP_DIM = POOL_WIDTH // POOL_GROUPS
AB_IN_WIDTH = 3 * DIFF_WIDTH + POOL_WIDTH
AB_OUT_IN = DIFF_WIDTH + POOL_WIDTH

GLA_HEADS = 4
GLA_KEY_DIM = D_MODEL // 2
GLA_VAL_DIM = D_MODEL
GLA_HK = GLA_KEY_DIM // GLA_HEADS
GLA_HV = GLA_VAL_DIM // GLA_HEADS
GLA_GATE_RANK = 16
GLA_GATE_TEMP = 16.0
GLA_IN_WIDTH = 2 * GLA_KEY_DIM + 2 * GLA_VAL_DIM + GLA_GATE_RANK

D_FF_2 = 4 * D_MODEL


def _rmsnorm(x, gain):
    xf = x.astype(jnp.float32)
    y = xf * lax.rsqrt(jnp.mean(xf * xf, axis=-1, keepdims=True) + RMS_EPS)
    return (y * gain.astype(jnp.float32)).astype(x.dtype)

def _lambda_init(layer_idx):
    return 0.8 - 0.6 * math.exp(-0.3 * layer_idx)

def _diff_attention(q, k, v, lam_params, subln_gain, layer_idx):
    bsz, seq, _ = q.shape
    q = q.reshape(bsz, seq, DIFF_HEADS, 2, DIFF_HEAD_DIM)
    k = k.reshape(bsz, seq, DIFF_HEADS, 2, DIFF_HEAD_DIM)
    q1 = q[:, :, :, 0].transpose(0, 2, 1, 3)
    q2 = q[:, :, :, 1].transpose(0, 2, 1, 3)
    k1 = k[:, :, :, 0].transpose(0, 2, 1, 3)
    k2 = k[:, :, :, 1].transpose(0, 2, 1, 3)
    v = v.reshape(bsz, seq, DIFF_HEADS, DIFF_V_DIM).transpose(0, 2, 1, 3)
    lam_p = lam_params.astype(jnp.float32)
    lam_init = _lambda_init(layer_idx)
    lam = jnp.exp(jnp.sum(lam_p[0] * lam_p[1])) - jnp.exp(jnp.sum(lam_p[2] * lam_p[3])) + lam_init
    n_blk = seq // Q_BLOCK

    def to_blocks(t):
        return t.reshape(bsz, DIFF_HEADS, n_blk, Q_BLOCK, DIFF_HEAD_DIM).transpose(2, 0, 1, 3, 4)

    key_chunk = jnp.arange(seq) // CHUNK
    scale = DIFF_HEAD_DIM ** -0.5

    def one_block(args):
        q1_b, q2_b, blk = args
        query_chunk = (blk * Q_BLOCK + jnp.arange(Q_BLOCK)) // CHUNK
        mask = key_chunk[None, :] <= query_chunk[:, None]
        s1 = jnp.einsum('bhqd,bhkd->bhqk', q1_b, k1).astype(jnp.float32) * scale
        s2 = jnp.einsum('bhqd,bhkd->bhqk', q2_b, k2).astype(jnp.float32) * scale
        p1 = jax.nn.softmax(jnp.where(mask, s1, -jnp.inf), axis=-1)
        p2 = jax.nn.softmax(jnp.where(mask, s2, -jnp.inf), axis=-1)
        p = p1 - lam * p2
        return jnp.einsum('bhqk,bhkv->bhqv', p.astype(v.dtype), v)

    o = lax.map(one_block, (to_blocks(q1), to_blocks(q2), jnp.arange(n_blk)))
    o = o.transpose(1, 2, 0, 3, 4).reshape(bsz, DIFF_HEADS, seq, DIFF_V_DIM)
    o = _rmsnorm(o, subln_gain) * (1.0 - lam_init)
    return o.transpose(0, 2, 1, 3).reshape(bsz, seq, DIFF_WIDTH)

def _pool_mixer(u, pool_w, pool_scale):
    bsz, seq, _ = u.shape
    u = u.reshape(bsz, seq, POOL_GROUPS, POOL_GROUP_DIM)
    pos = jnp.arange(seq)
    outs = []
    for g, w in enumerate(POOL_WINDOWS):
        ug = u[:, :, g].astype(jnp.float32)
        cs = jnp.cumsum(ug, axis=1)
        lagged = jnp.pad(cs, ((0, 0), (w, 0), (0, 0)))[:, :seq]
        count = jnp.minimum(pos + 1, w).astype(jnp.float32)
        outs.append((cs - lagged) / count[None, :, None] - ug)
    r = jnp.stack(outs, axis=2).astype(u.dtype)
    y = jnp.einsum('bsgc,gcd->bsgd', r, pool_w) * pool_scale.reshape(POOL_GROUPS, POOL_GROUP_DIM)
    return y.reshape(bsz, seq, POOL_WIDTH)

def _gla_mixer(h, w_in, w_gk_up, b_gk, norm_gain, w_out):
    bsz, seq, _ = h.shape
    n_chunk = seq // CHUNK
    proj = h @ w_in
    q, k, v, g_out, gk_low = jnp.split(
        proj,
        [GLA_KEY_DIM, 2 * GLA_KEY_DIM, 2 * GLA_KEY_DIM + GLA_VAL_DIM, 2 * GLA_KEY_DIM + 2 * GLA_VAL_DIM],
        axis=-1)
    log_a = jax.nn.log_sigmoid((gk_low @ w_gk_up + b_gk).astype(jnp.float32)) / GLA_GATE_TEMP

    def to_chunks(t, d):
        return t.reshape(bsz, n_chunk, CHUNK, GLA_HEADS, d).transpose(1, 0, 3, 2, 4)

    qc = to_chunks(q * (GLA_HK ** -0.5), GLA_HK)
    kc = to_chunks(k, GLA_HK)
    vc = to_chunks(v, GLA_HV)
    gc = to_chunks(log_a, GLA_HK)
    causal = jnp.tril(jnp.ones((CHUNK, CHUNK), dtype=bool))

    def step(state, inp):
        qi, ki, vi, gi = inp
        qi = qi.astype(jnp.float32)
        ki = ki.astype(jnp.float32)
        vi = vi.astype(jnp.float32)
        b = jnp.cumsum(gi, axis=2)
        o_inter = jnp.einsum('bhlk,bhkv->bhlv', qi * jnp.exp(b), state)
        diff = b[:, :, :, None, :] - b[:, :, None, :, :]
        decay = jnp.exp(jnp.where(causal[:, :, None], diff, -jnp.inf))
        attn = jnp.einsum('bhijk,bhjk->bhij', qi[:, :, :, None, :] * decay, ki)
        o_intra = jnp.einsum('bhij,bhjv->bhiv', attn, vi)
        b_last = b[:, :, -1:, :]
        new_state = (jnp.exp(b_last[:, :, 0, :])[..., None] * state
                     + jnp.einsum('bhlk,bhlv->bhkv', ki * jnp.exp(b_last - b), vi))
        return new_state, o_inter + o_intra

    state0 = jnp.zeros((bsz, GLA_HEADS, GLA_HK, GLA_HV), jnp.float32)
    _, o = lax.scan(step, state0, (qc, kc, vc, gc))
    o = o.transpose(1, 0, 3, 2, 4).reshape(bsz, seq, GLA_HEADS, GLA_HV).astype(h.dtype)
    gate = jax.nn.silu(g_out).reshape(bsz, seq, GLA_HEADS, GLA_HV)
    o = _rmsnorm(o, norm_gain) * gate
    return o.reshape(bsz, seq, GLA_VAL_DIM) @ w_out

def second_inputs(seed: int = 0) -> dict:
    key = jax.random.key(seed)
    ks = jax.random.split(key, 17)
    f32 = jnp.float32

    def nrm(k, shape, scale):
        return jax.random.normal(k, shape, f32) * scale

    return {
        'x': nrm(ks[0], (BATCH, SEQ, D_MODEL), 1.0),
        'norm_mix': 1.0 + nrm(ks[1], (DEPTH_2, D_MODEL), 0.02),
        'norm_ffn': 1.0 + nrm(ks[2], (DEPTH_2, D_MODEL), 0.02),
        'norm_final': 1.0 + nrm(ks[3], (D_MODEL,), 0.02),
        'ab_w_in': nrm(ks[4], (N_EVEN, D_MODEL, AB_IN_WIDTH), D_MODEL ** -0.5),
        'ab_lambda': nrm(ks[5], (N_EVEN, 4, DIFF_HEAD_DIM), 0.1),
        'ab_subln': 1.0 + nrm(ks[6], (N_EVEN, DIFF_V_DIM), 0.02),
        'pool_w': nrm(ks[7], (N_EVEN, POOL_GROUPS, POOL_GROUP_DIM, POOL_GROUP_DIM), POOL_GROUP_DIM ** -0.5),
        'pool_scale': 1.0 + nrm(ks[8], (N_EVEN, POOL_WIDTH), 0.1),
        'ab_w_out': nrm(ks[9], (N_EVEN, AB_OUT_IN, D_MODEL), AB_OUT_IN ** -0.5),
        'gla_w_in': nrm(ks[10], (N_ODD, D_MODEL, GLA_IN_WIDTH), D_MODEL ** -0.5),
        'gla_w_gk_up': nrm(ks[11], (N_ODD, GLA_GATE_RANK, GLA_KEY_DIM), GLA_GATE_RANK ** -0.5),
        'gla_b_gk': nrm(ks[12], (N_ODD, GLA_KEY_DIM), 0.1),
        'gla_norm': 1.0 + nrm(ks[13], (N_ODD, GLA_HEADS, GLA_HV), 0.02),
        'gla_w_out': nrm(ks[14], (N_ODD, GLA_VAL_DIM, D_MODEL), GLA_VAL_DIM ** -0.5),
        'ffn_w1': nrm(ks[15], (DEPTH_2, D_MODEL, D_FF_2), D_MODEL ** -0.5),
        'ffn_w2': nrm(ks[16], (DEPTH_2, D_FF_2, D_MODEL), D_FF_2 ** -0.5),
    }

def second_block(x, norm_mix, norm_ffn, norm_final, ab_w_in, ab_lambda, ab_subln, pool_w, pool_scale,
              ab_w_out, gla_w_in, gla_w_gk_up, gla_b_gk, gla_norm, gla_w_out, ffn_w1, ffn_w2):
    for i in range(DEPTH_2):
        h = _rmsnorm(x, norm_mix[i])
        if i % 2 == 0:
            e = i // 2
            proj = h @ ab_w_in[e]
            q, k, v, u = jnp.split(proj, [DIFF_WIDTH, 2 * DIFF_WIDTH, 3 * DIFF_WIDTH], axis=-1)
            a_out = _diff_attention(q, k, v, ab_lambda[e], ab_subln[e], i)
            b_out = _pool_mixer(u, pool_w[e], pool_scale[e])
            x = x + jnp.concatenate([a_out, b_out], axis=-1) @ ab_w_out[e]
        else:
            o = i // 2
            x = x + _gla_mixer(h, gla_w_in[o], gla_w_gk_up[o], gla_b_gk[o], gla_norm[o], gla_w_out[o])
        h = _rmsnorm(x, norm_ffn[i])
        x = x + jnp.square(jax.nn.relu(h @ ffn_w1[i])) @ ffn_w2[i]
    return _rmsnorm(x, norm_final)


def setup_inputs(seed=0):
    out = dict(first_inputs(seed))
    for name, value in second_inputs(seed + 1).items():
        if name != "x":
            out[name + "_2"] = value
    return out


def reference(
    x, p, g_mix, w_in, b_fox_f, fox_q_gain, fox_k_gain, sc_conv_w, dn_conv_w, dn_a_log,
    dn_dt_bias, dn_norm_gain, w_branch, w_o, g_ffn, w_up, ffn_conv_w, w_down, g_ple, w_ple_gate,
    w_ple, norm_mix_2, norm_ffn_2, norm_final_2, ab_w_in_2, ab_lambda_2, ab_subln_2, pool_w_2,
    pool_scale_2, ab_w_out_2, gla_w_in_2, gla_w_gk_up_2, gla_b_gk_2, gla_norm_2, gla_w_out_2,
    ffn_w1_2, ffn_w2_2,
):
    x = first_block(
        x, p, g_mix, w_in, b_fox_f, fox_q_gain, fox_k_gain, sc_conv_w, dn_conv_w, dn_a_log,
        dn_dt_bias, dn_norm_gain, w_branch, w_o, g_ffn, w_up, ffn_conv_w, w_down, g_ple,
        w_ple_gate, w_ple,
    )
    return second_block(
        x, norm_mix_2, norm_ffn_2, norm_final_2, ab_w_in_2, ab_lambda_2, ab_subln_2, pool_w_2,
        pool_scale_2, ab_w_out_2, gla_w_in_2, gla_w_gk_up_2, gla_b_gk_2, gla_norm_2,
        gla_w_out_2, ffn_w1_2, ffn_w2_2,
    )


_drawn_inputs = setup_inputs


def setup_inputs(seed=0):
    import zlib

    import numpy as np

    out = dict(_drawn_inputs(seed))
    spreads = {}
    factors = {'fox_q_gain': 8.0,
     'fox_k_gain': 8.0,
     'dn_norm_gain': 6.541,
     'g_ffn': 3.455,
     'g_ple': 200.0,
     'norm_ffn_2': 2.971,
     'norm_final_2': 22.958,
     'ab_lambda_2': 5.118,
     'ab_subln_2': 31.518,
     'gla_b_gk_2': 3.81,
     'gla_norm_2': 200.0,
     'pool_scale_2': 6.47}
    for name, (base, spread) in spreads.items():
        noise = np.random.default_rng([zlib.crc32(name.encode()), seed]).standard_normal(out[name].shape)
        drawn = base * np.exp(spread * noise) if base else spread * noise
        out[name] = jnp.asarray(drawn.astype(out[name].dtype))
    for name, factor in factors.items():
        out[name] = (out[name] * factor).astype(out[name].dtype)
    return out
```

```python
import math
from contextlib import ExitStack

import concourse.bass as bass
from concourse import mybir

P = 128
ALU = mybir.AluOpType
ACT = mybir.ActivationFunctionType
AX = mybir.AxisListType
F32 = mybir.dt.float32
F32R = mybir.dt.float32r

UNIT = 2048
RAW = 3
SPLIT = 3
LEAD = 2
PAD = 4
BIG = 1.0e30
EPS = 1e-6


def build(nc, a):
    T, D = a["x"].shape[1:]
    TT = T // P
    KD = D // P
    FH, FD = a["b_fox_f"].shape[1], a["fox_q_gain"].shape[1]
    FW = FH * FD
    SW = a["sc_conv_w"].shape[2]
    DH, DV = a["dn_a_log"].shape[1], a["dn_norm_gain"].shape[1]
    DW = DH * DV
    NB = a["w_branch"].shape[1]
    BT = SW // P
    DFF = a["w_down"].shape[1]
    UPT = DFF // P
    PLE = a["w_ple"].shape[1]
    CH = 64
    NCH = T // CH
    LI = 0.8 - 0.6 * math.exp(0.0)
    GK = a["gla_w_gk_up_2"].shape[2]
    GR = a["gla_w_gk_up_2"].shape[1]
    GH, GV = a["gla_norm_2"].shape[1:]
    DFF2 = a["ffn_w2_2"].shape[1]
    POOLS = (2, 4, 8, 16)

    w_in = a["w_in"][0]
    o_fox, o_f = 0, 3 * FW
    o_sc = o_f + FH
    o_dn = o_sc + 3 * SW
    o_b = o_dn + 3 * DW
    o_a = o_b + DH
    o_z = o_a + DH
    o_gate = o_z + DW
    NSM = FH + 2 * DH

    units = []
    taken = {"c4": 0, "c5": 0, "g0": 0, "g1": 0}

    def rows_by_tile(w, r0, rows, c0, cols):
        return w[r0:r0 + rows, c0:c0 + cols].rearrange("(k p) n -> p k n", p=P)

    def add(kind, src, act, needs, groups, **more):
        free = [(g, taken[g]) for g in groups if more.get("first", True)]
        units.append(dict(kind=kind, src=src, act=act, needs=needs, free=free, **more))
        if more.get("last", True):
            for g in groups:
                taken[g] += 1
        return len(units) - 1

    def unit_c(w, c0, act, needs):
        bank = 4 + sum(u["kind"] == "C" for u in units) % 2
        return add("C", rows_by_tile(w, 0, D, c0, 256), act, needs, [f"c{bank}"], bank=bank)

    def unit_b(w, c0, act, k0, g, needs):
        return add("B", rows_by_tile(w, 0, 512, c0, 512), act, needs, [f"g{g}"], bank=2 * g, k0=k0)

    def units_t(w, c0, act, g, needs):
        return [add("T", rows_by_tile(w, 512 * h, 512, c0, 512), act, needs, [f"g{g}"], bank=2 * g,
                    k0=4 * h, first=h == 0, last=h == 1) for h in range(2)]

    def unit_d(w, r0, act, k0, first, last, needs, c0=0):
        return add("D", rows_by_tile(w, r0, 256, c0, D), act, needs, ["g0", "g1"], k0=k0, first=first,
                   last=last)

    def after(g):
        return (g, taken[g])

    order = []

    def step(*s):
        order.append(s)

    def weave(fill, mixed):
        n, m, done = len(fill), len(mixed), 0
        for i, f in enumerate(fill):
            order.extend(f)
            upto = (i + 1) * m // n
            order.extend(mixed[done:upto])
            done = upto

    def attention(which):
        for g in range(7):
            if g < 6:
                yield ("att_scores", which, g)
            if g >= 1:
                yield ("att_turn", which, g - 1)
                yield ("att_values", which, g - 1)

    def out_product(w, act, needs):
        us = [unit_d(w, 256 * i, act, 2 * i, i == 0, i == 3, needs) for i in range(4)]
        for u in us:
            step("mm", u)
        return us[-1]

    step("norm", 0, [("x_in", 16)])
    h_ready = [("norm_lo", KD)]
    step("small")
    for j in range(3):
        us = units_t(w_in, o_fox + 512 * j, "h", j % 2, h_ready)
        for u in us:
            step("mm", u)
        step("fox_qkv", j, us[-1], after(f"g{j % 2}"))
    fill = []
    for e in range(BT // 2):
        for part in (1, 2, 0):
            u = unit_c(w_in, o_sc + part * SW + 256 * e, "h", h_ready)
            fill.append([("mm", u), ("sc", e, part, u)])
    for e in range(3 * DW // 256):
        u = unit_c(w_in, o_dn + 256 * e, "h", h_ready)
        fill.append([("mm", u), ("dn", e, u)])
    mixed = [("fox_norm",), ("fox_turn", 0), ("fox_turn", 1), ("fox_cum", 0), ("fox_cum", 1)]
    mixed += list(attention(0)) + [("fox_out",)]
    weave(fill, mixed)
    fill = []
    for e in range(DW // 256):
        u = unit_c(w_in, o_z + 256 * e, "h", h_ready)
        fill.append([("mm", u), ("z", e, u)])
    for e in range(NB * D // 256):
        u = unit_c(w_in, o_gate + 256 * e, "h", h_ready)
        fill.append([("mm", u), ("gate", e, u)])
    mixed = [("dn_square",), ("dn_unit",), ("dn_cum",)]
    for t in range(TT):
        mixed += [("dn_tok", t), ("dn_decay", t), ("dn_kk", t), ("dn_x0", t)]
        for l in range(1, 6):
            mixed += [("dn_y", t, l), ("dn_z", t, l)]
        mixed += [("dn_sol", t)]
    for c in range(NCH):
        mixed += [("dn_new", c), ("dn_state", c)]
    mixed += [("dn_out", 0), ("dn_out", 1)]
    weave(fill, mixed)
    for n, need in enumerate(("fox_lo", "sc_lo", "dn_lo")):
        for g in range(2):
            u = unit_b(a["w_branch"][0][n], 512 * g, "a", BT * n, g, [(need, 2)])
            step("mm", u)
            step("merge", n, g, u, after(f"g{g}"))
    out_product(a["w_o"][0], "h", [("merged_lo", 2)])
    step("resid", len(units) - 1)

    step("norm", 1, [after("g0"), after("g1")])
    downs = {}
    NF = UPT // 2
    for c in range(NF + 1):
        if c < NF:
            for part in range(2):
                u = unit_c(a["w_up"][0], DFF * part + 256 * c, "h", [("norm_lo", 2 * KD)])
                step("mm", u)
                step("up", c, part, u, downs.get(c - 2))
        if c >= 1:
            downs[c - 1] = unit_d(a["w_down"][0], 256 * (c - 1), "a", 2 * ((c - 1) % 2), c == 1, c == NF,
                                  [("glu_lo", c)])
            step("mm", downs[c - 1])
    step("resid", len(units) - 1)

    step("norm", 2, [after("g0"), after("g1")])
    out_product(a["w_ple_gate"][0], "h", [("norm_lo", 3 * KD)])
    step("ple_gate", len(units) - 1)
    step("ple_p")
    step("mm", unit_d(a["w_ple"][0], 0, "a", 0, True, True, [("ple_lo", 1)]))
    step("ple_x", len(units) - 1)

    step("norm", 3, [("ple_added", TT)])
    h_ready = [("norm_lo", 4 * KD)]
    w_ab = a["ab_w_in_2"][0]
    for e in range(4):
        u = unit_c(w_ab, 256 * e, "h", h_ready)
        step("mm", u)
        step("ab_qk", e, u)
    for u in units_t(w_ab, 1024, "h", 0, h_ready):
        step("mm", u)
    step("ab_v", len(units) - 1)
    for e in range(2):
        u = unit_c(w_ab, 1536 + 256 * e, "h", h_ready)
        step("mm", u)
        step("pool_u", e, u)
    step("lam")
    mixed = list(attention(1))
    order.extend(mixed[:8])
    step("pool_win")
    order.extend(mixed[8:])
    step("pool_mm")
    step("ab_out", 0)
    step("ab_out", 1)
    out_product(a["ab_w_out_2"][0], "a", [("ab_lo", 2), ("pool_lo", 1)])
    step("resid", len(units) - 1)

    def squared_relu_part(i, norm):
        step("norm", norm, [after("g0"), after("g1")])
        n, rows_of = DFF2 // 256, {}
        for c in range(n + 1):
            if c < n:
                u = unit_c(a["ffn_w1_2"][i], 256 * c, "h", [("norm_lo", (norm + 1) * KD)])
                step("mm", u)
                step("relu2", i * n + c, c, u, rows_of.get(c - 2))
            if c >= 1:
                rows_of[c - 1] = unit_d(a["ffn_w2_2"][i], 256 * (c - 1), "a", 2 * ((c - 1) % 2), c == 1,
                                        c == n, [("relu2_lo", i * n + c)])
                step("mm", rows_of[c - 1])
        step("resid", len(units) - 1)

    squared_relu_part(0, 4)

    step("norm", 5, [after("g0"), after("g1")])
    h_ready = [("norm_lo", 6 * KD)]
    w_gla = a["gla_w_in_2"][0]
    step("gla_low")
    step("gla_gate")
    for e in range(2 * GK // 256):
        u = unit_c(w_gla, 256 * e, "h", h_ready)
        step("mm", u)
        step("gla_qk", e, u)
    fill = []
    for i in range(4):
        u = unit_d(w_gla, 256 * i, "h", 2 * i, i == 0, i == 3, h_ready, c0=2 * GK)
        fill.append([("mm", u)] + ([("gla_v", u)] if i == 3 else []))
    for e in range(D // 256):
        u = unit_c(w_gla, 2 * GK + D + 256 * e, "h", h_ready)
        fill.append([("mm", u), ("gla_g", e, u)])
    mixed = [("gla_cum",), ("gla_pairs", 0)]
    for l in range(6):
        mixed += [("gla_level", l), ("gla_pairs", l + 1)]
    mixed += [("gla_decay",), ("gla_ktok",)]
    weave(fill, mixed)
    for c in range(NCH):
        step("gla_chunk", c)
    step("gla_out", 0)
    step("gla_out", 1)
    out_product(a["gla_w_out_2"][0], "a", [("gla_lo", 4)])
    step("resid", len(units) - 1)
    squared_relu_part(1, 6)
    step("final", [after("g0"), after("g1")])
    NU = len(units)

    ctx = ExitStack()
    with ctx:
        def sb(name, shape, dt=F32):
            return ctx.enter_context(nc.sbuf_tensor(name, shape, dt))

        sems = {}

        def sem(name):
            if name not in sems:
                sems[name] = ctx.enter_context(nc.semaphore(name))
            return sems[name]

        raw = sb("raw", [P, RAW, UNIT])
        whi = sb("whi", [P, SPLIT, UNIT], F32R)
        wlo = sb("wlo", [P, SPLIT, UNIT], F32R)
        hhi = sb("hhi", [P, KD, T], F32R)
        hlo = sb("hlo", [P, KD, T], F32R)
        ahi = sb("ahi", [P, 3 * BT, T], F32R)
        alo = sb("alo", [P, 3 * BT, T], F32R)
        xs = sb("xs", [P, TT, D])
        x = sb("xres", [P, TT, D])
        ps = ctx.enter_context(nc.psum_tensor("ps", [P, 8, 512], F32))

        ident = sb("ident", [P, P])
        ones = sb("ones", [P, P])
        tri = sb("tri", [P, P])
        tri64 = sb("tri64", [P, P])
        blk64 = sb("blk64", [P, P])
        lev = sb("lev", [P, 6, P])
        cneg = sb("cneg", [P, P])
        dneg = sb("dneg", [P, P])
        inv = sb("inv", [P, 4, 16])
        colp = sb("colp", [P, 3, P])
        gqk = sb("gqk", [P, 2, FD])
        bias16 = sb("bias16", [P, NSM])
        alog = sb("alog", [P, DH])
        wsm = sb("wsm", [P, KD, NSM])
        wlow = sb("wlow", [P, KD, GR])
        ss = sb("ss", [P, TT, 16])
        zz = sb("zz", [P, 4, TT, NSM])
        beta = sb("beta", [P, TT, DH])
        gg = sb("gg", [P, TT, DH])
        gx = sb("gx", [P, TT, 2, DH])
        gcol = sb("gcol", [P, TT, DH])
        gt = sb("gt", [P, TT, DH, 2])
        nmax = sb("nmax", [P, 2, 4])
        rsum = sb("rsum", [P, 2, 4])
        lamw = sb("lamw", [P, 8])
        conv = sb("conv", [P, 2, 2, PAD + T])
        cy = sb("cy", [P, 2, 2, T])
        ARENA = nc.sbuf_bytes_remaining // 4 - 16
        arena = sb("arena", [P, ARENA])

        def view(base, n):
            assert base + n <= ARENA, (base, n, ARENA)
            return arena[:, base:base + n]

        def tiles(ap):
            return ap.rearrange("p (c t) -> p c t", t=T)

        def by(ap, n):
            return ap.rearrange("p (h i) -> p h i", h=n)

        rows = view(0, 3 * P).rearrange("p (b n) -> p b n", b=3)
        dnT = tiles(view(0, 3072))
        kcT = dnT[:, 2 * DH:3 * DH, :]
        gates = tiles(view(3072, 6144))
        fqkv = view(3072, 3072).rearrange("p (t n) -> p t n", t=TT)
        fT = tiles(view(6144, 2048))
        S2 = view(8192, 1024).rearrange("p (b n) -> p b n", b=2)
        PT2 = view(9216, 1024).rearrange("p (b n) -> p b n", b=2)
        fcum = view(10240, 2048).rearrange("p (t h j) -> p t h j", t=TT, h=FH)
        fbias = xs[:, :, :].rearrange("p t n -> p (t n)").rearrange("p (h j) -> p h j", h=FH)
        dsq = view(10240, 2048)
        kdec, rhsk, vb, qkT = [view(9216 + 1024 * i, 1024).rearrange("p (t h d) -> p t h d", t=TT, h=DH)
                               for i in range(4)]
        X, XT, LT, DT = [by(view(13312 + 512 * i, 512), DH) for i in range(4)]
        Bl, Y = [by(cy[:, i, :, :].rearrange("p a t -> p (a t)"), DH) for i in range(2)]
        zT = xs[:, 0, :].rearrange("p (c t) -> p c t", t=T)
        S = by(xs[:, 1, 0:512], DH)
        EG = by(xs[:, 1, 512:1024], DH)
        mg = tiles(view(9216, 2048))
        mtmp = tiles(view(11264, 1024))
        sg = view(0, 2048).rearrange("p (t n) -> p t n", t=TT)
        ptok = view(2048, 512).rearrange("p (t n) -> p t n", t=TT)
        qkf = tiles(view(0, 2048))
        vtok = view(2048, 1024).rearrange("p (t n) -> p t n", t=TT)
        S2b = view(3072, 1024).rearrange("p (b n) -> p b n", b=2)
        PT2b = view(4096, 1024).rearrange("p (b n) -> p b n", b=2)
        ob = view(5120, 1024).rearrange("p (t h d) -> p t h d", t=TT, h=4)
        oy = by(view(6144, 512), 4)
        W0 = 16
        pu, p1, p2, p3, p4 = [view(6656 + 1088 * i, 4 * (W0 + T)).rearrange("p (g t) -> p g t", g=4)
                              for i in range(5)]
        pr = tiles(view(12096, 1024))
        pw = by(view(13120, 512), 4)
        pfix = view(13632, 64).rearrange("p (g t) -> p g t", g=4)
        lamr = by(view(13696, 4 * FD), 4)
        gqT = tiles(view(0, 2048))
        gla = view(2048, 1024).rearrange("p (t n) -> p t n", t=TT)
        gmin = view(3072, 1024).rearrange("p (t n) -> p t n", t=TT)
        bcum = tiles(view(4096, 1024))
        E1 = tiles(view(2048, 1024))
        Cl = tiles(view(3072, 1024))
        attn = view(5120, 1024).rearrange("p (g i) -> p g i", g=TT * GH)
        atmp = view(6144, 1024).rearrange("p (g i) -> p g i", g=TT * GH)
        kdt = view(7168, 1024).rearrange("p (g i) -> p g i", g=TT * GH)
        EB = tiles(view(8192, 1024))
        vg = view(9216, 2048).rearrange("p (t n) -> p t n", t=TT)
        sgT = tiles(view(11264, 2048))
        GS = view(13312, 1024).rearrange("p (h d) -> p h d", h=GH)
        gkT = view(14336, 256)
        wgu = view(14592, GK)[0:GR, :]
        bgk = view(9216, GK)[0:1, :]
        og = view(2048, 1024).rearrange("p (h d) -> p h d", h=GH)
        gy = view(6144, 1024).rearrange("p (c t) -> p c t", c=KD)
        gsq = view(7168, 1024).rearrange("p (h d) -> p h d", h=GH)
        nfin = view(0, D)

        def as_rows(ap, s):
            return ap.rearrange(s, p=P)

        sources, place = [], {}

        def param(name, src, block, n):
            at = sum(k for b, _, k in sources if b == block)
            place[name] = (block, at)
            sources.append((block, src, n))

        param("g_mix", as_rows(a["g_mix"][0], "(k p) -> k p"), 0, KD)
        param("g_ffn", as_rows(a["g_ffn"][0], "(k p) -> k p"), 0, KD)
        param("g_ple", as_rows(a["g_ple"][0], "(k p) -> k p"), 0, KD)
        param("norm_mix", as_rows(a["norm_mix_2"], "i (k p) -> (i k) p"), 0, 2 * KD)
        param("norm_ffn", as_rows(a["norm_ffn_2"], "i (k p) -> (i k) p"), 0, 2 * KD)
        param("gla_norm", as_rows(a["gla_norm_2"][0], "h (k p) -> (h k) p"), 0, KD)
        param("dn_gain", a["dn_norm_gain"], 0, 1)
        param("subln", a["ab_subln_2"], 0, 1)
        param("pool_scale", as_rows(a["pool_scale_2"][0], "(k p) -> k p"), 0, 4)
        param("sc_conv", as_rows(a["sc_conv_w"][0], "j (k p) -> (j k) p"), 0, 3 * BT)
        param("dn_conv", as_rows(a["dn_conv_w"][0], "j (k p) -> (j k) p"), 1, 4 * 3 * BT)
        for j in range(3):
            param(f"ffn_conv{j}", as_rows(a["ffn_conv_w"][0][j:j + 1], "j (k p) -> (j k) p"), (1, 2, 2)[j], 2 * UPT)

        def col(name, i):
            block, at = place[name]
            return colp[:, block, at + i:at + i + 1]

        def cols(name, n, width):
            block, at = place[name]
            return colp[:, block, at:at + n].unsqueeze(2).to_broadcast([P, n, width])

        gains = [("g_mix", 0), ("g_ffn", 0), ("g_ple", 0), ("norm_mix", 0), ("norm_ffn", 0),
                 ("norm_mix", KD), ("norm_ffn", KD)]
        n_par = len(sources) + 6
        groups = [(1, (2 * g, 2 * g + 1)) for g in range(4)] + [(0, tuple(range(4 * g, 4 * g + 4))) for g in range(2)]

        def turned(which, g):
            b, maps = groups[g]
            w = P * (b + 1)
            if which == 0:
                return [(i * w + kt * P, f, kt) for i, f in enumerate(maps) for kt in range(b + 1)]
            return [(i * w + kt * P, f // 2, kt) for i, f in enumerate(maps) if f % 2 == 0 for kt in range(b + 1)]

        att = [dict(q=fT[:, 0:4, :], k=fT[:, 4:8, :], S=S2, PT=PT2), dict(q=qkf[:, 0:4, :], k=qkf[:, 4:8, :], S=S2b, PT=PT2b)]

        def took(u):
            g, n = units[u]["free"][0]
            return sem(g), n + 1

        for name in ("params_in", "constants", "x_in", "unit_done", "hi_done", "lo_done"):
            sem(name)
        block = ctx.enter_context(nc.Block())

        @block.sync
        def _(sp):
            sp.dma_start(x[:, :, :], a["x"][0].rearrange("(t p) d -> p t d", p=P)).then_inc(sem("x_in"), 16)
            for u in range(NU):
                if u >= RAW:
                    sp.wait_ge(sem("lo_done"), u - RAW + 1)
                src = units[u]["src"]
                dst = raw[:, u % RAW, :].rearrange("p (k n) -> p k n", k=src.shape[1])
                sp.dma_start(dst, src).then_inc(sem(f"raw_in{u % RAW}"), 16)
            sp.wait_ge(sem("final_x"), TT)
            sp.dma_start(a["out"][0].rearrange("(t p) d -> p t d", p=P), xs[:, :, :]).then_inc(sem("stored"), 16)
            sp.wait_ge(sem("stored"), 16)

        @block.gpsimd
        def _(pool):
            n = [0]

            def then(ins):
                n[0] += 1
                ins.then_inc(sem("constants"), 1)
                pool.wait_ge(sem("constants"), n[0])

            then(pool.memset(rows[:, :, :], 0.0))
            for t_, v in ((ident, 0.0), (ones, 1.0), (tri, 1.0), (blk64, 0.0), (cneg, 0.0), (dneg, 0.0)):
                then(pool.memset(t_[:, :], v))
            then(pool.memset(lev[:, :, :], 0.0))
            then(pool.memset(conv[:, :, :, :], 0.0))
            then(pool.affine_select(out=ident[:, :], in_=ident[:, :], compare_op=ALU.not_equal, fill=1.0,
                                    base=0, pattern=[[-1, P]], channel_multiplier=1))
            then(pool.affine_select(out=tri[:, :], in_=tri[:, :], compare_op=ALU.is_ge, fill=0.0,
                                    base=0, pattern=[[1, P]], channel_multiplier=-1))
            then(pool.affine_select(out=cneg[:, :], in_=cneg[:, :], compare_op=ALU.is_ge, fill=-BIG,
                                    base=0, pattern=[[-1, P]], channel_multiplier=1))
            then(pool.memset(dneg[0:CH, CH:P], -BIG))
            then(pool.memset(blk64[0:CH, 0:CH], 1.0))
            then(pool.memset(blk64[CH:P, CH:P], 1.0))
            then(pool.tensor_copy(tri64[:, :], tri[:, :]))
            then(pool.memset(tri64[0:CH, CH:P], 0.0))
            for l in range(6):
                s = 1 << l
                right = lev[:, l, :].rearrange("p (n two s) -> p n two s", two=2, s=s)[:, :, 1, :]
                then(pool.memset(right, 1.0))
                nb = P // (2 * s)
                then(pool.affine_select(out=right, in_=right, compare_op=ALU.is_ge, fill=0.0, base=0,
                                        pattern=[[-2 * s, nb], [0, s]], channel_multiplier=1))
                then(pool.affine_select(out=right, in_=right, compare_op=ALU.is_ge, fill=0.0, base=s - 1,
                                        pattern=[[2 * s, nb], [0, s]], channel_multiplier=-1))
            for g, w in enumerate(POOLS):
                then(pool.memset(inv[:, g, :], 1.0 / w))
                for i in range(w - 1):
                    then(pool.memset(inv[:, g, i:i + 1], 1.0 / (i + 1)))

        n_const = [9 + 3 + 5 + 18 + 4 + sum(w - 1 for w in POOLS)]

        @block.scalar
        def _(act):
            n = [0]

            def link(ins):
                n[0] += 1
                ins.then_inc(sem("act_own"), 1)
                act.wait_ge(sem("act_own"), n[0])

            roots = [0]

            def root(ap):
                roots[0] += 1
                act.wait_ge(sem("root_in"), roots[0])
                act.activation(ap, ap, ACT.Sqrt).then_inc(sem("root_out"), 1)

            def split_high(u):
                act.wait_ge(sem(f"raw_in{u % RAW}"), 16 * (u // RAW + 1))
                if u >= SPLIT:
                    act.wait_ge(sem("unit_done"), u - SPLIT + 1)
                act.activation(whi[:, u % SPLIT, :], raw[:, u % RAW, :], ACT.Copy).then_inc(sem("hi_done"), 1)

            act.wait_ge(sem("constants"), 1)
            at = {}
            for b, src, k in sources:
                r = at.get(b, 0)
                act.dma_start(rows[r:r + k, b, :], src).then_inc(sem("params_in"), 16)
                at[b] = r + k
            act.dma_start(gqk[:, 0, :], a["fox_q_gain"][0].partition_broadcast(P)).then_inc(sem("params_in"), 16)
            act.dma_start(gqk[:, 1, :], a["fox_k_gain"][0].partition_broadcast(P)).then_inc(sem("params_in"), 16)
            act.dma_start(bias16[:, 0:FH], a["b_fox_f"][0].partition_broadcast(P)).then_inc(sem("params_in"), 16)
            act.dma_start(bias16[:, FH + DH:NSM], a["dn_dt_bias"][0].partition_broadcast(P))\
               .then_inc(sem("params_in"), 16)
            act.dma_start(alog[:, :], a["dn_a_log"][0].partition_broadcast(P)).then_inc(sem("params_in"), 16)
            act.dma_start(wlow[:, :, :], rows_by_tile(a["gla_w_in_2"][0], 0, D, 2 * GK + 2 * D, GR))\
               .then_inc(sem("params_in"), 16)
            act.dma_start(wsm[:, :, 0:FH], rows_by_tile(w_in, 0, D, o_f, FH)).then_inc(sem("small_in"), 16)
            act.dma_start(wsm[:, :, FH:NSM], rows_by_tile(w_in, 0, D, o_b, 2 * DH)).then_inc(sem("small_in"), 16)
            act.wait_ge(sem("constants"), n_const[0])

            def norm(i, waits):
                for s, v in waits:
                    act.wait_ge(sem(s), v)
                for t in range(TT):
                    act.activation(xs[:, t, :], x[:, t, :], ACT.Square, accum_out=ss[:, t, 0:1])\
                       .then_inc(sem("norm_sum"), 1)
                for t in range(TT):
                    root(ss[:, t, 0:1])
                name, k0 = gains[i]
                for b in range(4):
                    act.wait_ge(sem("norm_turned"), 4 * i + b + 1)
                    if i == 0 and b == 0:
                        act.wait_ge(sem("colp_done"), 1)
                    for k in (2 * b, 2 * b + 1):
                        act.activation(hhi[:, k, :], ps[:, b, (k % 2) * T:(k % 2 + 1) * T], ACT.Copy,
                                       scale=col(name, k0 + k)).then_inc(sem("norm_hi"), 1)
                if i == 4:
                    act.dma_start(bgk, a["gla_b_gk_2"]).then_inc(sem("gla_par"), 16)
                    act.dma_start(wgu, a["gla_w_gk_up_2"][0]).then_inc(sem("gla_par"), 16)

            def small():
                act.wait_ge(sem("small_abs"), 1)
                act.activation(zz[:, 1], zz[:, 1], ACT.Exp, scale=-1.0).then_inc(sem("small_exp"), 1)
                act.activation(alog[:, :], alog[:, :], ACT.Exp).then_inc(sem("small_exp"), 1)
                act.wait_ge(sem("small_exp"), 2)
                act.activation(zz[:, 2], zz[:, 1], ACT.Ln, bias=1.0).then_inc(sem("small_exp"), 1)
                act.wait_ge(sem("small_lsg"), 1)
                act.activation(beta[:, :, :], zz[:, 3, :, FH:FH + DH], ACT.Exp).then_inc(sem("small_exp"), 1)

            def fox_qkv(j, u, freed):
                act.wait_ge(sem("unit_done"), u + 1)
                g = j % 2
                for t in range(TT):
                    ins = act.activation(fqkv[:, t, 512 * j:512 * (j + 1)], ps[:, 2 * g + t, :], ACT.Copy)
                ins.then_inc(sem(f"g{g}"), 1)

            def sc(e, part, u):
                act.wait_ge(sem("unit_done"), u + 1)
                out = cy[:, e % 2, :, :]
                if part == 1:
                    act.activation(out, tiles(ps[:, units[u]["bank"], :]), ACT.Copy).then_inc(took(u)[0], 1)
                if part == 0:
                    act.wait_ge(*took(u))
                    act.activation(ahi[:, BT + 2 * e:BT + 2 * e + 2, :], out, ACT.Copy).then_inc(sem("sc_hi"), 1)

            def conv_copy(j, u):
                act.wait_ge(sem("unit_done"), u + 1)
                act.wait_ge(sem("conv_read"), j - 1)
                act.activation(conv[:, j % 2, :, PAD:PAD + T], tiles(ps[:, units[u]["bank"], :]), ACT.Copy)\
                   .then_inc(took(u)[0], 1)

            def dn(e, u):
                conv_copy(BT // 2 + e, u)
                act.wait_ge(sem("conv_read"), BT // 2 + e + 1)
                both = dnT[:, 2 * e:2 * e + 2, :]
                act.activation(both, both, ACT.Silu).then_inc(sem("dn_silu"), 1)

            def fox_turn(t):
                for b in range(2):
                    act.wait_ge(sem("fox_turned"), 2 * t + b + 1)
                    act.activation(fT[:, 4 * b:4 * b + 4, t * P:(t + 1) * P], by(ps[:, 2 * t + b, :], 4), ACT.Copy,
                                   scale=FD ** -0.5 if b == 0 else 1.0).then_inc(sem("fox_T"), 1)

            def fox_cum(t):
                for b in range(2):
                    act.wait_ge(sem("fox_cummed"), 2 * t + b + 1)
                    act.activation(fbias[:, 4 * b:4 * b + 4, t * P:(t + 1) * P], by(ps[:, 2 * t + b, :], 4), ACT.Copy,
                                   scale=-1.0).then_inc(sem("fox_bias"), 1)

            def att_scores(w, g):
                b, maps = groups[g]
                act.wait_ge(sem(f"att{w}_max"), g + 1)
                width = P * (b + 1)
                for i in range(len(maps)):
                    part = att[w]["S"][:, g % 2, i * width:(i + 1) * width]
                    ins = act.activation(part, part, ACT.Exp, bias=nmax[:, g % 2, i:i + 1],
                                         accum_out=rsum[:, g % 2, i:i + 1])
                    ins.then_inc(sem(f"att{w}_exp"), 1)

            def att_turn(w, g):
                act.wait_ge(sem(f"att{w}_turned"), g + 1)
                if g >= 2:
                    act.wait_ge(sem(f"att{w}_used"), g - 1)
                k = len(turned(w, g)) * P
                act.activation(att[w]["PT"][:, g % 2, 0:k], ps[:, 6 + g % 2, 0:k], ACT.Copy)\
                   .then_inc(sem(f"att{w}_PT"), 1)

            def fox_out():
                act.wait_ge(sem("att0_used"), 6)
                for b in range(2):
                    act.activation(ahi[:, 2 * b:2 * b + 2, :], tiles(ps[:, b, :]), ACT.Copy)\
                       .then_inc(sem("fox_hi"), 1)

            def z(e, u):
                act.wait_ge(sem("unit_done"), u + 1)
                act.activation(zT[:, 2 * e:2 * e + 2, :], tiles(ps[:, units[u]["bank"], :]), ACT.Silu)\
                   .then_inc(took(u)[0], 1)

            def gate(e, u):
                act.wait_ge(sem("unit_done"), u + 1)
                act.activation(gates[:, 2 * e:2 * e + 2, :], tiles(ps[:, units[u]["bank"], :]), ACT.Sigmoid)\
                   .then_inc(took(u)[0], 1)

            def dn_cum():
                act.wait_ge(sem("dn_gx"), 1)
                act.activation(gx[:, :, :, :], gx[:, :, :, :], ACT.Exp).then_inc(sem("dn_egx"), 1)

            def dn_decay(t):
                act.wait_ge(sem("dn_grow"), t + 1)
                if t >= 1:
                    act.wait_ge(sem("dn_lt"), t)
                act.activation(EG, by(ps[:, 6, :], DH), ACT.Exp).then_inc(sem("dn_eg"), 1)
                act.wait_ge(sem("dn_dt"), t + 1)
                act.activation(DT, DT, ACT.Exp).then_inc(sem("dn_edt"), 1)

            def dn_x0(t):
                act.wait_ge(sem("dn_x0_turned"), t + 1)
                act.activation(X, by(ps[:, 6, :], DH), ACT.Copy).then_inc(sem("dn_X"), 1)

            def dn_y(t, l):
                act.wait_ge(sem("dn_BX"), 5 * t + l)
                act.activation(Y, by(ps[:, 7, :], DH), ACT.Copy).then_inc(sem("dn_Y"), 1)

            def dn_sol(t):
                act.wait_ge(sem("dn_solved"), 2 * t + 2)
                act.activation(kcT[:, :, t * P:(t + 1) * P], by(ps[:, 7, :], DH), ACT.Copy)\
                   .then_inc(sem("dn_kcT"), 1)

            def dn_out(t):
                act.wait_ge(sem("dn_o"), 2 * t + 2)
                act.activation(rhsk[:, t, :, :], by(ps[:, 2 + t, :], DH), ACT.Copy).then_inc(sem("dn_ocopy"), 1)
                root(ss[:, 0, 0:DH])
                act.wait_ge(sem("dn_y2"), t + 1)
                act.activation(ahi[:, 2 * BT:3 * BT, t * P:(t + 1) * P], XT, ACT.Copy).then_inc(sem("dn_hi"), 1)

            def merge(n_, g, u, freed):
                if n_ == NB - 1:
                    act.wait_ge(sem("merged"), g + 1)
                    act.activation(hhi[:, 4 * g:4 * g + 4, :], mg[:, 4 * g:4 * g + 4, :], ACT.Copy)\
                       .then_inc(sem("merged_hi"), 1)

            def up(c, part, u, down):
                conv_copy(BT // 2 + 6 + 2 * c + part, u)
                if part == 0:
                    act.wait_ge(sem("conv_read"), BT // 2 + 6 + 2 * c + 1)
                    act.activation(cy[:, 0, :, :], cy[:, 0, :, :], ACT.Silu).then_inc(sem("glu_silu"), 1)
                else:
                    act.wait_ge(sem("glu_prod"), c + 1)
                    if down is not None:
                        act.wait_ge(sem("unit_done"), down + 1)
                    s = 2 * (c % 2)
                    act.activation(ahi[:, s:s + 2, :], cy[:, 1, :, :], ACT.Copy).then_inc(sem("glu_hi"), 1)

            def ple_gate(u):
                act.wait_ge(sem("unit_done"), u + 1)
                for t in range(TT):
                    act.activation(sg[:, t, :].rearrange("p (b n) -> p b n", b=2), ps[:, 2 * t:2 * t + 2, :],
                                   ACT.Sigmoid).then_inc(sem(f"g{t}"), 1)

            def ple_p():
                act.dma_start(ptok, a["p"][0][0].rearrange("(t p) d -> p t d", p=P)).then_inc(sem("p_in"), 16)
                act.wait_ge(sem("p_turned"), 1)
                act.activation(ahi[:, 0:2, :], tiles(ps[:, 6, :]), ACT.Copy).then_inc(sem("ple_hi"), 1)

            def ab_qk(e, u):
                act.wait_ge(sem("unit_done"), u + 1)
                act.wait_ge(sem("ple_added"), TT)
                act.activation(qkf[:, 2 * e:2 * e + 2, :], tiles(ps[:, units[u]["bank"], :]), ACT.Copy,
                               scale=FD ** -0.5 if e < 2 else 1.0).then_inc(took(u)[0], 1)

            def ab_v(u):
                act.wait_ge(sem("unit_done"), u + 1)
                for t in range(TT):
                    ins = act.activation(vtok[:, t, :], ps[:, t, :], ACT.Copy)
                ins.then_inc(sem("g0"), 1)
                act.dma_start(pw, a["pool_w_2"][0].rearrange("g c d -> c g d")).then_inc(sem("pw_in"), 16)
                act.dma_start(lamr, a["ab_lambda_2"][0].partition_broadcast(P)).then_inc(sem("lam_in"), 16)

            def pool_u(e, u):
                act.wait_ge(sem("unit_done"), u + 1)
                act.wait_ge(sem("pool_zero"), 1)
                act.activation(pu[:, 2 * e:2 * e + 2, W0:W0 + T], tiles(ps[:, units[u]["bank"], :]), ACT.Copy)\
                   .then_inc(took(u)[0], 1)

            def lam():
                act.wait_ge(sem("lam_sum"), 1)
                act.activation(lamw[:, 0:2], lamw[:, 0:2], ACT.Exp).then_inc(sem("lam_exp"), 1)

            def pool_mm():
                act.wait_ge(sem("pool_y"), 1)
                act.activation(ahi[:, 4:8, :], pr, ACT.Copy).then_inc(sem("pool_hi"), 1)

            def ab_out(b):
                act.wait_ge(sem("att1_used"), 6)
                act.activation(ob[:, b, :, :], by(ps[:, b, :], 4), ACT.Copy).then_inc(sem("ab_ocopy"), 1)
                root(ss[:, 0, 0:4])
                act.wait_ge(sem("ab_y"), b + 1)
                act.activation(ahi[:, 0:4, b * P:(b + 1) * P], oy, ACT.Copy).then_inc(sem("ab_hi"), 1)

            def relu2(i, c, u, down):
                act.wait_ge(sem("unit_done"), u + 1)
                if i >= 2:
                    act.wait_ge(sem("relu2_lo"), i - 1)
                act.activation(cy[:, i % 2, :, :], tiles(ps[:, units[u]["bank"], :]), ACT.Relu)\
                   .then_inc(took(u)[0], 1)
                act.wait_ge(sem("relu2_sq"), i + 1)
                if down is not None:
                    act.wait_ge(sem("unit_done"), down + 1)
                s = 2 * (c % 2)
                act.activation(ahi[:, s:s + 2, :], cy[:, i % 2, :, :], ACT.Copy).then_inc(sem("relu2_hi"), 1)

            def gla_low():
                act.wait_ge(sem("gla_lowed"), 1)
                act.activation(gkT[0:GR, :], ps[0:GR, 6, 0:T], ACT.Copy).then_inc(sem("gla_gkT"), 1)

            def gla_gate():
                act.wait_ge(sem("gla_abs"), 1)
                act.activation(gla[:, :, :], gla[:, :, :], ACT.Exp, scale=-1.0).then_inc(sem("gla_ln"), 1)
                act.wait_ge(sem("gla_ln"), 1)
                act.activation(gla[:, :, :], gla[:, :, :], ACT.Ln, bias=1.0).then_inc(sem("gla_ln"), 1)

            def gla_qk(e, u):
                act.wait_ge(sem("unit_done"), u + 1)
                act.activation(gqT[:, 2 * e:2 * e + 2, :], tiles(ps[:, units[u]["bank"], :]), ACT.Copy,
                               scale=(GK // GH) ** -0.5 if e < GK // 256 else 1.0).then_inc(took(u)[0], 1)

            def gla_cum():
                for b in range(2):
                    act.wait_ge(sem("gla_cummed"), b + 1)
                    act.activation(bcum[:, 2 * b:2 * b + 2, :], tiles(ps[:, 6 + b, :]), ACT.Copy,
                                   scale=1.0 / 16.0).then_inc(sem("gla_b"), 1)

            def gla_level(l):
                act.wait_ge(sem("gla_arg"), l + 1)
                act.activation(E1[:, :, :], E1[:, :, :], ACT.Exp).then_inc(sem("gla_E"), 1)

            def gla_decay():
                act.activation(EB[:, :, :], bcum[:, :, :], ACT.Exp).then_inc(sem("gla_EB"), 1)
                act.wait_ge(sem("gla_arg"), 7)
                act.activation(E1[:, :, :], E1[:, :, :], ACT.Exp).then_inc(sem("gla_E"), 1)

            def gla_ktok():
                for b in range(2):
                    act.wait_ge(sem("gla_kturned"), b + 1)
                    act.activation(kdt[:, 4 * b:4 * b + 4, :], by(ps[:, 6 + b, :], 4), ACT.Copy)\
                       .then_inc(sem("gla_kdt"), 1)

            def gla_v(u):
                act.wait_ge(sem("unit_done"), u + 1)
                for t in range(TT):
                    act.activation(vg[:, t, :].rearrange("p (b n) -> p b n", b=2), ps[:, 2 * t:2 * t + 2, :],
                                   ACT.Copy).then_inc(sem(f"g{t}"), 1)

            def gla_g(e, u):
                act.wait_ge(sem("unit_done"), u + 1)
                act.activation(sgT[:, 2 * e:2 * e + 2, :], tiles(ps[:, units[u]["bank"], :]), ACT.Silu)\
                   .then_inc(took(u)[0], 1)

            def gla_out(t):
                act.wait_ge(sem("gla_o"), 2 * t + 2)
                if t >= 1:
                    act.wait_ge(sem("gla_oturned"), 2 * t)
                act.activation(og[:, :, :].rearrange("p (b h) d -> p b (h d)", b=2), ps[:, 2 * t:2 * t + 2, :],
                               ACT.Copy).then_inc(sem("gla_ocopy"), 1)
                root(ss[:, 0, 0:GH])
                for b in range(2):
                    act.wait_ge(sem("gla_y"), 2 * t + b + 1)
                    act.activation(ahi[:, 4 * b:4 * b + 4, t * P:(t + 1) * P], gy[:, 4 * b:4 * b + 4, :],
                                   ACT.Copy).then_inc(sem("gla_hi"), 1)

            def final(waits):
                act.dma_start(nfin, a["norm_final_2"].partition_broadcast(P)).then_inc(sem("nfin_in"), 16)
                for s, v in waits:
                    act.wait_ge(sem(s), v)
                for t in range(TT):
                    act.activation(xs[:, t, :], x[:, t, :], ACT.Square, accum_out=ss[:, t, 0:1])\
                       .then_inc(sem("norm_sum"), 1)
                for t in range(TT):
                    root(ss[:, t, 0:1])

            def fox_norm():
                root(ss[:, :, :])

            def dn_unit():
                root(dsq)

            parts = dict(norm=norm, small=small, fox_qkv=fox_qkv, sc=sc, dn=dn, fox_turn=fox_turn,
                         fox_cum=fox_cum, att_scores=att_scores, att_turn=att_turn, fox_out=fox_out, z=z,
                         gate=gate, dn_cum=dn_cum, dn_decay=dn_decay, dn_x0=dn_x0, dn_y=dn_y,
                         dn_sol=dn_sol, dn_out=dn_out, merge=merge, up=up, ple_gate=ple_gate, ple_p=ple_p,
                         ab_qk=ab_qk, ab_v=ab_v, pool_u=pool_u, lam=lam, pool_mm=pool_mm, ab_out=ab_out,
                         relu2=relu2, gla_low=gla_low, gla_gate=gla_gate, gla_qk=gla_qk, gla_cum=gla_cum,
                         gla_level=gla_level, gla_decay=gla_decay, gla_ktok=gla_ktok, gla_v=gla_v,
                         gla_g=gla_g, gla_out=gla_out, final=final, fox_norm=fox_norm, dn_unit=dn_unit)
            parts["mm"] = lambda u: split_high(u + LEAD) if u + LEAD < NU else None
            for u in range(LEAD):
                split_high(u)
            for s in order:
                if s[0] in parts:
                    parts[s[0]](*s[1:])

        @block.vector
        def _(dve):
            n = [0]

            def link(ins):
                n[0] += 1
                ins.then_inc(sem("dve_own"), 1)
                dve.wait_ge(sem("dve_own"), n[0])

            def own(ins, name, value):
                ins.then_inc(sem(name), 1)
                dve.wait_ge(sem(name), value)

            def wide(ap, shape):
                return ap.to_broadcast([P] + shape)

            def split_low(u):
                dve.wait_ge(sem("hi_done"), u + 1)
                dve.tensor_tensor(wlo[:, u % SPLIT, :], raw[:, u % RAW, :], whi[:, u % SPLIT, :].bitcast(F32),
                                  ALU.subtract).then_inc(sem("lo_done"), 1)

            roots = [0]

            def root(ap, scale):
                rooted(dve.tensor_scalar(ap, ap, scale, EPS, ALU.mult, ALU.add), ap)

            def rooted(ins, ap):
                roots[0] += 1
                ins.then_inc(sem("root_in"), 1)
                dve.wait_ge(sem("root_out"), roots[0])
                link(dve.reciprocal(ap, ap))

            def norm(i, waits):
                for t in range(TT):
                    dve.wait_ge(sem("norm_sum"), TT * i + t + 1)
                    root(ss[:, t, 0:1], 1.0 / D)
                    dve.tensor_scalar(xs[:, t, :], x[:, t, :], ss[:, t, 0:1], None, ALU.mult)\
                       .then_inc(sem("norm_scaled"), 1)
                if i == 0:
                    dve.wait_ge(sem("colp_turned"), 1)
                    dve.tensor_copy(colp[:, :, :].rearrange("p b n -> p (b n)"), ps[:, 7, 0:3 * P])\
                       .then_inc(sem("colp_done"), 1)
                    dve.wait_ge(sem("colp_done"), 1)
                name, k0 = gains[i]
                for b in range(4):
                    dve.wait_ge(sem("norm_hi"), KD * i + 2 * b + 2)
                    for k in (2 * b, 2 * b + 1):
                        dve.scalar_tensor_tensor(out=hlo[:, k, :], in0=ps[:, b, (k % 2) * T:(k % 2 + 1) * T],
                                                 scalar=col(name, k0 + k), in1=hhi[:, k, :].bitcast(F32),
                                                 op0=ALU.mult, op1=ALU.subtract).then_inc(sem("norm_lo"), 1)

            def small():
                dve.wait_ge(sem("params_in"), 16 * n_par)
                link(dve.memset(bias16[:, FH:FH + DH], 0.0))
                dve.wait_ge(sem("small_done"), 1)
                link(dve.tensor_tensor(zz[:, 0], ps[:, 6, 0:TT * NSM].rearrange("p (t n) -> p t n", t=TT),
                                       wide(bias16[:, :].unsqueeze(1), [TT, NSM]), ALU.add))
                dve.scalar_tensor_tensor(out=zz[:, 1], in0=zz[:, 0], scalar=-1.0, in1=zz[:, 0], op0=ALU.mult,
                                         op1=ALU.max).then_inc(sem("small_abs"), 1)
                dve.wait_ge(sem("small_exp"), 3)
                link(dve.tensor_scalar(zz[:, 3], zz[:, 1], 1.0, None, ALU.add))
                link(dve.scalar_tensor_tensor(out=zz[:, 1], in0=zz[:, 3], scalar=-1.0, in1=zz[:, 1],
                                              op0=ALU.add, op1=ALU.subtract))
                link(dve.reciprocal(zz[:, 3], zz[:, 3]))
                link(dve.tensor_tensor(zz[:, 1], zz[:, 1], zz[:, 3], ALU.mult))
                link(dve.tensor_tensor(zz[:, 2], zz[:, 2], zz[:, 1], ALU.subtract))
                link(dve.scalar_tensor_tensor(out=gg[:, :, :], in0=zz[:, 0, :, FH + DH:NSM], scalar=0.0,
                                              in1=zz[:, 2, :, FH + DH:NSM], op0=ALU.max, op1=ALU.add))
                link(dve.scalar_tensor_tensor(out=gg[:, :, :], in0=gg[:, :, :], scalar=-1.0,
                                              in1=wide(alog[:, :].unsqueeze(1), [TT, DH]),
                                              op0=ALU.mult, op1=ALU.mult))
                own(dve.scalar_tensor_tensor(out=zz[:, 3], in0=zz[:, 0], scalar=0.0, in1=zz[:, 2],
                                             op0=ALU.min, op1=ALU.subtract), "small_lsg", 1)
                for t in range(TT):
                    dve.tensor_tensor(fcum[:, t], wide(tri[:, :].unsqueeze(1), [FH, P]),
                                      wide(zz[:, 3, t, 0:FH].unsqueeze(2), [FH, P]), ALU.mult)\
                       .then_inc(sem("fox_f"), 1)

            def sc(e, part, u):
                out = cy[:, e % 2, :, :]
                if part == 2:
                    dve.wait_ge(sem("unit_done"), u + 1)
                    dve.wait_ge(*took(u - 1))
                    own(dve.tensor_tensor(conv[:, e % 2, :, PAD:PAD + T], tiles(ps[:, units[u]["bank"], :]), out,
                                          ALU.mult), *took_name(u))
                    taps("sc_conv", 3, BT, 2 * e, e, out)
                if part == 0:
                    dve.wait_ge(sem("unit_done"), u + 1)
                    own(dve.tensor_tensor(out, tiles(ps[:, units[u]["bank"], :]), out, ALU.mult), *took_name(u))
                    dve.wait_ge(sem("sc_hi"), e + 1)
                    s = slice(BT + 2 * e, BT + 2 * e + 2)
                    dve.tensor_tensor(alo[:, s, :], out, ahi[:, s, :].bitcast(F32), ALU.subtract)\
                       .then_inc(sem("sc_lo"), 1)

            def took_name(u):
                g, k = units[u]["free"][0]
                return g, k + 1

            def taps(name, width, per_tap, tile0, j, out):
                for i in range(width - 1, -1, -1):
                    lag = width - 1 - i
                    for q in range(2):
                        src = conv[:, j % 2, q, PAD - lag:PAD - lag + T]
                        w = col(name, i * per_tap + tile0 + q) if width != 0 else None
                        if lag == 0:
                            ins = dve.tensor_scalar(out[:, q, :], src, w, None, ALU.mult)
                        else:
                            ins = dve.scalar_tensor_tensor(out=out[:, q, :], in0=src, scalar=w,
                                                           in1=out[:, q, :], op0=ALU.mult, op1=ALU.add)
                    if i > 0:
                        link(ins)
                own(ins, "conv_read", j + 1)

            def taps_ffn(tile0, j, out):
                for i in range(2, -1, -1):
                    for q in range(2):
                        src = conv[:, j % 2, q, PAD - 2 + i:PAD - 2 + i + T]
                        w = col(f"ffn_conv{i}", tile0 + q)
                        if i == 2:
                            ins = dve.tensor_scalar(out[:, q, :], src, w, None, ALU.mult)
                        else:
                            ins = dve.scalar_tensor_tensor(out=out[:, q, :], in0=src, scalar=w,
                                                           in1=out[:, q, :], op0=ALU.mult, op1=ALU.add)
                    if i > 0:
                        link(ins)
                own(ins, "conv_read", j + 1)

            def dn(e, u):
                dve.wait_ge(*took(u))
                taps("dn_conv", 4, 3 * BT, 2 * e, BT // 2 + e, dnT[:, 2 * e:2 * e + 2, :])

            def fox_norm():
                dve.wait_ge(*fox_ready[0])
                dve.wait_ge(*fox_ready[1])
                nh = 2 * FH
                qk = fqkv[:, :, 0:2 * FW].rearrange("p t (h d) -> p t h d", d=FD)
                sq = xs[:, :, 0:2 * FW].rearrange("p t (h d) -> p t h d", d=FD)
                link(dve.tensor_tensor(sq, qk, qk, ALU.mult))
                link(dve.tensor_reduce(ss[:, :, :], sq, AX.X, ALU.add))
                root(ss[:, :, :], 1.0 / FD)
                link(dve.tensor_tensor(qk, qk, wide(ss[:, :, :].unsqueeze(3), [TT, nh, FD]), ALU.mult))
                for i in range(2):
                    part = qk[:, :, i * FH:(i + 1) * FH, :]
                    dve.tensor_tensor(part, part, wide(gqk[:, i, :].unsqueeze(1).unsqueeze(1), [TT, FH, FD]),
                                      ALU.mult).then_inc(sem("fox_qk"), 1)

            def att_scores(w, g):
                b, maps = groups[g]
                k, width = len(maps), P * (b + 1)
                Sg = att[w]["S"][:, g % 2, :].rearrange("p (m j) -> p m j", m=k)
                halves_ = [(Sg[:, odd:k:2, :], by(ps[:, bank, 0:k // 2 * width], k // 2))
                           for odd, bank in ((0, 6 + g % 2), (1, 2 + g % 2))]
                dve.wait_ge(sem(f"att{w}_scored"), g + 1)
                if g >= 2:
                    dve.wait_ge(sem(f"att{w}_turned"), g - 1)
                diag = slice(b * P, width)
                if w == 0:
                    dve.wait_ge(sem("fox_bias"), 4)
                    for odd, (dst, src) in enumerate(halves_):
                        link(dve.tensor_tensor(dst, src, fbias[:, maps[0] + odd:maps[0] + k:2, 0:width], ALU.add))
                    link(dve.tensor_tensor(Sg[:, :, diag], Sg[:, :, diag], wide(cneg[:, :].unsqueeze(1), [k, P]),
                                           ALU.add))
                else:
                    for dst, src in halves_:
                        if b:
                            link(dve.tensor_copy(dst[:, :, 0:P], src[:, :, 0:P]))
                        link(dve.tensor_tensor(dst[:, :, diag], src[:, :, diag],
                                               wide(dneg[:, :].unsqueeze(1), [k // 2, P]), ALU.add))
                dve.tensor_reduce(nmax[:, g % 2, 0:k], Sg, AX.X, ALU.max, negate=True)\
                   .then_inc(sem(f"att{w}_max"), 1)
                exps = sum(len(m) for _, m in groups[:g + 1])
                dve.wait_ge(sem(f"att{w}_exp"), exps)
                r = rsum[:, g % 2, 0:k]
                link(dve.reciprocal(r, r))
                if w == 0:
                    dve.tensor_tensor(Sg, Sg, wide(r.unsqueeze(2), [k, width]), ALU.mult)\
                       .then_inc(sem("att0_p"), 1)
                    return
                r2 = rsum[:, g % 2, 0:k].rearrange("p (h m) -> p h m", m=2)[:, :, 1]
                link(dve.tensor_scalar(r2, r2, lamw[:, 2:3], None, ALU.mult))
                for i in range(0, k, 2):
                    link(dve.tensor_scalar(Sg[:, i, :], Sg[:, i, :], rsum[:, g % 2, i:i + 1], None, ALU.mult))
                    ins = dve.scalar_tensor_tensor(out=Sg[:, i, :], in0=Sg[:, i + 1, :],
                                                   scalar=rsum[:, g % 2, i + 1:i + 2], in1=Sg[:, i, :],
                                                   op0=ALU.mult, op1=ALU.add)
                ins.then_inc(sem("att1_p"), 1)

            def fox_out():
                for b in range(2):
                    dve.wait_ge(sem("fox_hi"), b + 1)
                    s = slice(2 * b, 2 * b + 2)
                    dve.tensor_tensor(alo[:, s, :], tiles(ps[:, b, :]), ahi[:, s, :].bitcast(F32), ALU.subtract)\
                       .then_inc(sem("fox_lo"), 1)

            def dn_square():
                dve.wait_ge(sem("dn_silu"), 6)
                qk = dnT[:, 0:2 * DH, :]
                dve.tensor_tensor(tiles(dsq), qk, qk, ALU.mult).then_inc(sem("dn_sq"), 1)

            def dn_unit():
                for b in range(4):
                    dve.wait_ge(sem("dn_ss"), b + 1)
                    ins = dve.tensor_scalar(dsq[:, 512 * b:512 * (b + 1)], ps[:, b, :], EPS, None, ALU.add)
                rooted(ins, dsq)
                q, k = dnT[:, 0:DH, :], dnT[:, DH:2 * DH, :]
                dve.scalar_tensor_tensor(out=q, in0=q, scalar=DV ** -0.5, in1=tiles(dsq[:, 0:1024]),
                                         op0=ALU.mult, op1=ALU.mult).then_inc(sem("dn_qk"), 1)
                dve.tensor_tensor(k, k, tiles(dsq[:, 1024:2048]), ALU.mult).then_inc(sem("dn_qk"), 1)
                dve.wait_ge(sem("dn_qk"), 2)

            def dn_cum():
                dve.wait_ge(sem("dn_gc"), 1)
                pg = ps[:, 6, 0:TT * 2 * DH].rearrange("p (t a h) -> p t a h", t=TT, a=2)
                link(dve.tensor_copy(gcol[:, :, :], pg[:, :, 0, :]))
                link(dve.tensor_copy(gx[:, :, 0, :], pg[:, :, 0, :]))
                dve.tensor_tensor(gx[:, :, 1, :], pg[:, :, 1, :], gcol[:, :, :], ALU.subtract)\
                   .then_inc(sem("dn_gx"), 1)
                dve.wait_ge(sem("dn_egx"), 1)
                link(dve.tensor_tensor(gx[:, :, 0, :], gx[:, :, 0, :], beta[:, :, :], ALU.mult))

            def dn_tok(t):
                dve.wait_ge(sem("dn_tokened"), 2 * t + 2)
                k, v = by(ps[:, 2 * t, :], DH), by(ps[:, 2 * t + 1, :], DH)
                dve.tensor_tensor(rhsk[:, t], k, wide(gx[:, t, 0, :].unsqueeze(2), [DH, P]), ALU.mult)\
                   .then_inc(sem("dn_tok"), 1)
                dve.tensor_tensor(kdec[:, t], k, wide(gx[:, t, 1, :].unsqueeze(2), [DH, P]), ALU.mult)\
                   .then_inc(sem("dn_tok"), 1)
                dve.tensor_tensor(vb[:, t], v, wide(beta[:, t, :].unsqueeze(2), [DH, P]), ALU.mult)\
                   .then_inc(sem("dn_tok"), 1)

            def dn_decay(t):
                if t >= 1:
                    dve.wait_ge(sem("dn_solved"), 2 * t)
                dve.tensor_tensor(X, wide(tri64[:, :].unsqueeze(1), [DH, P]),
                                  wide(gg[:, t, :].unsqueeze(2), [DH, P]), ALU.mult).then_inc(sem("dn_gb"), 1)
                dve.tensor_tensor(XT, wide(ident[:, :].unsqueeze(1), [DH, P]),
                                  wide(beta[:, t, :].unsqueeze(2), [DH, P]), ALU.mult).then_inc(sem("dn_gb"), 1)
                dve.wait_ge(sem("dn_eg"), t + 1)
                link(dve.tensor_tensor(DT, by(ps[:, 6, :], DH), wide(gcol[:, t, :].unsqueeze(2), [DH, P]),
                                       ALU.subtract))
                dve.tensor_scalar(DT, DT, 0.0, None, ALU.min).then_inc(sem("dn_dt"), 1)
                dve.tensor_copy(gt[:, t], EG[:, :, CH - 1:P:CH]).then_inc(sem("dn_gt"), 1)
                dve.wait_ge(sem("dn_edt"), t + 1)
                link(dve.tensor_tensor(DT, DT, wide(tri64[:, :].unsqueeze(1), [DH, P]), ALU.mult))

            def dn_kk(t):
                dve.wait_ge(sem("dn_kked"), 2 * t + 2)
                link(dve.tensor_tensor(LT, by(ps[:, 2 * t, :], DH), DT, ALU.mult))
                link(dve.tensor_tensor(LT, by(ps[:, 7, :], DH), LT, ALU.mult))
                link(dve.tensor_tensor(qkT[:, t], by(ps[:, 2 * t + 1, :], DH), DT, ALU.mult))
                q = dnT[:, 0:DH, t * P:(t + 1) * P]
                dve.tensor_tensor(q, q, EG, ALU.mult).then_inc(sem("dn_lt"), 1)

            def dn_x0(t):
                if t >= 1:
                    dve.wait_ge(sem("dn_solved"), 2 * t)
                link(dve.tensor_tensor(Bl, LT, wide(lev[:, 0, :].unsqueeze(1), [DH, P]), ALU.mult))
                dve.tensor_tensor(XT, wide(ident[:, :].unsqueeze(1), [DH, P]), Bl, ALU.subtract)\
                   .then_inc(sem("dn_x0"), 1)
                dve.wait_ge(sem("dn_x0"), t + 1)

            def dn_y(t, l):
                dve.tensor_tensor(Bl, LT, wide(lev[:, l, :].unsqueeze(1), [DH, P]), ALU.mult)\
                   .then_inc(sem("dn_B"), 1)

            def dn_z(t, l):
                dve.wait_ge(sem("dn_XBX"), 2 * (5 * t + l))
                own(dve.tensor_tensor(XT, XT, by(ps[:, 0, :], DH), ALU.subtract), "dn_X2", 2 * (5 * t + l) - 1)
                own(dve.tensor_tensor(X, X, by(ps[:, 1, :], DH), ALU.subtract), "dn_X2", 2 * (5 * t + l))

            def dn_sol(t):
                dve.wait_ge(sem("dn_solved"), 2 * t + 1)
                own(dve.tensor_copy(vb[:, t], by(ps[:, 6, :], DH)), "dn_u", t + 1)

            def dn_new(c):
                t, p0 = c // 2, CH * (c % 2)
                if c == 0:
                    return
                dve.wait_ge(sem("dn_kS"), c)
                part = vb[p0:p0 + CH, t]
                own(dve.tensor_tensor(part, part, by(ps[p0:p0 + CH, 0, :], DH), ALU.subtract), "dn_vnew", c)

            def dn_state(c):
                if c == NCH - 1:
                    return
                t = c // 2
                dve.wait_ge(sem("dn_supd"), c + 1)
                pS = by(ps[:, 1, :], DH)
                if c == 0:
                    own(dve.tensor_copy(S, pS), "dn_S", 1)
                    return
                for h in range(DH):
                    ins = dve.scalar_tensor_tensor(out=S[:, h, :], in0=S[:, h, :], scalar=gt[:, t, h, c % 2:c % 2 + 1],
                                                   in1=pS[:, h, :], op0=ALU.mult, op1=ALU.add)
                own(ins, "dn_S", c + 1)

            def head_norm(o, sq, heads, width):
                link(dve.tensor_tensor(sq, o, o, ALU.mult))
                r = ss[:, 0, 0:heads]
                link(dve.tensor_reduce(r, sq, AX.X, ALU.add))
                root(r, 1.0 / width)
                return dve.tensor_tensor(o, o, wide(r.unsqueeze(2), [heads, width]), ALU.mult)

            def dn_out(t):
                dve.wait_ge(sem("dn_ocopy"), t + 1)
                head_norm(rhsk[:, t], X, DH, DV).then_inc(sem("dn_onorm"), 1)
                dve.wait_ge(sem("dn_oturned"), t + 1)
                if t >= 1:
                    dve.wait_ge(sem("dn_hi"), t)
                own(dve.scalar_tensor_tensor(out=XT, in0=by(ps[:, 6, :], DH), scalar=col("dn_gain", 0),
                                             in1=zT[:, :, t * P:(t + 1) * P], op0=ALU.mult, op1=ALU.mult),
                    "dn_y2", t + 1)
                dve.wait_ge(sem("dn_hi"), t + 1)
                s = (slice(None), slice(2 * BT, 3 * BT), slice(t * P, (t + 1) * P))
                own(dve.tensor_tensor(alo[s], XT, ahi[s].bitcast(F32), ALU.subtract), "dn_lo", t + 1)

            def merge(n_, g, u, freed):
                dve.wait_ge(sem("unit_done"), u + 1)
                part = mg[:, 4 * g:4 * g + 4, :]
                two = ps[:, 2 * g:2 * g + 2, :].rearrange("p b (c t) -> p (b c) t", t=T)
                gate_ = gates[:, KD * n_ + 4 * g:KD * n_ + 4 * g + 4, :]
                if n_ == 0:
                    own(dve.tensor_tensor(part, two, gate_, ALU.mult), *freed)
                    return
                own(dve.tensor_tensor(mtmp[:, :, :], two, gate_, ALU.mult), *freed)
                ins = dve.tensor_tensor(part, part, mtmp[:, :, :], ALU.add)
                if n_ < NB - 1:
                    link(ins)
                    return
                own(ins, "merged", g + 1)
                dve.wait_ge(sem("merged_hi"), g + 1)
                s = slice(4 * g, 4 * g + 4)
                dve.tensor_tensor(hlo[:, s, :], part, hhi[:, s, :].bitcast(F32), ALU.subtract)\
                   .then_inc(sem("merged_lo"), 1)

            def resid(u):
                dve.wait_ge(sem("unit_done"), u + 1)
                for t in range(TT):
                    xt = x[:, t, :].rearrange("p (b n) -> p b n", b=2)
                    dve.tensor_tensor(xt, xt, ps[:, 2 * t:2 * t + 2, :], ALU.add).then_inc(sem(f"g{t}"), 1)

            def up(c, part, u, down):
                dve.wait_ge(*took(u))
                if part == 0 and c >= 1:
                    pass
                taps_ffn(UPT * part + 2 * c, BT // 2 + 6 + 2 * c + part, cy[:, part, :, :])
                if part == 1:
                    dve.wait_ge(sem("glu_silu"), c + 1)
                    own(dve.tensor_tensor(cy[:, 1, :, :], cy[:, 0, :, :], cy[:, 1, :, :], ALU.mult),
                        "glu_prod", c + 1)
                    dve.wait_ge(sem("glu_hi"), c + 1)
                    s = slice(2 * (c % 2), 2 * (c % 2) + 2)
                    own(dve.tensor_tensor(alo[:, s, :], cy[:, 1, :, :], ahi[:, s, :].bitcast(F32), ALU.subtract),
                        "glu_lo", c + 1)

            def ple_p():
                dve.wait_ge(sem("ple_hi"), 1)
                dve.tensor_tensor(alo[:, 0:2, :], tiles(ps[:, 6, :]), ahi[:, 0:2, :].bitcast(F32), ALU.subtract)\
                   .then_inc(sem("ple_lo"), 1)

            def ple_x(u):
                dve.wait_ge(sem("unit_done"), u + 1)
                for t in range(TT):
                    st_ = sg[:, t, :].rearrange("p (b n) -> p b n", b=2)
                    own(dve.tensor_tensor(st_, ps[:, 2 * t:2 * t + 2, :], st_, ALU.mult), f"g{t}",
                        units[u]["free"][t][1] + 1)
                    dve.tensor_tensor(x[:, t, :], x[:, t, :], sg[:, t, :], ALU.add).then_inc(sem("ple_added"), 1)

            def ab_qk(e, u):
                if e == 0:
                    dve.memset(pu[:, :, 0:W0], 0.0).then_inc(sem("pool_zero"), 1)

            def lam():
                dve.wait_ge(sem("lam_in"), 16)
                w4 = lamr[:, :, :].rearrange("p (a b) d -> p a b d", b=2)
                link(dve.tensor_tensor(w4[:, :, 0, :], w4[:, :, 0, :], w4[:, :, 1, :], ALU.mult))
                dve.tensor_reduce(lamw[:, 0:2], w4[:, :, 0, :], AX.X, ALU.add).then_inc(sem("lam_sum"), 1)
                dve.wait_ge(sem("lam_exp"), 1)
                link(dve.tensor_tensor(lamw[:, 2:3], lamw[:, 1:2], lamw[:, 0:1], ALU.subtract))
                link(dve.tensor_scalar(lamw[:, 2:3], lamw[:, 2:3], -LI, None, ALU.add))

            def pool_win():
                dve.wait_ge(*pool_ready[0])
                dve.wait_ge(*pool_ready[1])
                E_ = W0 + T
                sums, src = (p1, p2, p3, p4), pu
                at = 0
                for l, dst in enumerate(sums):
                    s, g0 = 1 << l, l
                    at = 2 * s - 1
                    link(dve.tensor_tensor(dst[:, g0:4, at:E_], src[:, g0:4, at:E_], src[:, g0:4, at - s:E_ - s],
                                           ALU.add))
                    src = dst
                for g, w in enumerate(POOLS):
                    link(dve.tensor_tensor(pfix[:, g, :], sums[g][:, g, W0:W0 + 16], inv[:, g, :], ALU.mult))
                    link(dve.scalar_tensor_tensor(out=pr[:, g, 16:T], in0=sums[g][:, g, W0 + 16:E_],
                                                  scalar=1.0 / w, in1=pu[:, g, W0 + 16:E_],
                                                  op0=ALU.mult, op1=ALU.subtract))
                own(dve.tensor_tensor(pr[:, :, 0:16], pfix, pu[:, :, W0:W0 + 16], ALU.subtract), "pool_r", 1)

            def pool_mm():
                dve.wait_ge(sem("pool_mmed"), 1)
                for g in range(4):
                    ins = dve.tensor_scalar(pr[:, g, :], tiles(ps[:, 2 + g // 2, :])[:, g % 2, :],
                                            col("pool_scale", g), None, ALU.mult)
                own(ins, "pool_y", 1)
                dve.wait_ge(sem("pool_hi"), 1)
                dve.tensor_tensor(alo[:, 4:8, :], pr, ahi[:, 4:8, :].bitcast(F32), ALU.subtract)\
                   .then_inc(sem("pool_lo"), 1)

            def ab_out(b):
                dve.wait_ge(sem("ab_ocopy"), b + 1)
                link(head_norm(ob[:, b], oy, 4, P))
                dve.tensor_scalar(ob[:, b], ob[:, b], 1.0 - LI, None, ALU.mult).then_inc(sem("ab_onorm"), 1)
                dve.wait_ge(sem("ab_oturned"), b + 1)
                own(dve.tensor_scalar(oy, by(ps[:, 6, :], 4), col("subln", 0), None, ALU.mult), "ab_y", b + 1)
                dve.wait_ge(sem("ab_hi"), b + 1)
                s = (slice(None), slice(0, 4), slice(b * P, (b + 1) * P))
                own(dve.tensor_tensor(alo[s], oy, ahi[s].bitcast(F32), ALU.subtract), "ab_lo", b + 1)

            def relu2(i, c, u, down):
                dve.wait_ge(*took(u))
                y = cy[:, i % 2, :, :]
                own(dve.tensor_tensor(y, y, y, ALU.mult), "relu2_sq", i + 1)
                dve.wait_ge(sem("relu2_hi"), i + 1)
                s = slice(2 * (c % 2), 2 * (c % 2) + 2)
                dve.tensor_tensor(alo[:, s, :], y, ahi[:, s, :].bitcast(F32), ALU.subtract)\
                   .then_inc(sem("relu2_lo"), 1)

            def gla_gate():
                dve.wait_ge(sem("gla_gated"), 2)
                two = ps[:, 0:2, :]
                link(dve.tensor_scalar(gmin, two, 0.0, None, ALU.min))
                dve.scalar_tensor_tensor(out=gla, in0=gmin, scalar=-2.0, in1=two, op0=ALU.mult, op1=ALU.add).then_inc(sem("gla_abs"), 1)
                dve.wait_ge(sem("gla_ln"), 2)
                own(dve.tensor_tensor(gla, gmin, gla, ALU.subtract), "gla_la", 1)

            def gla_pairs(l):
                dve.wait_ge(sem("gla_paired"), 2 * l + 2)
                two = ps[:, 6:8, :].rearrange("p b (g i) -> p (b g) i", i=P)
                mask = ident[:, :] if l == 0 else lev[:, l - 1, :]
                dst = attn if l == 0 else atmp
                own(dve.tensor_tensor(dst, two, wide(mask.unsqueeze(1), [TT * GH, P]), ALU.mult), "gla_took", l + 1)
                if l:
                    link(dve.tensor_tensor(attn, attn, atmp, ALU.add))

            def halves(ap, l):
                return ap.rearrange("p h t -> p (h t)").rearrange("p (m two s) -> p m two s", two=2, s=1 << l)

            def gla_level(l):
                s = 1 << l
                if l == 0:
                    dve.wait_ge(sem("gla_b"), 2)
                    dve.wait_ge(*gla_qk_ready[0])
                    dve.wait_ge(*gla_qk_ready[1])
                b_, e_, c_ = halves(bcum, l), halves(E1, l), halves(Cl, l)
                q_, k_ = halves(gqT[:, 0:GH, :], l), halves(gqT[:, GH:2 * GH, :], l)
                m = GH * T // (2 * s)
                ref = wide(b_[:, :, 0, s - 1:s], [m, s])
                dve.tensor_tensor(e_[:, :, 1, :], b_[:, :, 1, :], ref, ALU.subtract)
                own(dve.tensor_tensor(e_[:, :, 0, :], ref, b_[:, :, 0, :], ALU.subtract), "gla_arg", l + 1)
                dve.wait_ge(sem("gla_E"), l + 1)
                dve.tensor_tensor(c_[:, :, 1, :], e_[:, :, 1, :], q_[:, :, 1, :], ALU.mult)
                own(dve.tensor_tensor(c_[:, :, 0, :], e_[:, :, 0, :], k_[:, :, 0, :], ALU.mult), "gla_C", l + 1)

            def gla_decay():
                b_ = bcum.rearrange("p h (c s) -> p (h c) s", s=CH)
                e_ = E1.rearrange("p h (c s) -> p (h c) s", s=CH)
                own(dve.tensor_tensor(e_, wide(b_[:, :, CH - 1:CH], [GH * NCH, CH]), b_, ALU.subtract), "gla_arg", 7)
                dve.wait_ge(sem("gla_EB"), 1)
                q = gqT[:, 0:GH, :]
                link(dve.tensor_tensor(q, q, EB, ALU.mult))
                dve.wait_ge(sem("gla_E"), 7)
                own(dve.tensor_tensor(Cl, E1, gqT[:, GH:2 * GH, :], ALU.mult), "gla_C", 7)

            def gla_chunk(c):
                if c == NCH - 1:
                    return
                dve.wait_ge(sem("gla_supd"), 2 * c + 2)
                pS = ps[:, 6:8, :].rearrange("p b (h d) -> p (b h) d", d=GV)
                if c == 0:
                    own(dve.tensor_copy(GS, pS), "gla_S", 1)
                    return
                for h in range(GH):
                    ins = dve.scalar_tensor_tensor(out=GS[:, h, :], in0=GS[:, h, :],
                                                   scalar=EB[:, h, CH * c + CH - 1:CH * c + CH],
                                                   in1=pS[:, h, :], op0=ALU.mult, op1=ALU.add)
                own(ins, "gla_S", c + 1)

            def gla_out(t):
                dve.wait_ge(sem("gla_ocopy"), t + 1)
                head_norm(og, gsq, GH, GV).then_inc(sem("gla_onorm"), 1)
                for b in range(2):
                    dve.wait_ge(sem("gla_oturned"), 2 * t + b + 1)
                    for i in range(4 * b, 4 * b + 4):
                        ins = dve.scalar_tensor_tensor(out=gy[:, i, :], in0=by(ps[:, 6 + b, :], 4)[:, i % 4, :],
                                                       scalar=col("gla_norm", i),
                                                       in1=sgT[:, i, t * P:(t + 1) * P],
                                                       op0=ALU.mult, op1=ALU.mult)
                    own(ins, "gla_y", 2 * t + b + 1)
                for b in range(2):
                    dve.wait_ge(sem("gla_hi"), 2 * t + b + 1)
                    s = (slice(None), slice(4 * b, 4 * b + 4), slice(t * P, (t + 1) * P))
                    own(dve.tensor_tensor(alo[s], gy[:, 4 * b:4 * b + 4, :], ahi[s].bitcast(F32), ALU.subtract),
                        "gla_lo", 2 * t + b + 1)

            def final(waits):
                dve.wait_ge(sem("nfin_in"), 16)
                for t in range(TT):
                    dve.wait_ge(sem("norm_sum"), TT * 7 + t + 1)
                    root(ss[:, t, 0:1], 1.0 / D)
                    dve.scalar_tensor_tensor(out=xs[:, t, :], in0=x[:, t, :], scalar=ss[:, t, 0:1], in1=nfin,
                                             op0=ALU.mult, op1=ALU.mult).then_inc(sem("final_x"), 1)

            fox_ready = [(sem(s[3][0]), s[3][1]) for s in order if s[0] == "fox_qkv"][1:]
            pool_ready = [took(s[2]) for s in order if s[0] == "pool_u"]
            gla_qk_ready = [took(s[2]) for s in order if s[0] == "gla_qk"][2:]
            parts = dict(norm=norm, small=small, sc=sc, dn=dn, fox_norm=fox_norm, att_scores=att_scores,
                         fox_out=fox_out, dn_square=dn_square, dn_unit=dn_unit, dn_cum=dn_cum, dn_tok=dn_tok,
                         dn_decay=dn_decay, dn_kk=dn_kk, dn_x0=dn_x0, dn_y=dn_y, dn_z=dn_z, dn_sol=dn_sol,
                         dn_new=dn_new, dn_state=dn_state, dn_out=dn_out, merge=merge, resid=resid, up=up,
                         ple_p=ple_p, ple_x=ple_x, ab_qk=ab_qk, lam=lam, pool_win=pool_win, pool_mm=pool_mm,
                         ab_out=ab_out, relu2=relu2, gla_gate=gla_gate, gla_pairs=gla_pairs,
                         gla_level=gla_level, gla_decay=gla_decay, gla_chunk=gla_chunk, gla_out=gla_out,
                         final=final)
            parts["mm"] = lambda u: split_low(u + LEAD) if u + LEAD < NU else None
            dve.wait_ge(sem("constants"), n_const[0])
            for u in range(LEAD):
                split_low(u)
            for s in order:
                if s[0] in parts:
                    parts[s[0]](*s[1:])

        @block.tensor
        def _(pe):
            def mm(u):
                w = units[u]
                s = u % SPLIT
                pe.wait_ge(sem("lo_done"), u + 1)
                for name, v in w["needs"]:
                    pe.wait_ge(sem(name), v)
                for name, v in w["free"]:
                    if v:
                        pe.wait_ge(sem(name), v)
                hi, lo = (hhi, hlo) if w["act"] == "h" else (ahi, alo)
                if w["kind"] in "CB":
                    nk, width = (KD, 256) if w["kind"] == "C" else (4, 512)
                    k0 = w.get("k0", 0)
                    for ct in range(width // P):
                        out = ps[:, w["bank"] + ct // 2, (ct % 2) * T:(ct % 2 + 1) * T]
                        for k in range(nk):
                            at = k * width + ct * P
                            wh, wl = whi[:, s, at:at + P], wlo[:, s, at:at + P]
                            pe.matmul(out, wh, hi[:, k0 + k, :], start=k == 0, stop=False)
                            pe.matmul(out, wh, lo[:, k0 + k, :], start=False, stop=False)
                            ins = pe.matmul(out, wl, hi[:, k0 + k, :], start=False, stop=k == nk - 1)
                else:
                    nk, banks = (4, [(t, w.get("bank", 0) + t, 0) for t in range(TT)]) if w["kind"] == "T" else \
                        (2, [(t, 2 * t + b, b) for t in range(TT) for b in range(2)])
                    width = 512 if w["kind"] == "T" else D
                    for t, bank, b in banks:
                        out = ps[:, bank, :]
                        for k in range(nk):
                            at = k * width + 512 * b
                            wh, wl = whi[:, s, at:at + 512], wlo[:, s, at:at + 512]
                            xh = hi[:, w["k0"] + k, t * P:(t + 1) * P]
                            xl = lo[:, w["k0"] + k, t * P:(t + 1) * P]
                            first, last = w["first"] and k == 0, w["last"] and k == nk - 1
                            pe.matmul(out, xh, wh, start=first, stop=False)
                            pe.matmul(out, xh, wl, start=False, stop=False)
                            ins = pe.matmul(out, xl, wh, start=False, stop=last)
                ins.then_inc(sem("unit_done"), 1)

            def norm(i, waits):
                if i == 0:
                    pe.wait_ge(sem("params_in"), 16 * n_par)
                    for b in range(3):
                        ins = pe.transpose(ps[:, 7, b * P:(b + 1) * P], rows[:, b, :], ident[:, :])
                    ins.then_inc(sem("colp_turned"), 1)
                for b in range(4):
                    for t in range(TT):
                        pe.wait_ge(sem("norm_scaled"), TT * i + t + 1)
                        for k in (2 * b, 2 * b + 1):
                            at = (k % 2) * T + t * P
                            ins = pe.transpose(ps[:, b, at:at + P], xs[:, t, k * P:(k + 1) * P], ident[:, :])
                    ins.then_inc(sem("norm_turned"), 1)

            def small():
                pe.wait_ge(sem("small_in"), 32)
                pe.wait_ge(sem("norm_lo"), KD)
                for t in range(TT):
                    for k in range(KD):
                        for j, part in enumerate((hhi, hlo)):
                            ins = pe.matmul(ps[:, 6, t * NSM:(t + 1) * NSM], part[:, k, t * P:(t + 1) * P].bitcast(F32),
                                            wsm[:, k, :], start=k == 0 and j == 0, stop=k == KD - 1 and j == 1)
                ins.then_inc(sem("small_done"), 1)

            def fox_turn(t):
                pe.wait_ge(sem("fox_qk"), 2)
                for b in range(2):
                    for c in range(4):
                        at = FW * b + c * P
                        ins = pe.transpose(ps[:, 2 * t + b, c * P:(c + 1) * P], fqkv[:, t, at:at + P], ident[:, :])
                    ins.then_inc(sem("fox_turned"), 1)

            def fox_cum(t):
                pe.wait_ge(sem("fox_f"), TT)
                pe.wait_ge(sem("fox_T"), 4)
                for b in range(2):
                    out = by(ps[:, 2 * t + b, :], 4)
                    if t:
                        lf = zz[:, 3, 0, 4 * b:4 * b + 4].unsqueeze(2).to_broadcast([P, 4, P])
                        pe.matmul(out, ones[:, :], lf, start=True, stop=False)
                    pe.matmul(out, ones[:, :], fcum[:, t, 4 * b:4 * b + 4, :], start=t == 0, stop=True)\
                      .then_inc(sem("fox_cummed"), 1)

            def att_scores(w, g):
                b, maps = groups[g]
                width = P * (b + 1)
                q, k = att[w]["q"], att[w]["k"]
                if g == 0:
                    if w == 0:
                        pe.wait_ge(sem("fox_T"), 4)
                        pe.wait_ge(sem("fox_bias"), 4)
                    else:
                        for r in ab_qk_ready:
                            pe.wait_ge(*r)
                if g >= 2:
                    pe.wait_ge(sem(f"att{w}_PT"), g - 1)
                for i, f in enumerate(maps):
                    half = slice(FD * (f % 2), FD * (f % 2) + FD)
                    bank, at = (6 if f % 2 == 0 else 2) + g % 2, (i // 2) * width
                    ins = pe.matmul(ps[:, bank, at:at + width], q[half, f // 2, b * P:(b + 1) * P],
                                    k[half, f // 2, 0:width], start=True, stop=True)
                ins.then_inc(sem(f"att{w}_scored"), 1)

            def att_turn(w, g):
                pe.wait_ge(sem(f"att{w}_p"), g + 1)
                for i, (at, _, _) in enumerate(turned(w, g)):
                    ins = pe.transpose(ps[:, 6 + g % 2, i * P:(i + 1) * P], att[w]["S"][:, g % 2, at:at + P],
                                       ident[:, :])
                ins.then_inc(sem(f"att{w}_turned"), 1)

            def att_values(w, g):
                b, _ = groups[g]
                pe.wait_ge(sem(f"att{w}_PT"), g + 1)
                if g == 0:
                    if w == 0:
                        pe.wait_ge(sem("fox_bias"), 4)
                    else:
                        pe.wait_ge(*ab_v_ready)
                for i, (_, f, kt) in enumerate(turned(w, g)):
                    pT = att[w]["PT"][:, g % 2, i * P:(i + 1) * P]
                    if w == 0:
                        at = (f // 2 % 2) * T + b * P
                        ins = pe.matmul(ps[FD * (f % 2):FD * (f % 2) + FD, f // 4, at:at + P],
                                        fqkv[:, kt, 2 * FW + f * FD:2 * FW + (f + 1) * FD], pT,
                                        start=kt == 0, stop=kt == b)
                    else:
                        ins = pe.matmul(ps[:, b, f * P:(f + 1) * P], pT, vtok[:, kt, f * P:(f + 1) * P],
                                        start=kt == 0, stop=kt == b)
                ins.then_inc(sem(f"att{w}_used"), 1)

            def dn_square():
                pe.wait_ge(sem("dn_sq"), 1)
                pe.wait_ge(sem("fox_lo"), 2)
                for b in range(4):
                    pe.matmul(ps[:, b, :], ones[:, :], dsq[:, 512 * b:512 * (b + 1)], start=True, stop=True)\
                      .then_inc(sem("dn_ss"), 1)

            def dn_cum():
                pe.wait_ge(sem("att0_PT"), 6)
                for t in range(TT):
                    for j, m in enumerate((tri64, blk64)):
                        at = (2 * t + j) * DH
                        ins = pe.matmul(ps[:, 6, at:at + DH], m[:, :], gg[:, t, :], start=True, stop=True)
                ins.then_inc(sem("dn_gc"), 1)

            def dn_tok(t):
                pe.wait_ge(sem("dn_qk"), 2)
                for j, c0 in enumerate((DH, 2 * DH)):
                    for h in range(DH):
                        ins = pe.transpose(ps[:, 2 * t + j, h * P:(h + 1) * P], dnT[:, c0 + h, t * P:(t + 1) * P],
                                           ident[:, :])
                    ins.then_inc(sem("dn_tokened"), 1)

            def dn_decay(t):
                pe.wait_ge(sem("dn_gb"), 2 * t + 2)
                if t == 0:
                    pe.wait_ge(sem("dn_gx"), 1)
                else:
                    pe.wait_ge(sem("dn_u"), t)
                    pe.wait_ge(sem("dn_kcT"), t)
                pe.matmul(by(ps[:, 7, :], DH), ones[:, :], XT, start=True, stop=True)
                pe.matmul(by(ps[:, 6, :], DH), ones[:, :], X, start=True, stop=True).then_inc(sem("dn_grow"), 1)

            def dn_kk(t):
                pe.wait_ge(sem("dn_tok"), 3 * t + 3)
                for j in range(2):
                    for h in range(DH):
                        cols_ = slice(t * P, (t + 1) * P)
                        ins = pe.matmul(ps[:, 2 * t + j, h * P:(h + 1) * P], dnT[:, DH + h, cols_],
                                        dnT[:, (DH if j == 0 else 0) + h, cols_], start=True, stop=True)
                    ins.then_inc(sem("dn_kked"), 1)

            def dn_x0(t):
                pe.wait_ge(sem("dn_x0"), t + 1)
                pe.wait_ge(sem("dn_edt"), t + 1)
                for h in range(DH):
                    ins = pe.transpose(ps[:, 6, h * P:(h + 1) * P], XT[:, h, :], ident[:, :])
                ins.then_inc(sem("dn_x0_turned"), 1)

            def dn_y(t, l):
                pe.wait_ge(sem("dn_B"), 5 * t + l)
                pe.wait_ge(sem("dn_X"), t + 1)
                if l > 1:
                    pe.wait_ge(sem("dn_X2"), 2 * (5 * t + l - 1))
                for h in range(DH):
                    ins = pe.matmul(ps[:, 7, h * P:(h + 1) * P], Bl[:, h, :], X[:, h, :], start=True, stop=True)
                ins.then_inc(sem("dn_BX"), 1)

            def dn_z(t, l):
                pe.wait_ge(sem("dn_Y"), 5 * t + l)
                for h in range(DH):
                    ins = pe.matmul(ps[:, 0, h * P:(h + 1) * P], Y[:, h, :], XT[:, h, :], start=True, stop=True)
                ins.then_inc(sem("dn_XBX"), 1)
                for h in range(DH):
                    ins = pe.matmul(ps[:, 1, h * P:(h + 1) * P], XT[:, h, :], Y[:, h, :], start=True, stop=True)
                ins.then_inc(sem("dn_XBX"), 1)

            def dn_sol(t):
                pe.wait_ge(sem("dn_X2"), 2 * (5 * t + 5))
                for h in range(DH):
                    ins = pe.matmul(ps[:, 6, h * P:(h + 1) * P], XT[:, h, :], vb[:, t, h, :], start=True, stop=True)
                ins.then_inc(sem("dn_solved"), 1)
                for h in range(DH):
                    ins = pe.matmul(ps[:, 7, h * P:(h + 1) * P], rhsk[:, t, h, :], XT[:, h, :], start=True, stop=True)
                ins.then_inc(sem("dn_solved"), 1)

            def dn_new(c):
                if c == 0:
                    return
                t, p0 = c // 2, CH * (c % 2)
                pe.wait_ge(sem("dn_S"), c)
                pe.wait_ge(sem("dn_kcT"), t + 1)
                for h in range(DH):
                    ins = pe.matmul(ps[p0:p0 + CH, 0, h * P:(h + 1) * P], kcT[:, h, c * CH:(c + 1) * CH], S[:, h, :],
                                    start=True, stop=True)
                ins.then_inc(sem("dn_kS"), 1)

            def dn_state(c):
                t, p0 = c // 2, CH * (c % 2)
                own_ = slice(p0, p0 + CH)
                pe.wait_ge(sem("dn_u"), t + 1)
                if c:
                    pe.wait_ge(sem("dn_vnew"), c)
                for h in range(DH):
                    out = ps[own_, 2 + t, h * P:(h + 1) * P]
                    if c:
                        pe.matmul(out, dnT[:, h, c * CH:(c + 1) * CH], S[:, h, :], start=True, stop=False)
                    ins = pe.matmul(out, qkT[own_, t, h, own_], vb[own_, t, h, :], start=c == 0, stop=True)
                ins.then_inc(sem("dn_o"), 1)
                if c < NCH - 1:
                    for h in range(DH):
                        ins = pe.matmul(ps[:, 1, h * P:(h + 1) * P], kdec[own_, t, h, :], vb[own_, t, h, :],
                                        start=True, stop=True)
                    ins.then_inc(sem("dn_supd"), 1)

            def dn_out(t):
                pe.wait_ge(sem("dn_onorm"), t + 1)
                pe.wait_ge(sem("dn_u"), TT)
                if t:
                    pe.wait_ge(sem("dn_y2"), t)
                for h in range(DH):
                    ins = pe.transpose(ps[:, 6, h * P:(h + 1) * P], rhsk[:, t, h, :], ident[:, :])
                ins.then_inc(sem("dn_oturned"), 1)

            def ple_p():
                pe.wait_ge(sem("p_in"), 16)
                for k in range(2):
                    for t in range(TT):
                        at = k * T + t * P
                        ins = pe.transpose(ps[:, 6, at:at + P], ptok[:, t, k * P:(k + 1) * P], ident[:, :])
                ins.then_inc(sem("p_turned"), 1)

            def pool_mm():
                pe.wait_ge(sem("pool_r"), 1)
                pe.wait_ge(sem("pw_in"), 16)
                for g in range(4):
                    ins = pe.matmul(ps[:, 2 + g // 2, (g % 2) * T:(g % 2 + 1) * T], pw[:, g, :], pr[:, g, :],
                                    start=True, stop=True)
                ins.then_inc(sem("pool_mmed"), 1)

            def ab_out(b):
                pe.wait_ge(sem("ab_onorm"), b + 1)
                pe.wait_ge(sem("att1_PT"), 6)
                if b:
                    pe.wait_ge(sem("ab_y"), b)
                for h in range(4):
                    ins = pe.transpose(ps[:, 6, h * P:(h + 1) * P], ob[:, b, h, :], ident[:, :])
                ins.then_inc(sem("ab_oturned"), 1)

            def gla_low():
                pe.wait_ge(sem("norm_lo"), 6 * KD)
                for k in range(KD):
                    for j, part in enumerate((hhi, hlo)):
                        ins = pe.matmul(ps[0:GR, 6, 0:T], wlow[:, k, :], part[:, k, :].bitcast(F32),
                                        start=k == 0 and j == 0, stop=k == KD - 1 and j == 1)
                ins.then_inc(sem("gla_lowed"), 1)

            def gla_gate():
                pe.wait_ge(sem("gla_gkT"), 1)
                pe.wait_ge(sem("gla_par"), 32)
                for t in range(TT):
                    pe.matmul(ps[:, t, :], ones[0:1, :], bgk[:, :], start=True, stop=False)
                    pe.matmul(ps[:, t, :], gkT[0:GR, t * P:(t + 1) * P], wgu[:, :], start=False, stop=True)\
                      .then_inc(sem("gla_gated"), 1)

            def gla_cum():
                pe.wait_ge(sem("gla_la"), 1)
                for b in range(2):
                    for h in (2 * b, 2 * b + 1):
                        for t in range(TT):
                            at = (h % 2) * T + t * P
                            ins = pe.matmul(ps[:, 6 + b, at:at + P], gla[:, t, h * P:(h + 1) * P], tri64[:, :],
                                            start=True, stop=True)
                    ins.then_inc(sem("gla_cummed"), 1)

            def gla_pairs(l):
                if l == 0:
                    pe.wait_ge(sem("gla_b"), 2)
                    for r in gla_qk_ready:
                        pe.wait_ge(*r)
                else:
                    pe.wait_ge(sem("gla_C"), l)
                    pe.wait_ge(sem("gla_took"), l)
                for t in range(TT):
                    for h in range(GH):
                        c_ = slice(t * P, (t + 1) * P)
                        lhs = Cl[:, h, c_] if l else gqT[:, GH + h, c_]
                        rhs = Cl[:, h, c_] if l else gqT[:, h, c_]
                        ins = pe.matmul(ps[:, 6 + t, h * P:(h + 1) * P], lhs, rhs, start=True, stop=True)
                    ins.then_inc(sem("gla_paired"), 1)

            def gla_ktok():
                pe.wait_ge(sem("gla_C"), 7)
                pe.wait_ge(sem("gla_took"), 7)
                for t in range(TT):
                    for h in range(GH):
                        ins = pe.transpose(ps[:, 6 + t, h * P:(h + 1) * P], Cl[:, h, t * P:(t + 1) * P], ident[:, :])
                    ins.then_inc(sem("gla_kturned"), 1)

            def gla_chunk(c):
                t, p0 = c // 2, CH * (c % 2)
                own_ = slice(p0, p0 + CH)
                if c == 0:
                    pe.wait_ge(*gla_v_ready[0])
                    pe.wait_ge(*gla_v_ready[1])
                    pe.wait_ge(sem("gla_kdt"), 2)
                else:
                    pe.wait_ge(sem("gla_S"), min(c, NCH - 1))
                for h in range(GH):
                    out = ps[own_, 2 * t + h // 2, (h % 2) * GV:(h % 2 + 1) * GV]
                    if c:
                        pe.matmul(out, gqT[:, h, c * CH:(c + 1) * CH], GS[:, h, :], start=True, stop=False)
                    ins = pe.matmul(out, attn[own_, t * GH + h, own_], vg[own_, t, h * GV:(h + 1) * GV],
                                    start=c == 0, stop=True)
                ins.then_inc(sem("gla_o"), 1)
                if c < NCH - 1:
                    for b in range(2):
                        for h in (2 * b, 2 * b + 1):
                            ins = pe.matmul(ps[:, 6 + b, (h % 2) * GV:(h % 2 + 1) * GV], kdt[own_, t * GH + h, :],
                                            vg[own_, t, h * GV:(h + 1) * GV], start=True, stop=True)
                        ins.then_inc(sem("gla_supd"), 1)

            def gla_out(t):
                pe.wait_ge(sem("gla_onorm"), t + 1)
                if t:
                    pe.wait_ge(sem("gla_y"), 2 * t)
                else:
                    pe.wait_ge(sem("gla_S"), NCH - 1)
                for b in range(2):
                    for i in range(4):
                        at = (4 * b + i) * P
                        h, d0 = at // GV, at % GV
                        ins = pe.transpose(ps[:, 6 + b, i * P:(i + 1) * P], og[:, h, d0:d0 + P], ident[:, :])
                    ins.then_inc(sem("gla_oturned"), 1)

            ab_qk_ready = [took(s[2]) for s in order if s[0] == "ab_qk"][2:]
            ab_v_ready = [took(s[1] - 1) for s in order if s[0] == "ab_v"][0]
            gla_qk_ready = [took(s[2]) for s in order if s[0] == "gla_qk"][2:]
            v0 = [s[1] for s in order if s[0] == "gla_v"][0] - 3
            gla_v_ready = [(sem(g), v + 1) for g, v in units[v0]["free"]]
            parts = dict(mm=mm, norm=norm, small=small, fox_turn=fox_turn, fox_cum=fox_cum,
                         att_scores=att_scores, att_turn=att_turn, att_values=att_values,
                         dn_square=dn_square, dn_cum=dn_cum, dn_tok=dn_tok, dn_decay=dn_decay, dn_kk=dn_kk,
                         dn_x0=dn_x0, dn_y=dn_y, dn_z=dn_z, dn_sol=dn_sol, dn_new=dn_new, dn_state=dn_state,
                         dn_out=dn_out, ple_p=ple_p, pool_mm=pool_mm, ab_out=ab_out, gla_low=gla_low,
                         gla_gate=gla_gate, gla_cum=gla_cum, gla_pairs=gla_pairs, gla_ktok=gla_ktok,
                         gla_chunk=gla_chunk, gla_out=gla_out)
            pe.wait_ge(sem("constants"), n_const[0])
            for s in order:
                if s[0] in parts:
                    parts[s[0]](*s[1:])


_INS = ["x", "p", "g_mix", "w_in", "b_fox_f", "fox_q_gain", "fox_k_gain", "sc_conv_w", "dn_conv_w", "dn_a_log",
        "dn_dt_bias", "dn_norm_gain", "w_branch", "w_o", "g_ffn", "w_up", "ffn_conv_w", "w_down", "g_ple",
        "w_ple_gate", "w_ple", "norm_mix_2", "norm_ffn_2", "norm_final_2", "ab_w_in_2", "ab_lambda_2",
        "ab_subln_2", "pool_w_2", "pool_scale_2", "ab_w_out_2", "gla_w_in_2", "gla_w_gk_up_2", "gla_b_gk_2",
        "gla_norm_2", "gla_w_out_2", "ffn_w1_2", "ffn_w2_2"]


def kernel(**inputs):
    import numpy as _np
    import concourse.bacc as _bacc
    from concourse import mybir as _mybir
    from concourse.bass_utils import run_bass_kernel_spmd as _run

    nc = _bacc.Bacc("TRN2", target_bir_lowering=False, num_devices=1)
    arrays, args = {}, {}
    for name in _INS:
        v = _np.ascontiguousarray(inputs[name])
        arrays[f"in_{name}"] = v
        args[name] = nc.dram_tensor(f"in_{name}", v.shape, _mybir.dt.from_np(v.dtype), kind="ExternalInput").ap()
    shape = inputs["x"].shape
    args["out"] = nc.dram_tensor("out_0", shape, _mybir.dt.from_np(_np.dtype("float32")), kind="ExternalOutput").ap()
    build(nc, args)
    r = _run(nc, [arrays], core_ids=[0])
    return r.results[0]["out_0"]
```

```python
import math
from contextlib import ExitStack

import concourse.bass as bass
from concourse import mybir

P = 128
ALU = mybir.AluOpType
ACT = mybir.ActivationFunctionType
AX = mybir.AxisListType
F32 = mybir.dt.float32
F32R = mybir.dt.float32r

UNIT = 2048
RAW = 3
SPLIT = 3
LEAD = 2
PAD = 4
BIG = 1.0e30
EPS = 1e-6


def build(nc, a):
    T, D = a["x"].shape[1:]
    TT = T // P
    KD = D // P
    FH, FD = a["b_fox_f"].shape[1], a["fox_q_gain"].shape[1]
    FW = FH * FD
    SW = a["sc_conv_w"].shape[2]
    DH, DV = a["dn_a_log"].shape[1], a["dn_norm_gain"].shape[1]
    DW = DH * DV
    NB = a["w_branch"].shape[1]
    BT = SW // P
    DFF = a["w_down"].shape[1]
    UPT = DFF // P
    PLE = a["w_ple"].shape[1]
    CH = 64
    NCH = T // CH
    LI = 0.8 - 0.6 * math.exp(0.0)
    GK = a["gla_w_gk_up_2"].shape[2]
    GR = a["gla_w_gk_up_2"].shape[1]
    GH, GV = a["gla_norm_2"].shape[1:]
    DFF2 = a["ffn_w2_2"].shape[1]
    POOLS = (2, 4, 8, 16)

    w_in = a["w_in"][0]
    o_fox, o_f = 0, 3 * FW
    o_sc = o_f + FH
    o_dn = o_sc + 3 * SW
    o_b = o_dn + 3 * DW
    o_a = o_b + DH
    o_z = o_a + DH
    o_gate = o_z + DW
    NSM = FH + 2 * DH

    units = []
    taken = {"c4": 0, "c5": 0, "g0": 0, "g1": 0}

    def rows_by_tile(w, r0, rows, c0, cols):
        return w[r0:r0 + rows, c0:c0 + cols].rearrange("(k p) n -> p k n", p=P)

    def add(kind, src, act, needs, groups, **more):
        free = [(g, taken[g]) for g in groups if more.get("first", True)]
        units.append(dict(kind=kind, src=src, act=act, needs=needs, free=free, **more))
        if more.get("last", True):
            for g in groups:
                taken[g] += 1
        return len(units) - 1

    def unit_c(w, c0, act, needs):
        bank = 4 + sum(u["kind"] == "C" for u in units) % 2
        return add("C", rows_by_tile(w, 0, D, c0, 256), act, needs, [f"c{bank}"], bank=bank)

    def unit_b(w, c0, act, k0, needs):
        return add("B", rows_by_tile(w, 0, 512, c0, 512), act, needs, ["c4", "c5"], bank=4, k0=k0)

    def units_t(w, c0, act, g, needs):
        return [add("T", rows_by_tile(w, 512 * h, 512, c0, 512), act, needs, [f"g{g}"], bank=2 * g,
                    k0=4 * h, first=h == 0, last=h == 1) for h in range(2)]

    def unit_d(w, r0, act, k0, first, last, needs, c0=0):
        return add("D", rows_by_tile(w, r0, 256, c0, D), act, needs, ["g0", "g1"], k0=k0, first=first,
                   last=last)

    def after(g):
        return (g, taken[g])

    order = []

    def step(*s):
        order.append(s)

    def product(u, *then):
        order.append(("mm", u, 0))
        flush()
        order.append(("mm", u, 1))
        held.extend(then)

    held = []

    def flush():
        order.extend(held)
        held.clear()

    def weave(fill, mixed):
        halves_ = [(u, part, then) for u, *then in fill for part in range(2)]
        scale, credit, done = len(halves_) / sum(n for n, _ in mixed), 0.0, 0

        def put(u, part, then):
            order.append(("mm", u, part))
            if part == 0:
                flush()
            else:
                held.extend(then)

        for n, s in mixed:
            credit += n * scale
            while credit > 0.999 and done < len(halves_):
                put(*halves_[done])
                done += 1
                credit -= 1
            order.append(s)
        for h in halves_[done:]:
            put(*h)
        flush()

    def attention(which):
        for g in range(8):
            if g < 6:
                yield (1, ("att_scores", which, g))
            if 1 <= g < 7:
                yield (1, ("att_norm", which, g - 1))
                yield (0, ("att_turn", which, g - 1)) if g < 6 else (1, ("att_turn", which, g - 1))
            if g >= 2:
                yield (0 if g < 7 else 1, ("att_values", which, g - 2))

    def out_product(w, act, needs):
        us = [unit_d(w, 256 * i, act, 2 * i, i == 0, i == 3, needs) for i in range(4)]
        for u in us:
            product(u)
        return us[-1]

    step("norm", 0, [("x_in0", 16), ("x_in1", 16)])
    h_ready = [("norm_lo", KD)]
    for j in range(3):
        us = units_t(w_in, o_fox + 512 * j, "h", j % 2, h_ready)
        product(us[0])
        product(us[1], ("fox_qkv", j, us[-1], after(f"g{j % 2}")))
        if j == 1:
            step("params")
    fill = []
    convs = {}
    for e in range(3 * DW // 256):
        u = unit_c(w_in, o_dn + 256 * e, "h", h_ready)
        convs["dn", e] = len(convs)
        fill.append((u, ("dn", e, convs["dn", e], u)))
    for e in range(BT // 2):
        for part in (1, 2, 0):
            u = unit_c(w_in, o_sc + part * SW + 256 * e, "h", h_ready)
            if part == 1:
                convs["sc", e] = len(convs)
            fill.append((u, ("sc", e, part, convs["sc", e], u)))
    mixed = [(0, ("small",)), (1, ("fox_norm",)), (3, ("fox_turn", 0)), (0, ("fox_turn", 1)), (1, ("fox_cum", 0)),
             (0, ("fox_cum", 1))]
    mixed += list(attention(0)) + [(0, ("dn_silu",)), (1, ("fox_out",))]
    weave(fill, mixed)
    fill = []
    for e in range(DW // 256):
        u = unit_c(w_in, o_z + 256 * e, "h", h_ready)
        fill.append((u, ("z", e, u)))
    for e in range(NB * D // 256):
        u = unit_c(w_in, o_gate + 256 * e, "h", h_ready)
        fill.append((u, ("gate", e, u)))

    def branch(n, need):
        for g in range(2):
            u = unit_b(a["w_branch"][0][n], 512 * g, "a", BT * n, [(need, 2)])
            yield (u, ("merge", n, g, 0, u), ("merge", n, g, 1, u))

    fill += list(branch(0, "fox_lo")) + list(branch(1, "sc_lo"))
    mixed = [(0, ("dn_square",)), (0, ("dn_cum",)), (2, ("dn_unit",)), (1, ("dn_scale",))]
    for t in range(TT):
        mixed += [(4 if t == 0 else 1, ("dn_tok", t)), (1, ("dn_decay", t)), (1, ("dn_kk", t)), (2, ("dn_x0", t))]
        for l in range(1, 6):
            mixed += [(1, ("dn_y", t, l)), (0.5, ("dn_z", t, l))]
        mixed += [(1, ("dn_sol", t))]
    for c in range(NCH):
        mixed += [(1, ("dn_new", c)), (1, ("dn_state", c))]
        if c % 2:
            mixed += [(0, ("dn_sum", c // 2))]
    mixed += [(0, ("dn_out", 0)), (3, ("dn_out", 1))]
    weave(fill, mixed)
    for f in branch(2, "dn_lo"):
        product(*f)
    flush()
    u = out_product(a["w_o"][0], "h", [("merged_lo", 4)])
    step("resid", u)

    step("norm", 1, [after("g0"), after("g1")])
    downs = {}
    NF = UPT // 2
    for c in range(NF + 1):
        if c < NF:
            for part in range(2):
                u = unit_c(a["w_up"][0], DFF * part + 256 * c, "h", [("norm_lo", 2 * KD)])
                product(u, ("up", c, part, u))
            if c in (1, 3):
                step("ple_load" if c == 1 else "ple_p")
        if c >= 1:
            downs[c - 1] = unit_d(a["w_down"][0], 256 * (c - 1), "a", 2 * ((c - 1) % 2), c == 1, c == NF,
                                  [("glu_lo", c)])
            product(downs[c - 1])
        if c < NF:
            held.append(("glu", c, downs.get(c - 2)))
            if c == 0:
                flush()
    flush()
    step("resid", len(units) - 1)

    step("norm", 2, [after("g0"), after("g1")])
    u = out_product(a["w_ple_gate"][0], "h", [("norm_lo", 3 * KD)])
    step("ple_gate", u)
    product(unit_d(a["w_ple"][0], 0, "a", 4, True, True, [("ple_lo", 1)]))
    step("ple_x", len(units) - 1)

    step("norm", 3, [("ple_added", t + 1) for t in range(TT)])
    h_ready = [("norm_lo", 4 * KD)]
    w_ab = a["ab_w_in_2"][0]
    for e in range(4):
        u = unit_c(w_ab, 256 * e, "h", h_ready)
        product(u, ("ab_qk", e, u))
    step("lam")
    us = units_t(w_ab, 1024, "h", 0, h_ready)
    fill = [(us[0],), (us[1], ("ab_v", us[1]))]
    for e in range(2):
        u = unit_c(w_ab, 1536 + 256 * e, "h", h_ready)
        fill.append((u, ("pool_u", e, u)))
    mixed = list(attention(1))
    flush()
    weave(fill, mixed[:15])
    step("pool_win")
    order.extend(s for _, s in mixed[15:])
    for b in range(TT):
        step("ab_sum", b)
    step("pool_mm")
    for b in range(TT):
        step("ab_turn", b)
    u = out_product(a["ab_w_out_2"][0], "a", [("ab_lo", 2), ("pool_lo", 1)])
    step("resid", u)

    def squared_relu_part(i, norm):
        step("norm", norm, [after("g0"), after("g1")])
        n, rows_of = DFF2 // 256, {}
        for c in range(n + 1):
            if c < n:
                u = unit_c(a["ffn_w1_2"][i], 256 * c, "h", [("norm_lo", (norm + 1) * KD)])
                product(u, ("relu2", i * n + c, u))
            if c >= 1:
                rows_of[c - 1] = unit_d(a["ffn_w2_2"][i], 256 * (c - 1), "a", 2 * ((c - 1) % 2), c == 1,
                                        c == n, [("relu2_lo", i * n + c)])
                product(rows_of[c - 1])
            if c < n:
                held.append(("relu2_split", i * n + c, c, rows_of.get(c - 2)))
                if c == 0:
                    flush()
        flush()
        step("resid", len(units) - 1)

    squared_relu_part(0, 4)

    step("norm", 5, [after("g0"), after("g1")])
    h_ready = [("norm_lo", 6 * KD)]
    w_gla = a["gla_w_in_2"][0]
    fill = []
    for e in range(2 * GK // 256):
        u = unit_c(w_gla, 256 * e, "h", h_ready)
        fill.append((u, ("gla_qk", e, u)))
    weave(fill, [(1, ("gla_low",)), (3, ("gla_gate",)), (4, ("gla_cum",))])
    fill = []
    for i in range(4):
        u = unit_d(w_gla, 256 * i, "h", 2 * i, i == 0, i == 3, h_ready, c0=2 * GK)
        fill.append((u, ("gla_v", u)) if i == 3 else (u,))
    for e in range(2):
        u = unit_c(w_gla, 2 * GK + D + 256 * e, "h", h_ready)
        fill.append((u, ("gla_g", e, u)))
    mixed = [(1, ("gla_pairs", 0))]
    for l in range(6):
        mixed += [(1, ("gla_level", l)), (2, ("gla_pairs", l + 1))]
    mixed += [(1, ("gla_decay",)), (1, ("gla_ktok",))]
    weave(fill, mixed)
    fill = []
    for e in range(2, D // 256):
        u = unit_c(w_gla, 2 * GK + D + 256 * e, "h", h_ready)
        fill.append((u, ("gla_g", e, u)))
    weave(fill, [(0, ("gla_chunk", 0)), (1, ("gla_chunk", 1)), (0, ("gla_sum", 0)), (1, ("gla_chunk", 2)),
                 (1, ("gla_chunk", 3)), (0, ("gla_sum", 1))])
    for t in range(TT):
        step("gla_turn", t)
    u = out_product(a["gla_w_out_2"][0], "a", [("gla_lo", 4)])
    step("resid", u)
    squared_relu_part(1, 6)
    step("final", [after("g0"), after("g1")])
    fresh = {}
    for s, nxt in ((i, order[i:]) for i, s in enumerate(order) if s[0] == "norm"):
        fresh[next(n[1] for n in nxt if n[0] == "mm")] = order[s][1]
    NU = len(units)

    ctx = ExitStack()
    with ctx:
        def sb(name, shape, dt=F32):
            return ctx.enter_context(nc.sbuf_tensor(name, shape, dt))

        sems = {}

        def sem(name):
            if name not in sems:
                sems[name] = ctx.enter_context(nc.semaphore(name))
            return sems[name]

        raw = sb("raw", [P, RAW, UNIT])
        whi = sb("whi", [P, SPLIT, UNIT], F32R)
        wlo = sb("wlo", [P, SPLIT, UNIT], F32R)
        hhi = sb("hhi", [P, KD, T], F32R)
        hlo = sb("hlo", [P, KD, T], F32R)
        ahi = sb("ahi", [P, 3 * BT, T], F32R)
        alo = sb("alo", [P, 3 * BT, T], F32R)
        xs = sb("xs", [P, TT, D])
        x = sb("xres", [P, TT, D])
        ps = ctx.enter_context(nc.psum_tensor("ps", [P, 8, 512], F32))

        ident = sb("ident", [P, P])
        ones = sb("ones", [P, P])
        tri = sb("tri", [P, P])
        tri64 = sb("tri64", [P, P])
        blk64 = sb("blk64", [P, P])
        lev = sb("lev", [P, 6, P])
        cneg = sb("cneg", [P, P])
        dneg = sb("dneg", [P, P])
        inv = sb("inv", [P, 4, 16])
        colp = sb("colp", [P, 3, P])
        bias16 = sb("bias16", [P, NSM])
        alog = sb("alog", [P, DH])
        wsm = sb("wsm", [P, KD, NSM])
        wlow = sb("wlow", [P, KD, GR])
        ss = sb("ss", [P, TT, 16])
        zz = sb("zz", [P, 4, TT, NSM])
        eps = sb("eps", [P, 1])
        warm = sb("warm", [P, 1])
        gcol0 = sb("gcol0", [P, KD])
        beta = sb("beta", [P, TT, DH])
        gg = sb("gg", [P, TT, DH])
        gx = sb("gx", [P, TT, 2, DH])
        gcol = sb("gcol", [P, TT, DH])
        gt = sb("gt", [P, TT, DH, 2])
        nmax = sb("nmax", [P, 2, 4])
        rsum = sb("rsum", [P, 2, 4])
        lamw = sb("lamw", [P, 8])
        conv = sb("conv", [P, 2, 2, PAD + T])
        cy = sb("cy", [P, 2, 2, T])
        diag = cy[:, 0, 0, :].rearrange("p (t n) -> p t n", t=TT)
        ARENA = nc.sbuf_bytes_remaining // 4 - 16
        arena = sb("arena", [P, ARENA])

        def view(base, n):
            assert base + n <= ARENA, (base, n, ARENA)
            return arena[:, base:base + n]

        def tiles(ap):
            return ap.rearrange("p (c t) -> p c t", t=T)

        def by(ap, n):
            return ap.rearrange("p (h i) -> p h i", h=n)

        rows = view(0, 3 * P).rearrange("p (b n) -> p b n", b=3)
        grow = view(3 * P, P)[0:KD, :]
        dnT = tiles(view(0, 3072))
        kcT = dnT[:, 2 * DH:3 * DH, :]
        gates = tiles(view(3072, 6144))
        fqkv = view(3072, 3072).rearrange("p (t n) -> p t n", t=TT)
        fT = tiles(view(6144, 2048))
        S2 = view(8192, 1024).rearrange("p (b n) -> p b n", b=2)
        PT2 = view(9216, 1024).rearrange("p (b n) -> p b n", b=2)
        fcum = view(10240, 2048).rearrange("p (t h j) -> p t h j", t=TT, h=FH)
        fbias = xs[:, :, :].rearrange("p t n -> p (t n)").rearrange("p (h j) -> p h j", h=FH)
        dsq = view(10240, 2048)
        kdec, rhsk, vb, qkT = [view(9216 + 1024 * i, 1024).rearrange("p (t h d) -> p t h d", t=TT, h=DH)
                               for i in range(4)]
        X, XT, LT, DT = [by(view(13312 + 512 * i, 512), DH) for i in range(4)]
        Bl, Y = [by(cy[:, i, :, :].rearrange("p a t -> p (a t)"), DH) for i in range(2)]
        zT = xs[:, 0, :].rearrange("p (c t) -> p c t", t=T)
        S = by(xs[:, 1, 0:512], DH)
        EG = by(xs[:, 1, 512:1024], DH)
        mg = gates[:, 0:KD, :]
        sg = view(0, 2048).rearrange("p (t n) -> p t n", t=TT)
        ptok = view(2048, 512).rearrange("p (t n) -> p t n", t=TT)
        qkf = tiles(view(0, 2048))
        vtok = view(2048, 1024).rearrange("p (t n) -> p t n", t=TT)
        S2b = view(3072, 1024).rearrange("p (b n) -> p b n", b=2)
        PT2b = view(4096, 1024).rearrange("p (b n) -> p b n", b=2)
        ob = view(5120, 1024).rearrange("p (t h d) -> p t h d", t=TT, h=4)
        oy = by(view(6144, 512), 4)
        W0 = 16
        pu, p1, p2, p3, p4 = [view(6656 + 1088 * i, 4 * (W0 + T)).rearrange("p (g t) -> p g t", g=4)
                              for i in range(5)]
        pr = tiles(view(12096, 1024))
        pw = by(view(13120, 512), 4)
        pfix = view(13632, 64).rearrange("p (g t) -> p g t", g=4)
        lamr = by(view(13696, 4 * FD), 4)
        gqT = tiles(view(0, 2048))
        gla = view(2048, 1024).rearrange("p (t n) -> p t n", t=TT)
        gmin = view(3072, 1024).rearrange("p (t n) -> p t n", t=TT)
        bcum = tiles(view(4096, 1024))
        E1 = tiles(view(2048, 1024))
        Cl = tiles(view(3072, 1024))
        attn = view(5120, 1024).rearrange("p (g i) -> p g i", g=TT * GH)
        atmp = view(6144, 1024).rearrange("p (g i) -> p g i", g=TT * GH)
        kdt = view(7168, 1024).rearrange("p (g i) -> p g i", g=TT * GH)
        EB = tiles(view(8192, 1024))
        vg = view(9216, 2048).rearrange("p (t n) -> p t n", t=TT)
        sgT = tiles(view(11264, 2048))
        GS = view(13312, 1024).rearrange("p (h d) -> p h d", h=GH)
        gkT = view(14336, 256)
        wgu = view(14592, GK)[0:GR, :]
        bgk = view(9216, GK)[0:1, :]
        og = [by(view(at, 1024), GH) for at in (2048, 4096)]
        gy = view(6144, 1024).rearrange("p (c t) -> p c t", c=KD)
        nfin = view(0, D)

        def as_rows(ap, s):
            return ap.rearrange(s, p=P)

        sources, place = [], {}

        def param(name, src, block, n):
            at = sum(k for b, _, k in sources if b == block)
            place[name] = (block, at)
            sources.append((block, src, n))

        param("g_ffn", as_rows(a["g_ffn"][0], "(k p) -> k p"), 0, KD)
        param("g_ple", as_rows(a["g_ple"][0], "(k p) -> k p"), 0, KD)
        param("norm_mix", as_rows(a["norm_mix_2"], "i (k p) -> (i k) p"), 0, 2 * KD)
        param("norm_ffn", as_rows(a["norm_ffn_2"], "i (k p) -> (i k) p"), 0, 2 * KD)
        param("gla_norm", as_rows(a["gla_norm_2"][0], "h (k p) -> (h k) p"), 0, KD)
        param("fox_gain", [a["fox_q_gain"], a["fox_k_gain"]], 0, 2)
        param("dn_gain", a["dn_norm_gain"], 0, 1)
        param("subln", a["ab_subln_2"], 0, 1)
        param("pool_scale", as_rows(a["pool_scale_2"][0], "(k p) -> k p"), 0, 4)
        param("sc_conv", as_rows(a["sc_conv_w"][0], "j (k p) -> (j k) p"), 0, 3 * BT)
        param("dn_conv", as_rows(a["dn_conv_w"][0], "j (k p) -> (j k) p"), 1, 4 * 3 * BT)
        for j in range(3):
            param(f"ffn_conv{j}", as_rows(a["ffn_conv_w"][0][j:j + 1], "j (k p) -> (j k) p"), (1, 2, 2)[j], 2 * UPT)

        def col(name, i):
            block, at = place[name]
            return colp[:, block, at + i:at + i + 1]

        def gain(i, k):
            return gcol0[:, k:k + 1] if i == 0 else col(gains[i][0], gains[i][1] + k)

        def cols(name, n, width):
            block, at = place[name]
            return colp[:, block, at:at + n].unsqueeze(2).to_broadcast([P, n, width])

        gains = [None, ("g_ffn", 0), ("g_ple", 0), ("norm_mix", 0), ("norm_ffn", 0),
                 ("norm_mix", KD), ("norm_ffn", KD)]
        n_par = len(sources) + 3 + 6
        groups = [(1, (2 * g, 2 * g + 1)) for g in range(4)] + [(0, tuple(range(4 * g, 4 * g + 4))) for g in range(2)]

        def turned(which, g):
            b, maps = groups[g]
            w = P * (b + 1)
            if which == 0:
                return [(i * w + kt * P, f, kt) for i, f in enumerate(maps) for kt in range(b + 1)]
            return [(i * w + kt * P, f // 2, kt) for i, f in enumerate(maps) if f % 2 == 0 for kt in range(b + 1)]

        att = [dict(q=fT[:, 0:4, :], k=fT[:, 4:8, :], S=S2, PT=PT2), dict(q=qkf[:, 0:4, :], k=qkf[:, 4:8, :], S=S2b, PT=PT2b)]

        def took(u):
            g, n = units[u]["free"][0]
            return sem(g), n + 1

        for name in ("params_in", "constants", "unit_done", "hi_done", "lo_done"):
            sem(name)
        block = ctx.enter_context(nc.Block())

        @block.sync
        def _(sp):
            for t in range(TT):
                sp.dma_start(x[:, t, :], a["x"][0][t * P:(t + 1) * P, :]).then_inc(sem(f"x_in{t}"), 16)
            for u in range(NU):
                if u >= RAW:
                    sp.wait_ge(sem("lo_done"), u - RAW + 1)
                src = units[u]["src"]
                dst = raw[:, u % RAW, :].rearrange("p (k n) -> p k n", k=src.shape[1])
                sp.dma_start(dst, src).then_inc(sem(f"raw_in{u % RAW}"), 16)
            sp.wait_ge(sem("final_x"), TT)
            sp.dma_start(a["out"][0].rearrange("(t p) d -> p t d", p=P), xs[:, :, :]).then_inc(sem("stored"), 16)
            sp.wait_ge(sem("stored"), 16)

        made = {}

        @block.gpsimd
        def _(pool):
            n = [0]

            def then(ins):
                n[0] += 1
                ins.then_inc(sem("constants"), 1)
                pool.wait_ge(sem("constants"), n[0])

            then(pool.memset(ident[:, :], 0.0))
            then(pool.affine_select(out=ident[:, :], in_=ident[:, :], compare_op=ALU.not_equal, fill=1.0,
                                    base=0, pattern=[[-1, P]], channel_multiplier=1))
            then(pool.memset(warm[:, :], 0.0))
            then(pool.memset(eps[:, :], EPS))
            made["ident"] = n[0]
            then(pool.memset(rows[:, :, :], 0.0))
            made["rows"] = n[0]
            for t_, v in ((ones, 1.0), (tri, 1.0), (blk64, 0.0), (cneg, 0.0), (dneg, 0.0)):
                then(pool.memset(t_[:, :], v))
            then(pool.memset(lev[:, :, :], 0.0))
            then(pool.memset(conv[:, :, :, :], 0.0))
            then(pool.affine_select(out=tri[:, :], in_=tri[:, :], compare_op=ALU.is_ge, fill=0.0,
                                    base=0, pattern=[[1, P]], channel_multiplier=-1))
            then(pool.affine_select(out=cneg[:, :], in_=cneg[:, :], compare_op=ALU.is_ge, fill=-BIG,
                                    base=0, pattern=[[-1, P]], channel_multiplier=1))
            then(pool.memset(dneg[0:CH, CH:P], -BIG))
            then(pool.memset(blk64[0:CH, 0:CH], 1.0))
            then(pool.memset(blk64[CH:P, CH:P], 1.0))
            then(pool.tensor_copy(tri64[:, :], tri[:, :]))
            then(pool.memset(tri64[0:CH, CH:P], 0.0))
            for l in range(6):
                s = 1 << l
                right = lev[:, l, :].rearrange("p (n two s) -> p n two s", two=2, s=s)[:, :, 1, :]
                then(pool.memset(right, 1.0))
                nb = P // (2 * s)
                then(pool.affine_select(out=right, in_=right, compare_op=ALU.is_ge, fill=0.0, base=0,
                                        pattern=[[-2 * s, nb], [0, s]], channel_multiplier=1))
                then(pool.affine_select(out=right, in_=right, compare_op=ALU.is_ge, fill=0.0, base=s - 1,
                                        pattern=[[2 * s, nb], [0, s]], channel_multiplier=-1))
            for g, w in enumerate(POOLS):
                then(pool.memset(inv[:, g, :], 1.0 / w))
                for i in range(w - 1):
                    then(pool.memset(inv[:, g, i:i + 1], 1.0 / (i + 1)))
            made["all"] = n[0]

        @block.scalar
        def _(act):
            n = [0]

            def link(ins):
                n[0] += 1
                ins.then_inc(sem("act_own"), 1)
                act.wait_ge(sem("act_own"), n[0])

            roots = [0]

            def root(ap, scale):
                roots[0] += 1
                act.wait_ge(sem("root_in"), roots[0])
                act.activation(ap, ap, ACT.Sqrt, scale=scale, bias=eps[:, :]).then_inc(sem("root_out"), 1)

            def square_sums(parts_):
                for junk, src, total in parts_:
                    ins = act.activation(junk, src, ACT.Square, accum_out=total)
                link(ins)

            def split_high(u):
                act.wait_ge(sem(f"raw_in{u % RAW}"), 16 * (u // RAW + 1))
                if u >= SPLIT:
                    act.wait_ge(sem("unit_done"), u - SPLIT + 1)
                act.activation(whi[:, u % SPLIT, :], raw[:, u % RAW, :], ACT.Copy).then_inc(sem("hi_done"), 1)

            def load_params():
                act.wait_ge(sem("constants"), made["rows"])
                at = {}
                for b, src, k in sources:
                    r = at.get(b, 0)
                    if isinstance(src, list):
                        for i, j in ((0, 0), (0, 1), (1, 0), (1, 1)):
                            act.dma_start(rows[r + i:r + i + 1, b, FD * j:FD * (j + 1)], src[i])\
                               .then_inc(sem("params_in"), 16)
                    else:
                        act.dma_start(rows[r:r + k, b, :], src).then_inc(sem("params_in"), 16)
                    at[b] = r + k
                act.dma_start(bias16[:, 0:FH], a["b_fox_f"][0].partition_broadcast(P)).then_inc(sem("params_in"), 16)
                act.dma_start(bias16[:, FH + DH:NSM], a["dn_dt_bias"][0].partition_broadcast(P))\
                   .then_inc(sem("params_in"), 16)
                act.dma_start(alog[:, :], a["dn_a_log"][0].partition_broadcast(P)).then_inc(sem("params_in"), 16)
                act.dma_start(wlow[:, :, :], rows_by_tile(a["gla_w_in_2"][0], 0, D, 2 * GK + 2 * D, GR))\
                   .then_inc(sem("params_in"), 16)
                act.dma_start(wsm[:, :, 0:FH], rows_by_tile(w_in, 0, D, o_f, FH)).then_inc(sem("params_in"), 16)
                act.dma_start(wsm[:, :, FH:NSM], rows_by_tile(w_in, 0, D, o_b, 2 * DH)).then_inc(sem("params_in"), 16)

            def norm(i, waits):
                link(act.activation(warm[:, :], warm[:, :], ACT.Sqrt))
                for t in range(TT):
                    act.wait_ge(sem(waits[t][0]), waits[t][1])
                    square_sums([(xs[:, t, :], x[:, t, :], ss[:, t, 0:1])])
                    act.activation(ss[:, t, 0:1], ss[:, t, 0:1], ACT.Sqrt, scale=1.0 / D, bias=eps[:, :])\
                       .then_inc(sem("root_out"), 1)
                if i == 0:
                    split_high(0)
                for k in range(KD):
                    act.wait_ge(sem("norm_turned"), KD // 2 * i + k // 2 + 1)
                    if i == 0 and k == 0:
                        act.wait_ge(sem("gcol0_done"), 1)
                    act.activation(hhi[:, k, :], ps[:, k // 2, (k % 2) * T:(k % 2 + 1) * T], ACT.Copy,
                                   scale=gain(i, k)).then_inc(sem("norm_hi"), 1)
                if i == 0:
                    split_high(1)
                    load_params()
                    act.wait_ge(sem("constants"), made["all"])
                if i == 4:
                    act.dma_start(bgk, a["gla_b_gk_2"]).then_inc(sem("gla_par"), 16)
                    act.dma_start(wgu, a["gla_w_gk_up_2"][0]).then_inc(sem("gla_par"), 16)

            def params():
                act.wait_ge(sem("colp_done"), 3)

            def small():
                act.wait_ge(sem("small_abs"), 1)
                act.activation(zz[:, 1], zz[:, 1], ACT.Exp, scale=-1.0).then_inc(sem("small_exp"), 1)
                act.activation(alog[:, :], alog[:, :], ACT.Exp).then_inc(sem("small_exp"), 1)
                act.wait_ge(sem("small_exp"), 2)
                act.activation(zz[:, 2], zz[:, 1], ACT.Ln, bias=1.0).then_inc(sem("small_exp"), 1)
                act.wait_ge(sem("small_lsg"), 1)
                act.activation(beta[:, :, :], zz[:, 3, :, FH:FH + DH], ACT.Exp).then_inc(sem("small_exp"), 1)

            def fox_qkv(j, u, freed):
                act.wait_ge(sem("unit_done"), u + 1)
                g = j % 2
                for t in range(TT):
                    ins = act.activation(fqkv[:, t, 512 * j:512 * (j + 1)], ps[:, 2 * g + t, :], ACT.Copy)
                ins.then_inc(sem(f"g{g}"), 1)

            def sc(e, part, j, u):
                act.wait_ge(sem("unit_done"), u + 1)
                out = cy[:, e % 2, :, :]
                if part == 1:
                    act.activation(out, tiles(ps[:, units[u]["bank"], :]), ACT.Copy).then_inc(took(u)[0], 1)
                if part == 0:
                    act.wait_ge(*took(u))
                    act.activation(ahi[:, BT + 2 * e:BT + 2 * e + 2, :], out, ACT.Copy).then_inc(sem("sc_hi"), 1)

            def conv_copy(j, u):
                act.wait_ge(sem("unit_done"), u + 1)
                if j >= 2:
                    act.wait_ge(sem("conv_read"), j - 1)
                act.activation(conv[:, j % 2, :, PAD:PAD + T], tiles(ps[:, units[u]["bank"], :]), ACT.Copy)\
                   .then_inc(took(u)[0], 1)

            def dn(e, j, u):
                conv_copy(j, u)

            def fox_turn(t):
                for b in range(2):
                    act.wait_ge(sem("fox_turned"), 2 * t + b + 1)
                    act.activation(fT[:, 4 * b:4 * b + 4, t * P:(t + 1) * P], by(ps[:, 2 * t + b, :], 4), ACT.Copy,
                                   scale=col("fox_gain", b)).then_inc(sem("fox_T"), 1)

            def fox_cum(t):
                for b in range(2):
                    act.wait_ge(sem("fox_cummed"), 2 * t + b + 1)
                    act.activation(fbias[:, 4 * b:4 * b + 4, t * P:(t + 1) * P], by(ps[:, 2 * t + b, :], 4), ACT.Copy,
                                   scale=-1.0).then_inc(sem("fox_bias"), 1)

            def att_scores(w, g):
                b, maps = groups[g]
                act.wait_ge(sem(f"att{w}_max"), g + 1)
                width = P * (b + 1)
                for i in range(len(maps)):
                    part = att[w]["S"][:, g % 2, i * width:(i + 1) * width]
                    ins = act.activation(part, part, ACT.Exp, bias=nmax[:, g % 2, i:i + 1],
                                         accum_out=rsum[:, g % 2, i:i + 1])
                    ins.then_inc(sem(f"att{w}_exp"), 1)

            def att_turn(w, g):
                act.wait_ge(sem(f"att{w}_turned"), g + 1)
                if g >= 2:
                    act.wait_ge(sem(f"att{w}_used"), g - 1)
                k = len(turned(w, g)) * P
                act.activation(att[w]["PT"][:, g % 2, 0:k], ps[:, 6 + g % 2, 0:k], ACT.Copy)\
                   .then_inc(sem(f"att{w}_PT"), 1)

            def fox_out():
                act.wait_ge(sem("att0_used"), 6)
                for b in range(2):
                    act.activation(ahi[:, 2 * b:2 * b + 2, :], tiles(ps[:, b, :]), ACT.Copy)\
                       .then_inc(sem("fox_hi"), 1)

            def z(e, u):
                act.wait_ge(sem("unit_done"), u + 1)
                act.activation(zT[:, 2 * e:2 * e + 2, :], tiles(ps[:, units[u]["bank"], :]), ACT.Silu)\
                   .then_inc(took(u)[0], 1)

            def gate(e, u):
                act.wait_ge(sem("unit_done"), u + 1)
                act.activation(gates[:, 2 * e:2 * e + 2, :], tiles(ps[:, units[u]["bank"], :]), ACT.Sigmoid)\
                   .then_inc(took(u)[0], 1)

            def dn_cum():
                act.wait_ge(sem("dn_gx"), 1)
                act.activation(gx[:, :, :, :], gx[:, :, :, :], ACT.Exp).then_inc(sem("dn_egx"), 1)

            def dn_decay(t):
                act.wait_ge(sem("dn_grow"), t + 1)
                if t >= 1:
                    act.wait_ge(sem("dn_lt"), t)
                act.activation(EG, by(ps[:, 6, :], DH), ACT.Exp).then_inc(sem("dn_eg"), 1)
                act.wait_ge(sem("dn_dt"), t + 1)
                act.activation(DT, DT, ACT.Exp).then_inc(sem("dn_edt"), 1)

            def dn_x0(t):
                act.wait_ge(sem("dn_x0_turned"), t + 1)
                act.activation(X, by(ps[:, 6, :], DH), ACT.Copy).then_inc(sem("dn_X"), 1)

            def dn_y(t, l):
                act.wait_ge(sem("dn_BX"), 5 * t + l)
                act.activation(Y, by(ps[:, 7, :], DH), ACT.Copy).then_inc(sem("dn_Y"), 1)

            def dn_sol(t):
                act.wait_ge(sem("dn_solved"), 2 * t + 2)
                act.activation(kcT[:, :, t * P:(t + 1) * P], by(ps[:, 7, :], DH), ACT.Copy)\
                   .then_inc(sem("dn_kcT"), 1)

            def head_sums(t, src, width, junk):
                n_h = src.shape[1]
                square_sums([(junk[:, h, :], src[:, h, :], ss[:, t, h:h + 1]) for h in range(n_h)])
                r_ = ss[:, t, 0:n_h]
                act.activation(r_, r_, ACT.Sqrt, scale=1.0 / width, bias=eps[:, :]).then_inc(sem("root_out"), 1)

            def dn_sum(t):
                act.wait_ge(sem("dn_o"), 2 * t + 2)
                head_sums(t, by(ps[:, 2 + t, :], DH), DV, Y)

            def dn_out(t):
                act.wait_ge(sem("dn_y2"), t + 1)
                act.activation(ahi[:, 2 * BT:3 * BT, t * P:(t + 1) * P], XT, ACT.Copy).then_inc(sem("dn_hi"), 1)

            def merge(n_, g, b, u):
                if n_ == NB - 1:
                    s = slice(4 * g + 2 * b, 4 * g + 2 * b + 2)
                    act.wait_ge(sem("merged"), 2 * g + b + 1)
                    act.activation(hhi[:, s, :], mg[:, s, :], ACT.Copy).then_inc(sem("merged_hi"), 1)

            def up(c, part, u):
                conv_copy(len(convs) + 2 * c + part, u)

            def glu(c, down):
                act.wait_ge(sem("conv_read"), len(convs) + 2 * c + 1)
                act.activation(cy[:, 0, :, :], cy[:, 0, :, :], ACT.Silu).then_inc(sem("glu_silu"), 1)
                act.wait_ge(sem("glu_prod"), c + 1)
                if down is not None:
                    act.wait_ge(sem("unit_done"), down + 1)
                s = 2 * (c % 2)
                act.activation(ahi[:, s:s + 2, :], cy[:, 1, :, :], ACT.Copy).then_inc(sem("glu_hi"), 1)

            def ple_gate(u):
                for t in range(TT):
                    act.wait_ge(sem("half_done") if t == 0 else sem("unit_done"), u + 1)
                    act.activation(sg[:, t, :].rearrange("p (b n) -> p b n", b=2), ps[:, 2 * t:2 * t + 2, :],
                                   ACT.Sigmoid).then_inc(sem(f"g{t}"), 1)

            def ple_load():
                act.dma_start(ptok, a["p"][0][0].rearrange("(t p) d -> p t d", p=P)).then_inc(sem("p_in"), 16)

            def ple_p():
                act.wait_ge(sem("p_turned"), 1)
                act.activation(ahi[:, 4:6, :], tiles(ps[:, 6, :]), ACT.Copy).then_inc(sem("ple_hi"), 1)

            def ab_qk(e, u):
                act.wait_ge(sem("unit_done"), u + 1)
                act.wait_ge(sem("ple_added"), TT)
                act.activation(qkf[:, 2 * e:2 * e + 2, :], tiles(ps[:, units[u]["bank"], :]), ACT.Copy,
                               scale=FD ** -0.5 if e < 2 else 1.0).then_inc(took(u)[0], 1)
                if e == 0:
                    act.dma_start(pw, a["pool_w_2"][0].rearrange("g c d -> c g d")).then_inc(sem("pw_in"), 16)
                    act.dma_start(lamr, a["ab_lambda_2"][0].partition_broadcast(P)).then_inc(sem("pw_in"), 16)

            def ab_v(u):
                act.wait_ge(sem("unit_done"), u + 1)
                for t in range(TT):
                    ins = act.activation(vtok[:, t, :], ps[:, t, :], ACT.Copy)
                ins.then_inc(sem("g0"), 1)

            def pool_u(e, u):
                act.wait_ge(sem("unit_done"), u + 1)
                act.wait_ge(sem("pool_zero"), 1)
                act.activation(pu[:, 2 * e:2 * e + 2, W0:W0 + T], tiles(ps[:, units[u]["bank"], :]), ACT.Copy)\
                   .then_inc(took(u)[0], 1)

            def lam():
                act.wait_ge(sem("lam_sum"), 1)
                act.activation(lamw[:, 0:2], lamw[:, 0:2], ACT.Exp).then_inc(sem("lam_exp"), 1)

            def pool_mm():
                act.wait_ge(sem("pool_y"), 1)
                act.activation(ahi[:, 4:8, :], pr, ACT.Copy).then_inc(sem("pool_hi"), 1)

            def ab_sum(b):
                act.wait_ge(sem("att1_used"), 6)
                head_sums(b, by(ps[:, b, :], 4), P, oy)

            def ab_turn(b):
                act.wait_ge(sem("ab_oturned"), b + 1)
                act.activation(ahi[:, 0:4, b * P:(b + 1) * P], by(ps[:, 6 + b, :], 4), ACT.Copy,
                               scale=col("subln", 0)).then_inc(sem("ab_hi"), 1)

            def relu2(i, u):
                act.wait_ge(sem("unit_done"), u + 1)
                if i >= 2:
                    act.wait_ge(sem("relu2_lo"), i - 1)
                act.activation(cy[:, i % 2, :, :], tiles(ps[:, units[u]["bank"], :]), ACT.Relu)\
                   .then_inc(took(u)[0], 1)

            def relu2_split(i, c, down):
                act.wait_ge(sem("relu2_sq"), i + 1)
                if down is not None:
                    act.wait_ge(sem("unit_done"), down + 1)
                s = 2 * (c % 2)
                act.activation(ahi[:, s:s + 2, :], cy[:, i % 2, :, :], ACT.Copy).then_inc(sem("relu2_hi"), 1)

            def gla_low():
                act.wait_ge(sem("gla_lowed"), 1)
                act.activation(gkT[0:GR, :], ps[0:GR, 6, 0:T], ACT.Copy).then_inc(sem("gla_gkT"), 1)

            def gla_gate():
                act.wait_ge(sem("gla_abs"), 1)
                act.activation(gla[:, :, :], gla[:, :, :], ACT.Exp, scale=-1.0).then_inc(sem("gla_ln"), 1)
                act.wait_ge(sem("gla_ln"), 1)
                act.activation(gla[:, :, :], gla[:, :, :], ACT.Ln, bias=1.0).then_inc(sem("gla_ln"), 1)

            def gla_qk(e, u):
                act.wait_ge(sem("unit_done"), u + 1)
                act.activation(gqT[:, 2 * e:2 * e + 2, :], tiles(ps[:, units[u]["bank"], :]), ACT.Copy,
                               scale=(GK // GH) ** -0.5 if e < GK // 256 else 1.0).then_inc(took(u)[0], 1)

            def gla_cum():
                for b in range(2):
                    act.wait_ge(sem("gla_cummed"), b + 1)
                    act.activation(bcum[:, 2 * b:2 * b + 2, :], tiles(ps[:, 6 + b, :]), ACT.Copy,
                                   scale=1.0 / 16.0).then_inc(sem("gla_b"), 1)

            def gla_level(l):
                act.wait_ge(sem("gla_arg"), l + 1)
                act.activation(E1[:, :, :], E1[:, :, :], ACT.Exp).then_inc(sem("gla_E"), 1)

            def gla_decay():
                act.activation(EB[:, :, :], bcum[:, :, :], ACT.Exp).then_inc(sem("gla_EB"), 1)
                act.wait_ge(sem("gla_arg"), 7)
                act.activation(E1[:, :, :], E1[:, :, :], ACT.Exp).then_inc(sem("gla_E"), 1)

            def gla_ktok():
                for b in range(2):
                    act.wait_ge(sem("gla_kturned"), b + 1)
                    act.activation(kdt[:, 4 * b:4 * b + 4, :], by(ps[:, 6 + b, :], 4), ACT.Copy)\
                       .then_inc(sem("gla_kdt"), 1)

            def gla_v(u):
                for t in range(TT):
                    act.wait_ge(sem("half_done") if t == 0 else sem("unit_done"), u + 1)
                    act.activation(vg[:, t, :].rearrange("p (b n) -> p b n", b=2), ps[:, 2 * t:2 * t + 2, :],
                                   ACT.Copy).then_inc(sem(f"g{t}"), 1)

            def gla_g(e, u):
                act.wait_ge(sem("unit_done"), u + 1)
                act.activation(sgT[:, 2 * e:2 * e + 2, :], tiles(ps[:, units[u]["bank"], :]), ACT.Silu)\
                   .then_inc(took(u)[0], 1)

            def gla_sum(t):
                act.wait_ge(sem("gla_o"), 2 * t + 2)
                src = ps[:, 2 * t:2 * t + 2, :].rearrange("p b (h d) -> p (b h) d", d=GV)
                head_sums(t, src, GV, gy.rearrange("p (h c) t -> p h (c t)", h=GH))

            def gla_turn(t):
                for b in range(2):
                    act.wait_ge(sem("gla_y"), 2 * t + b + 1)
                    act.activation(ahi[:, 4 * b:4 * b + 4, t * P:(t + 1) * P], gy[:, 4 * b:4 * b + 4, :],
                                   ACT.Copy).then_inc(sem("gla_hi"), 1)

            def final(waits):
                act.dma_start(nfin, a["norm_final_2"].partition_broadcast(P)).then_inc(sem("nfin_in"), 16)
                link(act.activation(warm[:, :], warm[:, :], ACT.Sqrt))
                for t in range(TT):
                    act.wait_ge(sem(waits[t][0]), waits[t][1])
                    square_sums([(xs[:, t, :], x[:, t, :], ss[:, t, 0:1])])
                    act.activation(ss[:, t, 0:1], ss[:, t, 0:1], ACT.Sqrt, scale=1.0 / D, bias=eps[:, :])\
                       .then_inc(sem("root_out"), 1)

            def fox_norm():
                for g, v in fox_taken:
                    act.wait_ge(sem(g), v)
                act.activation(xs[:, :, 0:2 * FW], fqkv[:, :, 0:2 * FW], ACT.Square).then_inc(sem("fox_sq"), 1)
                root(ss[:, :, :], 1.0 / FD)

            def dn_silu():
                act.wait_ge(sem("conv_read"), 3 * DW // 256)
                for i in range(3):
                    part = dnT[:, DH * i:DH * (i + 1), :]
                    act.activation(part, part, ACT.Silu).then_inc(sem("dn_silu"), 1)
                for i in range(2):
                    act.wait_ge(sem("dn_silu"), i + 1)
                    act.activation(tiles(dsq[:, 1024 * i:1024 * (i + 1)]), dnT[:, DH * i:DH * (i + 1), :], ACT.Square)\
                       .then_inc(sem("dn_sq"), 1)

            def dn_unit():
                act.wait_ge(sem("dn_ss"), 1)
                act.activation(ss[:, 0, :], ps[:, 0, 0:16], ACT.Sqrt, bias=eps[:, :]).then_inc(sem("root_out"), 1)

            fox_taken = [s[3] for s in order if s[0] == "fox_qkv"]

            parts = dict(norm=norm, params=params, small=small, fox_qkv=fox_qkv, sc=sc, dn=dn, fox_turn=fox_turn,
                         glu=glu, relu2_split=relu2_split, ple_load=ple_load,
                         fox_cum=fox_cum, att_scores=att_scores, att_turn=att_turn, fox_out=fox_out, z=z,
                         gate=gate, dn_cum=dn_cum, dn_decay=dn_decay, dn_x0=dn_x0, dn_y=dn_y,
                         dn_sol=dn_sol, dn_out=dn_out, merge=merge, up=up, ple_gate=ple_gate, ple_p=ple_p,
                         ab_qk=ab_qk, ab_v=ab_v, pool_u=pool_u, lam=lam, pool_mm=pool_mm,
                         relu2=relu2, gla_low=gla_low, gla_gate=gla_gate, gla_qk=gla_qk, gla_cum=gla_cum,
                         gla_level=gla_level, gla_decay=gla_decay, gla_ktok=gla_ktok, gla_v=gla_v,
                         gla_g=gla_g, gla_sum=gla_sum, gla_turn=gla_turn, final=final, fox_norm=fox_norm,
                         dn_silu=dn_silu, dn_unit=dn_unit, dn_sum=dn_sum, ab_sum=ab_sum, ab_turn=ab_turn)
            parts["mm"] = lambda u, part: split_high(u + LEAD) if part == 0 and u + LEAD < NU else None
            act.dma_start(grow[:, :], a["g_mix"][0].rearrange("(k p) -> k p", p=P)).then_inc(sem("gmix_in"), 16)
            act.wait_ge(sem("constants"), made["ident"])
            for s in order:
                if s[0] in parts:
                    parts[s[0]](*s[1:])

        @block.vector
        def _(dve):
            n = [0]

            def link(ins):
                n[0] += 1
                ins.then_inc(sem("dve_own"), 1)
                dve.wait_ge(sem("dve_own"), n[0])

            def own(ins, name, value):
                ins.then_inc(sem(name), 1)
                dve.wait_ge(sem(name), value)

            def wide(ap, shape):
                return ap.to_broadcast([P] + shape)

            def split_low(u):
                dve.wait_ge(sem("hi_done"), u + 1)
                dve.tensor_tensor(wlo[:, u % SPLIT, :], raw[:, u % RAW, :], whi[:, u % SPLIT, :].bitcast(F32),
                                  ALU.subtract).then_inc(sem("lo_done"), 1)

            roots = [0]

            def root(ap, ins=None):
                roots[0] += 1
                if ins is not None:
                    ins.then_inc(sem("root_in"), 1)
                dve.wait_ge(sem("root_out"), roots[0])
                link(dve.reciprocal(ap, ap))

            def norm(i, waits):
                for t in range(TT):
                    root(ss[:, t, 0:1])
                    dve.tensor_scalar(diag[:, t, :], ident[:, :], ss[:, t, 0:1], None, ALU.mult)\
                       .then_inc(sem("norm_diag"), 1)
                if i == 0:
                    dve.wait_ge(sem("gmix_turned"), 1)
                    dve.tensor_copy(gcol0[:, :], ps[:, 7, 0:KD]).then_inc(sem("gcol0_done"), 1)
                    dve.wait_ge(sem("gcol0_done"), 1)
                    split_low(0)
                for k in range(KD):
                    dve.wait_ge(sem("norm_hi"), KD * i + (k | 1) + 1)
                    dve.scalar_tensor_tensor(out=hlo[:, k, :], in0=ps[:, k // 2, (k % 2) * T:(k % 2 + 1) * T],
                                             scalar=gain(i, k), in1=hhi[:, k, :].bitcast(F32),
                                             op0=ALU.mult, op1=ALU.subtract).then_inc(sem("norm_lo"), 1)
                if i == 0:
                    split_low(1)
                    dve.wait_ge(sem("constants"), made["all"])

            def params():
                dve.wait_ge(sem("colp_turned"), 1)
                own(dve.tensor_copy(colp[:, :, :].rearrange("p b n -> p (b n)"), ps[:, 7, 0:3 * P]), "colp_done", 1)
                own(dve.tensor_scalar(col("fox_gain", 0), col("fox_gain", 0), FD ** -0.5, None, ALU.mult),
                    "colp_done", 2)
                own(dve.tensor_scalar(col("subln", 0), col("subln", 0), 1.0 - LI, None, ALU.mult), "colp_done", 3)

            def small():
                dve.wait_ge(sem("params_in"), 16 * n_par)
                link(dve.memset(bias16[:, FH:FH + DH], 0.0))
                dve.wait_ge(sem("small_done"), 1)
                link(dve.tensor_tensor(zz[:, 0], ps[:, 6, 0:TT * NSM].rearrange("p (t n) -> p t n", t=TT),
                                       wide(bias16[:, :].unsqueeze(1), [TT, NSM]), ALU.add))
                dve.scalar_tensor_tensor(out=zz[:, 1], in0=zz[:, 0], scalar=-1.0, in1=zz[:, 0], op0=ALU.mult,
                                         op1=ALU.max).then_inc(sem("small_abs"), 1)
                dve.wait_ge(sem("small_exp"), 3)
                link(dve.tensor_scalar(zz[:, 3], zz[:, 1], 1.0, None, ALU.add))
                link(dve.scalar_tensor_tensor(out=zz[:, 1], in0=zz[:, 3], scalar=-1.0, in1=zz[:, 1],
                                              op0=ALU.add, op1=ALU.subtract))
                link(dve.reciprocal(zz[:, 3], zz[:, 3]))
                link(dve.tensor_tensor(zz[:, 1], zz[:, 1], zz[:, 3], ALU.mult))
                link(dve.tensor_tensor(zz[:, 2], zz[:, 2], zz[:, 1], ALU.subtract))
                link(dve.scalar_tensor_tensor(out=gg[:, :, :], in0=zz[:, 0, :, FH + DH:NSM], scalar=0.0,
                                              in1=zz[:, 2, :, FH + DH:NSM], op0=ALU.max, op1=ALU.add))
                link(dve.scalar_tensor_tensor(out=gg[:, :, :], in0=gg[:, :, :], scalar=-1.0,
                                              in1=wide(alog[:, :].unsqueeze(1), [TT, DH]),
                                              op0=ALU.mult, op1=ALU.mult))
                own(dve.scalar_tensor_tensor(out=zz[:, 3], in0=zz[:, 0], scalar=0.0, in1=zz[:, 2],
                                             op0=ALU.min, op1=ALU.subtract), "small_lsg", 1)
                for t in range(TT):
                    dve.tensor_tensor(fcum[:, t], wide(tri[:, :].unsqueeze(1), [FH, P]),
                                      wide(zz[:, 3, t, 0:FH].unsqueeze(2), [FH, P]), ALU.mult)\
                       .then_inc(sem("fox_f"), 1)

            def sc(e, part, j, u):
                out = cy[:, e % 2, :, :]
                if part == 2:
                    dve.wait_ge(sem("unit_done"), u + 1)
                    dve.wait_ge(*took(u - 1))
                    own(dve.tensor_tensor(conv[:, j % 2, :, PAD:PAD + T], tiles(ps[:, units[u]["bank"], :]), out,
                                          ALU.mult), *took_name(u))
                    taps("sc_conv", 3, BT, 2 * e, j, out)
                if part == 0:
                    dve.wait_ge(sem("unit_done"), u + 1)
                    own(dve.tensor_tensor(out, tiles(ps[:, units[u]["bank"], :]), out, ALU.mult), *took_name(u))
                    dve.wait_ge(sem("sc_hi"), e + 1)
                    s = slice(BT + 2 * e, BT + 2 * e + 2)
                    dve.tensor_tensor(alo[:, s, :], out, ahi[:, s, :].bitcast(F32), ALU.subtract)\
                       .then_inc(sem("sc_lo"), 1)

            def took_name(u):
                g, k = units[u]["free"][0]
                return g, k + 1

            def taps(name, width, per_tap, tile0, j, out):
                for i in range(width - 1, -1, -1):
                    lag = width - 1 - i
                    for q in range(2):
                        src = conv[:, j % 2, q, PAD - lag:PAD - lag + T]
                        w = col(name, i * per_tap + tile0 + q)
                        if lag == 0:
                            ins = dve.tensor_scalar(out[:, q, :], src, w, None, ALU.mult)
                        else:
                            ins = dve.scalar_tensor_tensor(out=out[:, q, :], in0=src, scalar=w,
                                                           in1=out[:, q, :], op0=ALU.mult, op1=ALU.add)
                    if i > 0:
                        link(ins)
                own(ins, "conv_read", j + 1)

            def taps_ffn(tile0, j, out):
                for i in range(2, -1, -1):
                    for q in range(2):
                        src = conv[:, j % 2, q, PAD - 2 + i:PAD - 2 + i + T]
                        w = col(f"ffn_conv{i}", tile0 + q)
                        if i == 2:
                            ins = dve.tensor_scalar(out[:, q, :], src, w, None, ALU.mult)
                        else:
                            ins = dve.scalar_tensor_tensor(out=out[:, q, :], in0=src, scalar=w,
                                                           in1=out[:, q, :], op0=ALU.mult, op1=ALU.add)
                    if i > 0:
                        link(ins)
                own(ins, "conv_read", j + 1)

            def dn(e, j, u):
                dve.wait_ge(*took(u))
                taps("dn_conv", 4, 3 * BT, 2 * e, j, dnT[:, 2 * e:2 * e + 2, :])

            def fox_norm():
                dve.wait_ge(sem("fox_sq"), 1)
                nh = 2 * FH
                qk = fqkv[:, :, 0:2 * FW].rearrange("p t (h d) -> p t h d", d=FD)
                sq = xs[:, :, 0:2 * FW].rearrange("p t (h d) -> p t h d", d=FD)
                root(ss[:, :, :], dve.tensor_reduce(ss[:, :, :], sq, AX.X, ALU.add))
                for t in range(TT):
                    dve.tensor_tensor(qk[:, t], qk[:, t], wide(ss[:, t, :].unsqueeze(2), [nh, FD]), ALU.mult)\
                       .then_inc(sem("fox_qk"), 1)

            def att_scores(w, g):
                b, maps = groups[g]
                k, width = len(maps), P * (b + 1)
                Sg = att[w]["S"][:, g % 2, :].rearrange("p (m j) -> p m j", m=k)
                halves_ = [(Sg[:, odd:k:2, :], by(ps[:, bank, 0:k // 2 * width], k // 2))
                           for odd, bank in ((0, 6 + g % 2), (1, 2 + g % 2))]
                dve.wait_ge(sem(f"att{w}_scored"), g + 1)
                if g >= 2:
                    dve.wait_ge(sem(f"att{w}_turned"), g - 1)
                diag = slice(b * P, width)
                if w == 0:
                    dve.wait_ge(sem("fox_bias"), 4)
                    for odd, (dst, src) in enumerate(halves_):
                        link(dve.tensor_tensor(dst, src, fbias[:, maps[0] + odd:maps[0] + k:2, 0:width], ALU.add))
                    link(dve.tensor_tensor(Sg[:, :, diag], Sg[:, :, diag], wide(cneg[:, :].unsqueeze(1), [k, P]),
                                           ALU.add))
                else:
                    for dst, src in halves_:
                        if b:
                            link(dve.tensor_copy(dst[:, :, 0:P], src[:, :, 0:P]))
                        link(dve.tensor_tensor(dst[:, :, diag], src[:, :, diag],
                                               wide(dneg[:, :].unsqueeze(1), [k // 2, P]), ALU.add))
                dve.tensor_reduce(nmax[:, g % 2, 0:k], Sg, AX.X, ALU.max, negate=True)\
                   .then_inc(sem(f"att{w}_max"), 1)

            def att_norm(w, g):
                b, maps = groups[g]
                k, width = len(maps), P * (b + 1)
                Sg = att[w]["S"][:, g % 2, :].rearrange("p (m j) -> p m j", m=k)
                exps = sum(len(m) for _, m in groups[:g + 1])
                dve.wait_ge(sem(f"att{w}_exp"), exps)
                r = rsum[:, g % 2, 0:k]
                link(dve.reciprocal(r, r))
                if w == 0:
                    dve.tensor_tensor(Sg, Sg, wide(r.unsqueeze(2), [k, width]), ALU.mult)\
                       .then_inc(sem("att0_p"), 1)
                    return
                r2 = rsum[:, g % 2, 0:k].rearrange("p (h m) -> p h m", m=2)[:, :, 1]
                link(dve.tensor_scalar(r2, r2, lamw[:, 2:3], None, ALU.mult))
                for i in range(0, k, 2):
                    link(dve.tensor_scalar(Sg[:, i, :], Sg[:, i, :], rsum[:, g % 2, i:i + 1], None, ALU.mult))
                    ins = dve.scalar_tensor_tensor(out=Sg[:, i, :], in0=Sg[:, i + 1, :],
                                                   scalar=rsum[:, g % 2, i + 1:i + 2], in1=Sg[:, i, :],
                                                   op0=ALU.mult, op1=ALU.add)
                ins.then_inc(sem("att1_p"), 1)

            def fox_out():
                for b in range(2):
                    dve.wait_ge(sem("fox_hi"), b + 1)
                    s = slice(2 * b, 2 * b + 2)
                    dve.tensor_tensor(alo[:, s, :], tiles(ps[:, b, :]), ahi[:, s, :].bitcast(F32), ALU.subtract)\
                       .then_inc(sem("fox_lo"), 1)

            def dn_unit():
                root(ss[:, 0, :])
                for i in range(2):
                    dve.tensor_tensor(by(dsq[:, 1024 * i:1024 * (i + 1)], 8), wide(ident[:, :].unsqueeze(1), [8, P]),
                                      wide(ss[:, 0, 8 * i:8 * i + 8].unsqueeze(2), [8, P]), ALU.mult)\
                       .then_inc(sem("dn_dd"), 1)

            def dn_scale():
                q, k = dnT[:, 0:DH, :], dnT[:, DH:2 * DH, :]
                for i, (part, s) in enumerate(((q, DV ** -0.5), (k, 1.0))):
                    dve.wait_ge(sem("dn_bc"), 2 * i + 2)
                    two = ps[:, 2 * i:2 * i + 2, :].rearrange("p b (c t) -> p (b c) t", t=T)
                    own(dve.scalar_tensor_tensor(out=part, in0=part, scalar=s, in1=two, op0=ALU.mult,
                                                 op1=ALU.mult), "dn_qk", i + 1)

            def dn_cum():
                dve.wait_ge(sem("dn_gc"), 1)
                pg = ps[:, 6, 0:TT * 2 * DH].rearrange("p (t a h) -> p t a h", t=TT, a=2)
                link(dve.tensor_copy(gcol[:, :, :], pg[:, :, 0, :]))
                link(dve.tensor_copy(gx[:, :, 0, :], pg[:, :, 0, :]))
                dve.tensor_tensor(gx[:, :, 1, :], pg[:, :, 1, :], gcol[:, :, :], ALU.subtract)\
                   .then_inc(sem("dn_gx"), 1)
                dve.wait_ge(sem("dn_egx"), 1)
                link(dve.tensor_tensor(gx[:, :, 0, :], gx[:, :, 0, :], beta[:, :, :], ALU.mult))

            def dn_tok(t):
                dve.wait_ge(sem("dn_tokened"), 2 * t + 2)
                k, v = by(ps[:, 2 * t, :], DH), by(ps[:, 2 * t + 1, :], DH)
                dve.tensor_tensor(rhsk[:, t], k, wide(gx[:, t, 0, :].unsqueeze(2), [DH, P]), ALU.mult)\
                   .then_inc(sem("dn_tok"), 1)
                dve.tensor_tensor(kdec[:, t], k, wide(gx[:, t, 1, :].unsqueeze(2), [DH, P]), ALU.mult)\
                   .then_inc(sem("dn_tok"), 1)
                dve.tensor_tensor(vb[:, t], v, wide(beta[:, t, :].unsqueeze(2), [DH, P]), ALU.mult)\
                   .then_inc(sem("dn_tok"), 1)

            def dn_decay(t):
                if t >= 1:
                    dve.wait_ge(sem("dn_solved"), 2 * t)
                dve.tensor_tensor(X, wide(tri64[:, :].unsqueeze(1), [DH, P]),
                                  wide(gg[:, t, :].unsqueeze(2), [DH, P]), ALU.mult).then_inc(sem("dn_gb"), 1)
                dve.tensor_tensor(XT, wide(ident[:, :].unsqueeze(1), [DH, P]),
                                  wide(beta[:, t, :].unsqueeze(2), [DH, P]), ALU.mult).then_inc(sem("dn_gb"), 1)
                dve.wait_ge(sem("dn_eg"), t + 1)
                link(dve.tensor_tensor(DT, by(ps[:, 6, :], DH), wide(gcol[:, t, :].unsqueeze(2), [DH, P]),
                                       ALU.subtract))
                dve.tensor_scalar(DT, DT, 0.0, None, ALU.min).then_inc(sem("dn_dt"), 1)
                dve.tensor_copy(gt[:, t], EG[:, :, CH - 1:P:CH]).then_inc(sem("dn_gt"), 1)
                dve.wait_ge(sem("dn_edt"), t + 1)
                link(dve.tensor_tensor(DT, DT, wide(tri64[:, :].unsqueeze(1), [DH, P]), ALU.mult))

            def dn_kk(t):
                dve.wait_ge(sem("dn_kked"), 2 * t + 2)
                link(dve.tensor_tensor(LT, by(ps[:, 2 * t, :], DH), DT, ALU.mult))
                link(dve.tensor_tensor(LT, by(ps[:, 7, :], DH), LT, ALU.mult))
                link(dve.tensor_tensor(qkT[:, t], by(ps[:, 2 * t + 1, :], DH), DT, ALU.mult))
                q = dnT[:, 0:DH, t * P:(t + 1) * P]
                dve.tensor_tensor(q, q, EG, ALU.mult).then_inc(sem("dn_lt"), 1)

            def dn_x0(t):
                if t >= 1:
                    dve.wait_ge(sem("dn_solved"), 2 * t)
                link(dve.tensor_tensor(Bl, LT, wide(lev[:, 0, :].unsqueeze(1), [DH, P]), ALU.mult))
                dve.tensor_tensor(XT, wide(ident[:, :].unsqueeze(1), [DH, P]), Bl, ALU.subtract)\
                   .then_inc(sem("dn_x0"), 1)
                dve.wait_ge(sem("dn_x0"), t + 1)

            def dn_y(t, l):
                dve.tensor_tensor(Bl, LT, wide(lev[:, l, :].unsqueeze(1), [DH, P]), ALU.mult)\
                   .then_inc(sem("dn_B"), 1)

            def dn_z(t, l):
                dve.wait_ge(sem("dn_XBX"), 2 * (5 * t + l))
                own(dve.tensor_tensor(XT, XT, by(ps[:, 0, :], DH), ALU.subtract), "dn_X2", 2 * (5 * t + l) - 1)
                own(dve.tensor_tensor(X, X, by(ps[:, 1, :], DH), ALU.subtract), "dn_X2", 2 * (5 * t + l))

            def dn_sol(t):
                dve.wait_ge(sem("dn_solved"), 2 * t + 1)
                own(dve.tensor_copy(vb[:, t], by(ps[:, 6, :], DH)), "dn_u", t + 1)

            def dn_new(c):
                t, p0 = c // 2, CH * (c % 2)
                if c == 0:
                    return
                dve.wait_ge(sem("dn_kS"), c)
                part = vb[p0:p0 + CH, t]
                own(dve.tensor_tensor(part, part, by(ps[p0:p0 + CH, 0, :], DH), ALU.subtract), "dn_vnew", c)

            def dn_state(c):
                if c == NCH - 1:
                    return
                t = c // 2
                dve.wait_ge(sem("dn_supd"), c + 1)
                pS = by(ps[:, 1, :], DH)
                if c == 0:
                    own(dve.tensor_copy(S, pS), "dn_S", 1)
                    return
                for h in range(DH):
                    ins = dve.scalar_tensor_tensor(out=S[:, h, :], in0=S[:, h, :], scalar=gt[:, t, h, c % 2:c % 2 + 1],
                                                   in1=pS[:, h, :], op0=ALU.mult, op1=ALU.add)
                own(ins, "dn_S", c + 1)

            def head_scale(t, out, src, width):
                heads = src.shape[1]
                r_ = ss[:, t, 0:heads]
                root(r_)
                return dve.tensor_tensor(out, src, wide(r_.unsqueeze(2), [heads, width]), ALU.mult)

            def dn_sum(t):
                head_scale(t, rhsk[:, t], by(ps[:, 2 + t, :], DH), DV).then_inc(sem("dn_onorm"), 1)

            def dn_out(t):
                dve.wait_ge(sem("dn_oturned"), t + 1)
                if t >= 1:
                    dve.wait_ge(sem("dn_hi"), t)
                own(dve.scalar_tensor_tensor(out=XT, in0=by(ps[:, 6, :], DH), scalar=col("dn_gain", 0),
                                             in1=zT[:, :, t * P:(t + 1) * P], op0=ALU.mult, op1=ALU.mult),
                    "dn_y2", t + 1)
                dve.wait_ge(sem("dn_hi"), t + 1)
                s = (slice(None), slice(2 * BT, 3 * BT), slice(t * P, (t + 1) * P))
                own(dve.tensor_tensor(alo[s], XT, ahi[s].bitcast(F32), ALU.subtract), "dn_lo", t + 1)

            def merge(n_, g, b, u):
                done = sem("half_done") if b == 0 else sem("unit_done")
                dve.wait_ge(done, u + 1)
                s = 4 * g + 2 * b
                merged = mg[:, s:s + 2, :]
                gate_ = gates[:, KD * n_ + s:KD * n_ + s + 2, :]
                own(dve.tensor_tensor(gate_, tiles(ps[:, 4 + b, :]), gate_, ALU.mult), f"c{4 + b}",
                    units[u]["free"][b][1] + 1)
                if n_ == 0:
                    return
                ins = dve.tensor_tensor(merged, merged, gate_, ALU.add)
                if n_ < NB - 1:
                    link(ins)
                    return
                own(ins, "merged", 2 * g + b + 1)
                dve.wait_ge(sem("merged_hi"), 2 * g + b + 1)
                dve.tensor_tensor(hlo[:, s:s + 2, :], merged, hhi[:, s:s + 2, :].bitcast(F32), ALU.subtract)\
                   .then_inc(sem("merged_lo"), 1)

            def resid(u):
                for t in range(TT):
                    dve.wait_ge(sem("half_done") if t == 0 else sem("unit_done"), u + 1)
                    xt = x[:, t, :].rearrange("p (b n) -> p b n", b=2)
                    dve.tensor_tensor(xt, xt, ps[:, 2 * t:2 * t + 2, :], ALU.add).then_inc(sem(f"g{t}"), 1)

            def up(c, part, u):
                dve.wait_ge(*took(u))
                taps_ffn(UPT * part + 2 * c, len(convs) + 2 * c + part, cy[:, part, :, :])

            def glu(c, down):
                dve.wait_ge(sem("glu_silu"), c + 1)
                own(dve.tensor_tensor(cy[:, 1, :, :], cy[:, 0, :, :], cy[:, 1, :, :], ALU.mult), "glu_prod", c + 1)
                dve.wait_ge(sem("glu_hi"), c + 1)
                s = slice(2 * (c % 2), 2 * (c % 2) + 2)
                own(dve.tensor_tensor(alo[:, s, :], cy[:, 1, :, :], ahi[:, s, :].bitcast(F32), ALU.subtract),
                    "glu_lo", c + 1)

            def ple_p():
                dve.wait_ge(sem("ple_hi"), 1)
                dve.tensor_tensor(alo[:, 4:6, :], tiles(ps[:, 6, :]), ahi[:, 4:6, :].bitcast(F32), ALU.subtract)\
                   .then_inc(sem("ple_lo"), 1)

            def ple_x(u):
                for t in range(TT):
                    dve.wait_ge(sem("half_done") if t == 0 else sem("unit_done"), u + 1)
                    st_ = sg[:, t, :].rearrange("p (b n) -> p b n", b=2)
                    own(dve.tensor_tensor(st_, ps[:, 2 * t:2 * t + 2, :], st_, ALU.mult), f"g{t}",
                        units[u]["free"][t][1] + 1)
                    dve.tensor_tensor(x[:, t, :], x[:, t, :], sg[:, t, :], ALU.add).then_inc(sem("ple_added"), 1)

            def ab_qk(e, u):
                if e == 0:
                    dve.memset(pu[:, :, 0:W0], 0.0).then_inc(sem("pool_zero"), 1)

            def lam():
                dve.wait_ge(sem("pw_in"), 32)
                w4 = lamr[:, :, :].rearrange("p (a b) d -> p a b d", b=2)
                link(dve.tensor_tensor(w4[:, :, 0, :], w4[:, :, 0, :], w4[:, :, 1, :], ALU.mult))
                dve.tensor_reduce(lamw[:, 0:2], w4[:, :, 0, :], AX.X, ALU.add).then_inc(sem("lam_sum"), 1)
                dve.wait_ge(sem("lam_exp"), 1)
                link(dve.tensor_tensor(lamw[:, 2:3], lamw[:, 1:2], lamw[:, 0:1], ALU.subtract))
                link(dve.tensor_scalar(lamw[:, 2:3], lamw[:, 2:3], -LI, None, ALU.add))

            def pool_win():
                dve.wait_ge(*pool_ready[0])
                dve.wait_ge(*pool_ready[1])
                E_ = W0 + T
                sums, src = (p1, p2, p3, p4), pu
                at = 0
                for l, dst in enumerate(sums):
                    s, g0 = 1 << l, l
                    at = 2 * s - 1
                    link(dve.tensor_tensor(dst[:, g0:4, at:E_], src[:, g0:4, at:E_], src[:, g0:4, at - s:E_ - s],
                                           ALU.add))
                    src = dst
                for g, w in enumerate(POOLS):
                    link(dve.tensor_tensor(pfix[:, g, :], sums[g][:, g, W0:W0 + 16], inv[:, g, :], ALU.mult))
                    link(dve.scalar_tensor_tensor(out=pr[:, g, 16:T], in0=sums[g][:, g, W0 + 16:E_],
                                                  scalar=1.0 / w, in1=pu[:, g, W0 + 16:E_],
                                                  op0=ALU.mult, op1=ALU.subtract))
                own(dve.tensor_tensor(pr[:, :, 0:16], pfix, pu[:, :, W0:W0 + 16], ALU.subtract), "pool_r", 1)

            def pool_mm():
                dve.wait_ge(sem("pool_mmed"), 1)
                for g in range(4):
                    ins = dve.tensor_scalar(pr[:, g, :], tiles(ps[:, 2 + g // 2, :])[:, g % 2, :],
                                            col("pool_scale", g), None, ALU.mult)
                own(ins, "pool_y", 1)
                dve.wait_ge(sem("pool_hi"), 1)
                dve.tensor_tensor(alo[:, 4:8, :], pr, ahi[:, 4:8, :].bitcast(F32), ALU.subtract)\
                   .then_inc(sem("pool_lo"), 1)

            def ab_sum(b):
                head_scale(b, ob[:, b], by(ps[:, b, :], 4), P).then_inc(sem("ab_onorm"), 1)

            def ab_turn(b):
                dve.wait_ge(sem("ab_hi"), b + 1)
                s = (slice(None), slice(0, 4), slice(b * P, (b + 1) * P))
                dve.scalar_tensor_tensor(out=alo[s], in0=by(ps[:, 6 + b, :], 4), scalar=col("subln", 0),
                                         in1=ahi[s].bitcast(F32), op0=ALU.mult, op1=ALU.subtract)\
                   .then_inc(sem("ab_lo"), 1)

            def relu2(i, u):
                dve.wait_ge(*took(u))
                y = cy[:, i % 2, :, :]
                own(dve.tensor_tensor(y, y, y, ALU.mult), "relu2_sq", i + 1)

            def relu2_split(i, c, down):
                dve.wait_ge(sem("relu2_hi"), i + 1)
                s = slice(2 * (c % 2), 2 * (c % 2) + 2)
                dve.tensor_tensor(alo[:, s, :], cy[:, i % 2, :, :], ahi[:, s, :].bitcast(F32), ALU.subtract)\
                   .then_inc(sem("relu2_lo"), 1)

            def gla_gate():
                dve.wait_ge(sem("gla_gated"), 2)
                two = ps[:, 0:2, :]
                link(dve.tensor_scalar(gmin, two, 0.0, None, ALU.min))
                dve.scalar_tensor_tensor(out=gla, in0=gmin, scalar=-2.0, in1=two, op0=ALU.mult, op1=ALU.add).then_inc(sem("gla_abs"), 1)
                dve.wait_ge(sem("gla_ln"), 2)
                own(dve.tensor_tensor(gla, gmin, gla, ALU.subtract), "gla_la", 1)

            def gla_pairs(l):
                dve.wait_ge(sem("gla_paired"), 2 * l + 2)
                two = ps[:, 6:8, :].rearrange("p b (g i) -> p (b g) i", i=P)
                mask = ident[:, :] if l == 0 else lev[:, l - 1, :]
                dst = attn if l == 0 else atmp
                own(dve.tensor_tensor(dst, two, wide(mask.unsqueeze(1), [TT * GH, P]), ALU.mult), "gla_took", l + 1)
                if l:
                    link(dve.tensor_tensor(attn, attn, atmp, ALU.add))

            def halves(ap, l):
                return ap.rearrange("p h t -> p (h t)").rearrange("p (m two s) -> p m two s", two=2, s=1 << l)

            def gla_level(l):
                s = 1 << l
                if l == 0:
                    dve.wait_ge(sem("gla_b"), 2)
                    dve.wait_ge(*gla_qk_ready[0])
                    dve.wait_ge(*gla_qk_ready[1])
                b_, e_, c_ = halves(bcum, l), halves(E1, l), halves(Cl, l)
                q_, k_ = halves(gqT[:, 0:GH, :], l), halves(gqT[:, GH:2 * GH, :], l)
                m = GH * T // (2 * s)
                ref = wide(b_[:, :, 0, s - 1:s], [m, s])
                dve.tensor_tensor(e_[:, :, 1, :], b_[:, :, 1, :], ref, ALU.subtract)
                own(dve.tensor_tensor(e_[:, :, 0, :], ref, b_[:, :, 0, :], ALU.subtract), "gla_arg", l + 1)
                dve.wait_ge(sem("gla_E"), l + 1)
                dve.tensor_tensor(c_[:, :, 1, :], e_[:, :, 1, :], q_[:, :, 1, :], ALU.mult)
                own(dve.tensor_tensor(c_[:, :, 0, :], e_[:, :, 0, :], k_[:, :, 0, :], ALU.mult), "gla_C", l + 1)

            def gla_decay():
                b_ = bcum.rearrange("p h (c s) -> p (h c) s", s=CH)
                e_ = E1.rearrange("p h (c s) -> p (h c) s", s=CH)
                own(dve.tensor_tensor(e_, wide(b_[:, :, CH - 1:CH], [GH * NCH, CH]), b_, ALU.subtract), "gla_arg", 7)
                dve.wait_ge(sem("gla_EB"), 1)
                q = gqT[:, 0:GH, :]
                link(dve.tensor_tensor(q, q, EB, ALU.mult))
                dve.wait_ge(sem("gla_E"), 7)
                own(dve.tensor_tensor(Cl, E1, gqT[:, GH:2 * GH, :], ALU.mult), "gla_C", 7)

            def gla_chunk(c):
                if c == NCH - 1:
                    return
                dve.wait_ge(sem("gla_supd"), 2 * c + 2)
                pS = ps[:, 6:8, :].rearrange("p b (h d) -> p (b h) d", d=GV)
                if c == 0:
                    own(dve.tensor_copy(GS, pS), "gla_S", 1)
                    return
                for h in range(GH):
                    ins = dve.scalar_tensor_tensor(out=GS[:, h, :], in0=GS[:, h, :],
                                                   scalar=EB[:, h, CH * c + CH - 1:CH * c + CH],
                                                   in1=pS[:, h, :], op0=ALU.mult, op1=ALU.add)
                own(ins, "gla_S", c + 1)

            def gla_sum(t):
                head_scale(t, og[t], ps[:, 2 * t:2 * t + 2, :].rearrange("p b (h d) -> p (b h) d", d=GV), GV)\
                    .then_inc(sem("gla_onorm"), 1)

            def gla_turn(t):
                if t == 0:
                    for ready in gla_g_ready:
                        dve.wait_ge(*ready)
                for b in range(2):
                    dve.wait_ge(sem("gla_oturned"), 2 * t + b + 1)
                    for i in range(4 * b, 4 * b + 4):
                        ins = dve.scalar_tensor_tensor(out=gy[:, i, :], in0=by(ps[:, 6 + b, :], 4)[:, i % 4, :],
                                                       scalar=col("gla_norm", i),
                                                       in1=sgT[:, i, t * P:(t + 1) * P],
                                                       op0=ALU.mult, op1=ALU.mult)
                    own(ins, "gla_y", 2 * t + b + 1)
                for b in range(2):
                    dve.wait_ge(sem("gla_hi"), 2 * t + b + 1)
                    s = (slice(None), slice(4 * b, 4 * b + 4), slice(t * P, (t + 1) * P))
                    own(dve.tensor_tensor(alo[s], gy[:, 4 * b:4 * b + 4, :], ahi[s].bitcast(F32), ALU.subtract),
                        "gla_lo", 2 * t + b + 1)

            def final(waits):
                dve.wait_ge(sem("nfin_in"), 16)
                for t in range(TT):
                    root(ss[:, t, 0:1])
                    dve.scalar_tensor_tensor(out=xs[:, t, :], in0=x[:, t, :], scalar=ss[:, t, 0:1], in1=nfin,
                                             op0=ALU.mult, op1=ALU.mult).then_inc(sem("final_x"), 1)

            gla_g_ready = [took(s[2]) for s in order if s[0] == "gla_g"][-2:]
            pool_ready = [took(s[2]) for s in order if s[0] == "pool_u"]
            gla_qk_ready = [took(s[2]) for s in order if s[0] == "gla_qk"][2:]
            parts = dict(norm=norm, params=params, small=small, sc=sc, dn=dn, fox_norm=fox_norm, dn_scale=dn_scale,
                         dn_sum=dn_sum, ab_sum=ab_sum, ab_turn=ab_turn, gla_sum=gla_sum, gla_turn=gla_turn,
                         att_scores=att_scores, att_norm=att_norm, glu=glu, relu2_split=relu2_split,
                         fox_out=fox_out, dn_unit=dn_unit, dn_cum=dn_cum, dn_tok=dn_tok,
                         dn_decay=dn_decay, dn_kk=dn_kk, dn_x0=dn_x0, dn_y=dn_y, dn_z=dn_z, dn_sol=dn_sol,
                         dn_new=dn_new, dn_state=dn_state, dn_out=dn_out, merge=merge, resid=resid, up=up,
                         ple_p=ple_p, ple_x=ple_x, ab_qk=ab_qk, lam=lam, pool_win=pool_win, pool_mm=pool_mm,
                         relu2=relu2, gla_gate=gla_gate, gla_pairs=gla_pairs,
                         gla_level=gla_level, gla_decay=gla_decay, gla_chunk=gla_chunk,
                         final=final)
            parts["mm"] = lambda u, part: split_low(u + LEAD) if part == 1 and u + LEAD < NU else None
            dve.wait_ge(sem("constants"), made["ident"])
            for s in order:
                if s[0] in parts:
                    parts[s[0]](*s[1:])

        @block.tensor
        def _(pe):
            def mm(u, part):
                w = units[u]
                s = u % SPLIT
                if part == 0:
                    pe.wait_ge(sem("lo_done"), u + 1)
                    if u not in fresh:
                        for name, v in w["needs"]:
                            pe.wait_ge(sem(name), v)
                first = part == 0
                free = w["free"] if w["kind"] == "T" else w["free"][part:part + 1]
                for name, v in free:
                    if v:
                        pe.wait_ge(sem(name), v)
                hi, lo = (hhi, hlo) if w["act"] == "h" else (ahi, alo)
                k0 = w.get("k0", 0)

                def normed(k):
                    if first and u in fresh:
                        pe.wait_ge(sem("norm_lo"), KD * fresh[u] + (k + 1 if w["kind"] == "C" else KD))

                if w["kind"] in "CB":
                    nk, width = (KD, 256) if w["kind"] == "C" else (4, 512)
                    n = width // P // 2
                    for ct in range(part * n, part * n + n):
                        out = ps[:, w["bank"] + ct // 2, (ct % 2) * T:(ct % 2 + 1) * T]
                        for k in range(nk):
                            at = k * width + ct * P
                            wh, wl = whi[:, s, at:at + P], wlo[:, s, at:at + P]
                            normed(k)
                            pe.matmul(out, wh, hi[:, k0 + k, :], start=k == 0, stop=False)
                            pe.matmul(out, wh, lo[:, k0 + k, :], start=False, stop=False)
                            ins = pe.matmul(out, wl, hi[:, k0 + k, :], start=False, stop=k == nk - 1)
                else:
                    nk, banks = (4, [(w.get("bank", 0) + part, 0)]) if w["kind"] == "T" else \
                        (2, [(2 * part + b, b) for b in range(2)])
                    width = 512 if w["kind"] == "T" else D
                    for bank, b in banks:
                        out = ps[:, bank, :]
                        for k in range(nk):
                            at = k * width + 512 * b
                            wh, wl = whi[:, s, at:at + 512], wlo[:, s, at:at + 512]
                            xh = hi[:, k0 + k, part * P:(part + 1) * P]
                            xl = lo[:, k0 + k, part * P:(part + 1) * P]
                            start, stop = w["first"] and k == 0, w["last"] and k == nk - 1
                            if b == 0:
                                normed(k0 + k)
                            pe.matmul(out, xh, wh, start=start, stop=False)
                            pe.matmul(out, xh, wl, start=False, stop=False)
                            ins = pe.matmul(out, xl, wh, start=False, stop=stop)
                ins.then_inc(sem("half_done") if part == 0 else sem("unit_done"), 1)

            def norm(i, waits):
                if i == 0:
                    pe.wait_ge(sem("gmix_in"), 16)
                    pe.transpose(ps[:, 7, 0:KD], grow[:, :], ident[0:KD, 0:KD]).then_inc(sem("gmix_turned"), 1)
                for t in range(TT):
                    pe.wait_ge(sem("norm_diag"), TT * i + t + 1)
                    for k in range(KD):
                        at = (k % 2) * T + t * P
                        ins = pe.matmul(ps[:, k // 2, at:at + P], x[:, t, k * P:(k + 1) * P], diag[:, t, :],
                                        start=True, stop=True)
                        if t == TT - 1 and k % 2:
                            ins.then_inc(sem("norm_turned"), 1)

            def params():
                pe.wait_ge(sem("params_in"), 16 * n_par)
                for b in range(3):
                    ins = pe.transpose(ps[:, 7, b * P:(b + 1) * P], rows[:, b, :], ident[:, :])
                ins.then_inc(sem("colp_turned"), 1)

            def small():
                pe.wait_ge(sem("norm_lo"), KD)
                for t in range(TT):
                    for k in range(KD):
                        for j, part in enumerate((hhi, hlo)):
                            ins = pe.matmul(ps[:, 6, t * NSM:(t + 1) * NSM], part[:, k, t * P:(t + 1) * P].bitcast(F32),
                                            wsm[:, k, :], start=k == 0 and j == 0, stop=k == KD - 1 and j == 1)
                ins.then_inc(sem("small_done"), 1)

            def fox_turn(t):
                pe.wait_ge(sem("fox_qk"), t + 1)
                for b in range(2):
                    for c in range(4):
                        at = FW * b + c * P
                        ins = pe.transpose(ps[:, 2 * t + b, c * P:(c + 1) * P], fqkv[:, t, at:at + P], ident[:, :])
                    ins.then_inc(sem("fox_turned"), 1)

            def fox_cum(t):
                pe.wait_ge(sem("fox_f"), TT)
                pe.wait_ge(sem("fox_T"), 4)
                for b in range(2):
                    out = by(ps[:, 2 * t + b, :], 4)
                    if t:
                        lf = zz[:, 3, 0, 4 * b:4 * b + 4].unsqueeze(2).to_broadcast([P, 4, P])
                        pe.matmul(out, ones[:, :], lf, start=True, stop=False)
                    pe.matmul(out, ones[:, :], fcum[:, t, 4 * b:4 * b + 4, :], start=t == 0, stop=True)\
                      .then_inc(sem("fox_cummed"), 1)

            def att_scores(w, g):
                b, maps = groups[g]
                width = P * (b + 1)
                q, k = att[w]["q"], att[w]["k"]
                if g == 0:
                    if w == 0:
                        pe.wait_ge(sem("fox_T"), 4)
                        pe.wait_ge(sem("fox_bias"), 4)
                    else:
                        for r in ab_qk_ready:
                            pe.wait_ge(*r)
                if g >= 2:
                    pe.wait_ge(sem(f"att{w}_PT"), g - 1)
                for i, f in enumerate(maps):
                    half = slice(FD * (f % 2), FD * (f % 2) + FD)
                    bank, at = (6 if f % 2 == 0 else 2) + g % 2, (i // 2) * width
                    ins = pe.matmul(ps[:, bank, at:at + width], q[half, f // 2, b * P:(b + 1) * P],
                                    k[half, f // 2, 0:width], start=True, stop=True)
                ins.then_inc(sem(f"att{w}_scored"), 1)

            def att_turn(w, g):
                pe.wait_ge(sem(f"att{w}_p"), g + 1)
                for i, (at, _, _) in enumerate(turned(w, g)):
                    ins = pe.transpose(ps[:, 6 + g % 2, i * P:(i + 1) * P], att[w]["S"][:, g % 2, at:at + P],
                                       ident[:, :])
                ins.then_inc(sem(f"att{w}_turned"), 1)

            def att_values(w, g):
                b, _ = groups[g]
                pe.wait_ge(sem(f"att{w}_PT"), g + 1)
                if g == 0:
                    if w == 0:
                        pe.wait_ge(sem("fox_bias"), 4)
                    else:
                        pe.wait_ge(*ab_v_ready)
                for i, (_, f, kt) in enumerate(turned(w, g)):
                    pT = att[w]["PT"][:, g % 2, i * P:(i + 1) * P]
                    if w == 0:
                        at = (f // 2 % 2) * T + b * P
                        ins = pe.matmul(ps[FD * (f % 2):FD * (f % 2) + FD, f // 4, at:at + P],
                                        fqkv[:, kt, 2 * FW + f * FD:2 * FW + (f + 1) * FD], pT,
                                        start=kt == 0, stop=kt == b)
                    else:
                        ins = pe.matmul(ps[:, b, f * P:(f + 1) * P], pT, vtok[:, kt, f * P:(f + 1) * P],
                                        start=kt == 0, stop=kt == b)
                ins.then_inc(sem(f"att{w}_used"), 1)

            def dn_square():
                pe.wait_ge(sem("dn_sq"), 2)
                pe.wait_ge(sem("fox_lo"), 2)
                for i in range(16):
                    ins = pe.matmul(ps[:, 0, i:i + 1], dsq[:, P * i:P * (i + 1)], ones[:, 0:1], start=True, stop=True)
                ins.then_inc(sem("dn_ss"), 1)

            def dn_unit():
                for b in range(4):
                    pe.wait_ge(sem("dn_dd"), b // 2 + 1)
                    pe.matmul(ps[:, b, :], ones[:, :], dsq[:, 512 * b:512 * (b + 1)], start=True, stop=True)\
                      .then_inc(sem("dn_bc"), 1)

            def dn_cum():
                pe.wait_ge(sem("att0_PT"), 6)
                for t in range(TT):
                    for j, m in enumerate((tri64, blk64)):
                        at = (2 * t + j) * DH
                        ins = pe.matmul(ps[:, 6, at:at + DH], m[:, :], gg[:, t, :], start=True, stop=True)
                ins.then_inc(sem("dn_gc"), 1)

            def dn_tok(t):
                pe.wait_ge(sem("dn_qk"), 2)
                for j, c0 in enumerate((DH, 2 * DH)):
                    for h in range(DH):
                        ins = pe.transpose(ps[:, 2 * t + j, h * P:(h + 1) * P], dnT[:, c0 + h, t * P:(t + 1) * P],
                                           ident[:, :])
                    ins.then_inc(sem("dn_tokened"), 1)

            def dn_decay(t):
                pe.wait_ge(sem("dn_gb"), 2 * t + 2)
                if t == 0:
                    pe.wait_ge(sem("dn_gx"), 1)
                else:
                    pe.wait_ge(sem("dn_u"), t)
                    pe.wait_ge(sem("dn_kcT"), t)
                pe.matmul(by(ps[:, 7, :], DH), ones[:, :], XT, start=True, stop=True)
                pe.matmul(by(ps[:, 6, :], DH), ones[:, :], X, start=True, stop=True).then_inc(sem("dn_grow"), 1)

            def dn_kk(t):
                pe.wait_ge(sem("dn_tok"), 3 * t + 3)
                for j in range(2):
                    for h in range(DH):
                        cols_ = slice(t * P, (t + 1) * P)
                        ins = pe.matmul(ps[:, 2 * t + j, h * P:(h + 1) * P], dnT[:, DH + h, cols_],
                                        dnT[:, (DH if j == 0 else 0) + h, cols_], start=True, stop=True)
                    ins.then_inc(sem("dn_kked"), 1)

            def dn_x0(t):
                pe.wait_ge(sem("dn_x0"), t + 1)
                pe.wait_ge(sem("dn_edt"), t + 1)
                for h in range(DH):
                    ins = pe.transpose(ps[:, 6, h * P:(h + 1) * P], XT[:, h, :], ident[:, :])
                ins.then_inc(sem("dn_x0_turned"), 1)

            def dn_y(t, l):
                pe.wait_ge(sem("dn_B"), 5 * t + l)
                pe.wait_ge(sem("dn_X"), t + 1)
                if l > 1:
                    pe.wait_ge(sem("dn_X2"), 2 * (5 * t + l - 1))
                for h in range(DH):
                    ins = pe.matmul(ps[:, 7, h * P:(h + 1) * P], Bl[:, h, :], X[:, h, :], start=True, stop=True)
                ins.then_inc(sem("dn_BX"), 1)

            def dn_z(t, l):
                pe.wait_ge(sem("dn_Y"), 5 * t + l)
                for h in range(DH):
                    ins = pe.matmul(ps[:, 0, h * P:(h + 1) * P], Y[:, h, :], XT[:, h, :], start=True, stop=True)
                ins.then_inc(sem("dn_XBX"), 1)
                for h in range(DH):
                    ins = pe.matmul(ps[:, 1, h * P:(h + 1) * P], XT[:, h, :], Y[:, h, :], start=True, stop=True)
                ins.then_inc(sem("dn_XBX"), 1)

            def dn_sol(t):
                pe.wait_ge(sem("dn_X2"), 2 * (5 * t + 5))
                for h in range(DH):
                    ins = pe.matmul(ps[:, 6, h * P:(h + 1) * P], XT[:, h, :], vb[:, t, h, :], start=True, stop=True)
                ins.then_inc(sem("dn_solved"), 1)
                for h in range(DH):
                    ins = pe.matmul(ps[:, 7, h * P:(h + 1) * P], rhsk[:, t, h, :], XT[:, h, :], start=True, stop=True)
                ins.then_inc(sem("dn_solved"), 1)

            def dn_new(c):
                if c == 0:
                    return
                t, p0 = c // 2, CH * (c % 2)
                pe.wait_ge(sem("dn_S"), c)
                pe.wait_ge(sem("dn_kcT"), t + 1)
                for h in range(DH):
                    ins = pe.matmul(ps[p0:p0 + CH, 0, h * P:(h + 1) * P], kcT[:, h, c * CH:(c + 1) * CH], S[:, h, :],
                                    start=True, stop=True)
                ins.then_inc(sem("dn_kS"), 1)

            def dn_state(c):
                t, p0 = c // 2, CH * (c % 2)
                own_ = slice(p0, p0 + CH)
                pe.wait_ge(sem("dn_u"), t + 1)
                if c:
                    pe.wait_ge(sem("dn_vnew"), c)
                for h in range(DH):
                    out = ps[own_, 2 + t, h * P:(h + 1) * P]
                    if c:
                        pe.matmul(out, dnT[:, h, c * CH:(c + 1) * CH], S[:, h, :], start=True, stop=False)
                    ins = pe.matmul(out, qkT[own_, t, h, own_], vb[own_, t, h, :], start=c == 0, stop=True)
                ins.then_inc(sem("dn_o"), 1)
                if c < NCH - 1:
                    for h in range(DH):
                        ins = pe.matmul(ps[:, 1, h * P:(h + 1) * P], kdec[own_, t, h, :], vb[own_, t, h, :],
                                        start=True, stop=True)
                    ins.then_inc(sem("dn_supd"), 1)

            def dn_out(t):
                pe.wait_ge(sem("dn_onorm"), t + 1)
                pe.wait_ge(sem("dn_u"), TT)
                if t:
                    pe.wait_ge(sem("dn_y2"), t)
                for h in range(DH):
                    ins = pe.transpose(ps[:, 6, h * P:(h + 1) * P], rhsk[:, t, h, :], ident[:, :])
                ins.then_inc(sem("dn_oturned"), 1)

            def ple_p():
                pe.wait_ge(sem("p_in"), 16)
                for k in range(2):
                    for t in range(TT):
                        at = k * T + t * P
                        ins = pe.transpose(ps[:, 6, at:at + P], ptok[:, t, k * P:(k + 1) * P], ident[:, :])
                ins.then_inc(sem("p_turned"), 1)

            def pool_mm():
                pe.wait_ge(sem("pool_r"), 1)
                pe.wait_ge(sem("pw_in"), 32)
                for g in range(4):
                    ins = pe.matmul(ps[:, 2 + g // 2, (g % 2) * T:(g % 2 + 1) * T], pw[:, g, :], pr[:, g, :],
                                    start=True, stop=True)
                ins.then_inc(sem("pool_mmed"), 1)

            def ab_turn(b):
                pe.wait_ge(sem("ab_onorm"), b + 1)
                pe.wait_ge(sem("att1_PT"), 6)
                for h in range(4):
                    ins = pe.transpose(ps[:, 6 + b, h * P:(h + 1) * P], ob[:, b, h, :], ident[:, :])
                ins.then_inc(sem("ab_oturned"), 1)

            def gla_low():
                pe.wait_ge(sem("norm_lo"), 6 * KD)
                for k in range(KD):
                    for j, part in enumerate((hhi, hlo)):
                        ins = pe.matmul(ps[0:GR, 6, 0:T], wlow[:, k, :], part[:, k, :].bitcast(F32),
                                        start=k == 0 and j == 0, stop=k == KD - 1 and j == 1)
                ins.then_inc(sem("gla_lowed"), 1)

            def gla_gate():
                pe.wait_ge(sem("gla_gkT"), 1)
                pe.wait_ge(sem("gla_par"), 32)
                for t in range(TT):
                    pe.matmul(ps[:, t, :], ones[0:1, :], bgk[:, :], start=True, stop=False)
                    pe.matmul(ps[:, t, :], gkT[0:GR, t * P:(t + 1) * P], wgu[:, :], start=False, stop=True)\
                      .then_inc(sem("gla_gated"), 1)

            def gla_cum():
                pe.wait_ge(sem("gla_la"), 1)
                for b in range(2):
                    for h in (2 * b, 2 * b + 1):
                        for t in range(TT):
                            at = (h % 2) * T + t * P
                            ins = pe.matmul(ps[:, 6 + b, at:at + P], gla[:, t, h * P:(h + 1) * P], tri64[:, :],
                                            start=True, stop=True)
                    ins.then_inc(sem("gla_cummed"), 1)

            def gla_pairs(l):
                if l == 0:
                    pe.wait_ge(sem("gla_b"), 2)
                    for r in gla_qk_ready:
                        pe.wait_ge(*r)
                else:
                    pe.wait_ge(sem("gla_C"), l)
                    pe.wait_ge(sem("gla_took"), l)
                for t in range(TT):
                    for h in range(GH):
                        c_ = slice(t * P, (t + 1) * P)
                        lhs = Cl[:, h, c_] if l else gqT[:, GH + h, c_]
                        rhs = Cl[:, h, c_] if l else gqT[:, h, c_]
                        ins = pe.matmul(ps[:, 6 + t, h * P:(h + 1) * P], lhs, rhs, start=True, stop=True)
                    ins.then_inc(sem("gla_paired"), 1)

            def gla_ktok():
                pe.wait_ge(sem("gla_C"), 7)
                pe.wait_ge(sem("gla_took"), 7)
                for t in range(TT):
                    for h in range(GH):
                        ins = pe.transpose(ps[:, 6 + t, h * P:(h + 1) * P], Cl[:, h, t * P:(t + 1) * P], ident[:, :])
                    ins.then_inc(sem("gla_kturned"), 1)

            def gla_chunk(c):
                t, p0 = c // 2, CH * (c % 2)
                own_ = slice(p0, p0 + CH)
                if c == 0:
                    pe.wait_ge(*gla_v_ready[0])
                    pe.wait_ge(*gla_v_ready[1])
                    pe.wait_ge(sem("gla_kdt"), 2)
                else:
                    pe.wait_ge(sem("gla_S"), min(c, NCH - 1))
                for h in range(GH):
                    out = ps[own_, 2 * t + h // 2, (h % 2) * GV:(h % 2 + 1) * GV]
                    if c:
                        pe.matmul(out, gqT[:, h, c * CH:(c + 1) * CH], GS[:, h, :], start=True, stop=False)
                    ins = pe.matmul(out, attn[own_, t * GH + h, own_], vg[own_, t, h * GV:(h + 1) * GV],
                                    start=c == 0, stop=True)
                ins.then_inc(sem("gla_o"), 1)
                if c < NCH - 1:
                    for b in range(2):
                        for h in (2 * b, 2 * b + 1):
                            ins = pe.matmul(ps[:, 6 + b, (h % 2) * GV:(h % 2 + 1) * GV], kdt[own_, t * GH + h, :],
                                            vg[own_, t, h * GV:(h + 1) * GV], start=True, stop=True)
                        ins.then_inc(sem("gla_supd"), 1)

            def gla_turn(t):
                pe.wait_ge(sem("gla_onorm"), t + 1)
                if t:
                    pe.wait_ge(sem("gla_y"), 2 * t)
                else:
                    pe.wait_ge(sem("gla_S"), NCH - 1)
                for b in range(2):
                    for i in range(4):
                        at = (4 * b + i) * P
                        h, d0 = at // GV, at % GV
                        ins = pe.transpose(ps[:, 6 + b, i * P:(i + 1) * P], og[t][:, h, d0:d0 + P], ident[:, :])
                    ins.then_inc(sem("gla_oturned"), 1)

            ab_qk_ready = [took(s[2]) for s in order if s[0] == "ab_qk"][2:]
            ab_v_ready = [took(s[1] - 1) for s in order if s[0] == "ab_v"][0]
            gla_qk_ready = [took(s[2]) for s in order if s[0] == "gla_qk"][2:]
            v0 = [s[1] for s in order if s[0] == "gla_v"][0] - 3
            gla_v_ready = [(sem(g), v + 1) for g, v in units[v0]["free"]]
            parts = dict(mm=mm, norm=norm, params=params, small=small, fox_turn=fox_turn, fox_cum=fox_cum,
                         att_scores=att_scores, att_turn=att_turn, att_values=att_values,
                         dn_square=dn_square, dn_cum=dn_cum, dn_tok=dn_tok, dn_decay=dn_decay, dn_kk=dn_kk,
                         dn_x0=dn_x0, dn_y=dn_y, dn_z=dn_z, dn_sol=dn_sol, dn_new=dn_new, dn_state=dn_state,
                         dn_out=dn_out, dn_unit=dn_unit, ple_p=ple_p, pool_mm=pool_mm, ab_turn=ab_turn, gla_low=gla_low,
                         gla_gate=gla_gate, gla_cum=gla_cum, gla_pairs=gla_pairs, gla_ktok=gla_ktok,
                         gla_chunk=gla_chunk, gla_turn=gla_turn)
            pe.wait_ge(sem("constants"), made["ident"])
            for s in order:
                if s[0] == "params":
                    pe.wait_ge(sem("constants"), made["all"])
                if s[0] in parts:
                    parts[s[0]](*s[1:])


_INS = ["x", "p", "g_mix", "w_in", "b_fox_f", "fox_q_gain", "fox_k_gain", "sc_conv_w", "dn_conv_w", "dn_a_log",
        "dn_dt_bias", "dn_norm_gain", "w_branch", "w_o", "g_ffn", "w_up", "ffn_conv_w", "w_down", "g_ple",
        "w_ple_gate", "w_ple", "norm_mix_2", "norm_ffn_2", "norm_final_2", "ab_w_in_2", "ab_lambda_2",
        "ab_subln_2", "pool_w_2", "pool_scale_2", "ab_w_out_2", "gla_w_in_2", "gla_w_gk_up_2", "gla_b_gk_2",
        "gla_norm_2", "gla_w_out_2", "ffn_w1_2", "ffn_w2_2"]


def kernel(**inputs):
    import numpy as _np
    import concourse.bacc as _bacc
    from concourse import mybir as _mybir
    from concourse.bass_utils import run_bass_kernel_spmd as _run

    nc = _bacc.Bacc("TRN2", target_bir_lowering=False, num_devices=1)
    arrays, args = {}, {}
    for name in _INS:
        v = _np.ascontiguousarray(inputs[name])
        arrays[f"in_{name}"] = v
        args[name] = nc.dram_tensor(f"in_{name}", v.shape, _mybir.dt.from_np(v.dtype), kind="ExternalInput").ap()
    shape = inputs["x"].shape
    args["out"] = nc.dram_tensor("out_0", shape, _mybir.dt.from_np(_np.dtype("float32")), kind="ExternalOutput").ap()
    build(nc, args)
    r = _run(nc, [arrays], core_ids=[0])
    return r.results[0]["out_0"]
```

```python
import math
from contextlib import ExitStack

import concourse.bass as bass
from concourse import mybir

P = 128
ALU = mybir.AluOpType
ACT = mybir.ActivationFunctionType
AX = mybir.AxisListType
F32 = mybir.dt.float32
F32R = mybir.dt.float32r

UNIT = 2048
RAW = 3
SPLIT = 3
LEAD = 2
PAD = 4
BIG = 1.0e30
EPS = 1e-6


def build(nc, a):
    T, D = a["x"].shape[1:]
    TT = T // P
    KD = D // P
    FH, FD = a["b_fox_f"].shape[1], a["fox_q_gain"].shape[1]
    FW = FH * FD
    SW = a["sc_conv_w"].shape[2]
    DH, DV = a["dn_a_log"].shape[1], a["dn_norm_gain"].shape[1]
    DW = DH * DV
    NB = a["w_branch"].shape[1]
    BT = SW // P
    DFF = a["w_down"].shape[1]
    UPT = DFF // P
    PLE = a["w_ple"].shape[1]
    CH = 64
    NCH = T // CH
    LI = 0.8 - 0.6 * math.exp(0.0)
    GK = a["gla_w_gk_up_2"].shape[2]
    GR = a["gla_w_gk_up_2"].shape[1]
    GH, GV = a["gla_norm_2"].shape[1:]
    DFF2 = a["ffn_w2_2"].shape[1]
    POOLS = (2, 4, 8, 16)

    w_in = a["w_in"][0]
    o_fox, o_f = 0, 3 * FW
    o_sc = o_f + FH
    o_dn = o_sc + 3 * SW
    o_b = o_dn + 3 * DW
    o_a = o_b + DH
    o_z = o_a + DH
    o_gate = o_z + DW
    NSM = FH + 2 * DH

    units = []
    taken = {"c4": 0, "c5": 0, "g0": 0, "g1": 0}

    def rows_by_tile(w, r0, rows, c0, cols):
        return w[r0:r0 + rows, c0:c0 + cols].rearrange("(k p) n -> p k n", p=P)

    def add(kind, src, act, needs, groups, **more):
        free = [(g, taken[g]) for g in groups if more.get("first", True)]
        units.append(dict(kind=kind, src=src, act=act, needs=needs, free=free, **more))
        if more.get("last", True):
            for g in groups:
                taken[g] += 1
        return len(units) - 1

    def unit_c(w, c0, act, needs):
        before = [u for u in units if u["kind"] in "CB"]
        bank = 5 if before and before[-1]["kind"] == "C" and before[-1]["bank"] == 4 else 4
        return add("C", rows_by_tile(w, 0, D, c0, 256), act, needs, [f"c{bank}"], bank=bank)

    def unit_b(w, c0, act, k0, needs, bank, groups):
        return add("B", rows_by_tile(w, 0, 512, c0, 512), act, needs, groups, bank=bank, k0=k0)

    def units_t(w, c0, act, g, needs):
        return [add("T", rows_by_tile(w, 512 * h, 512, c0, 512), act, needs, [f"g{g}"], bank=2 * g,
                    k0=4 * h, first=h == 0, last=h == 1) for h in range(2)]

    def unit_d(w, r0, act, k0, first, last, needs, c0=0):
        return add("D", rows_by_tile(w, r0, 256, c0, D), act, needs, ["g0", "g1"], k0=k0, first=first,
                   last=last)

    def after(g):
        return (g, taken[g])

    order = []

    def step(*s):
        order.append(s)

    def product(u, *then):
        order.append(("mm", u, 0))
        flush()
        order.append(("mm", u, 1))
        held.extend(then)

    late = set()

    def last_product(u, add_, i):
        late.add(u)
        order.append(("mm", u, 0))
        flush()
        step(add_, u, 0)
        order.append(("mm", u, 1))
        step("norm_root", i, 0)
        step(add_, u, 1)
        step("norm_root", i, 1)
        step("split_late", u)
        if i < 7:
            step("norm", i, [("ple_added", t + 1) for t in range(TT)] if add_ == "ple_x" else
                 [(g, taken[g]) for g in ("g0", "g1")])
        else:
            step("final", [after("g0"), after("g1")])

    held = []

    def flush():
        order.extend(held)
        held.clear()

    def weave(fill, mixed):
        pending = []
        halves_ = [(u, part, then) for u, *then in fill for part in range(2)]
        scale, credit, done = len(halves_) / sum(n for n, _ in mixed), 0.0, 0

        def put(u, part, then):
            order.append(("mm", u, part))
            if part == 0 and (units[u]["kind"] == "B" or held and held[0][0] == "merge"):
                flush()
            elif part == 1 and then and then[0][0] == "merge":
                flush()
                order.append(then[0])
                held.extend(then[1:])
            elif part == 0:
                pending.append(1)
            else:
                if pending:
                    flush()
                    pending.clear()
                held.extend(then)

        if held:
            put(*halves_[0])
            flush()
            pending.clear()
            done = 1
        for n, s in mixed:
            credit += n * scale
            while credit > 0.999 and done < len(halves_):
                put(*halves_[done])
                done += 1
                credit -= 1
            order.append(s)
            if pending:
                flush()
                pending.clear()
        for h in halves_[done:]:
            put(*h)
        flush()

    def attention(which):
        for g in range(8):
            if 1 <= g < 7:
                yield (1, ("att_norm", which, g - 1))
            if g < 6:
                yield (1.0 if g else 1, ("att_scores", which, g))
            if 1 <= g < 7:
                yield (1, ("att_turn", which, g - 1))
            if g >= 2:
                yield (1.5 if g == 7 else 0, ("att_values", which, g - 2))

    step("norm_root", 0, 0)
    step("norm_root", 0, 1)
    step("norm", 0, [("x_in0", 16), ("x_in1", 16)])
    h_ready = [("norm_lo", KD)]
    for j in range(3):
        us = units_t(w_in, o_fox + 512 * j, "h", j % 2, h_ready)
        product(us[0])
        product(us[1], ("fox_qkv", j, us[-1], after(f"g{j % 2}")))
        if j == 0:
            step("load_params")
    flush()
    step("params")
    fill = []
    convs = {}
    for e in range(3 * DW // 256):
        u = unit_c(w_in, o_dn + 256 * e, "h", h_ready)
        convs["dn", e] = len(convs)
        fill.append((u, ("dn", e, convs["dn", e], u)))
    for e in range(BT // 2):
        for part in (1, 2, 0):
            u = unit_c(w_in, o_sc + part * SW + 256 * e, "h", h_ready)
            if part == 1:
                convs["sc", e] = len(convs)
            fill.append((u, ("sc", e, part, convs["sc", e], u)))
    mixed = [(0, ("small",)), (0, ("small_turn",)),
             (0.5, ("fox_norm",)), (4, ("fox_turn", 0)), (0.5, ("fox_turn", 1)), (1, ("fox_cum", 0)),
             (0, ("fox_cum", 1))]
    mixed += list(attention(0)) + [(0, ("dn_silu",)), (0.5, ("fox_out",))]
    weave(fill, mixed)
    def branch(n, g, need):
        bank, groups = (4, ["c4", "c5"]) if n < NB - 1 else (2 * g, [f"g{g}"])
        u = unit_b(a["w_branch"][0][n], 512 * g, "a", BT * n, [(need, 2)], bank, groups)
        return (u, ("merge", n, g, 0, u), ("merge", n, g, 1, u))

    fill = []
    for e in range(DW // 256):
        u = unit_c(w_in, o_z + 256 * e, "h", h_ready)
        fill.append((u, ("z", e, u)))
    products = {1: (0, 0), 3: (0, 1), 5: (1, 0), 8: (1, 1)}
    for e in range(NB * D // 256):
        if e == 8:
            early = len(fill)
        u = unit_c(w_in, o_gate + 256 * e, "h", h_ready)
        fill.append((u, ("gate", e, u)))
        if e in products:
            fill.append(branch(*products[e], ("fox_lo", "sc_lo")[products[e][0]]))
    mixed = [(0, ("dn_square",)), (0, ("dn_cum",)), (2, ("dn_unit",)), (1.5, ("dn_scale",))]
    for t in range(TT):
        mixed += [(4 if t == 0 else 1, ("dn_tok", t)), (1, ("dn_decay", t)), (1, ("dn_kk", t)), (2.5, ("dn_x0", t))]
    for l in range(1, 6):
        mixed += [(0.5, ("dn_y", 0, l)), (0, ("dn_y", 1, l)), (0.5, ("dn_z", 0, l)), (0, ("dn_z", 1, l))]
    mixed += [(1, ("dn_sol", 0)), (0, ("dn_sol", 1))]
    weave(fill[:early], mixed)
    mixed = []
    for c in range(NCH):
        mixed += [(1, ("dn_new", c)), (1, ("dn_state", c))]
        if c % 2:
            mixed += [(0, ("dn_sum", c // 2))]
    mixed += [(0, ("dn_out", 0)), (2, ("dn_out", 1))]
    weave(fill[early:], mixed)
    for g in range(2):
        u, *then = branch(NB - 1, g, "dn_lo")
        product(u)
        order.append(then[0])
        held.append(then[1])
        if g:
            held.append(("merge_lo", 1))
        held.append(("merge_lo", 2 * g))
    flush()
    step("merge_lo", 3)
    us = [unit_d(a["w_o"][0], 256 * i, "h", 2 * i, i == 0, i == 3, [("merged_lo", i + 1)]) for i in range(4)]
    for u in us[:3]:
        product(u)
    last_product(us[3], "resid", 1)

    downs = {}
    NF = UPT // 2
    for c in range(NF + 1):
        if c < NF:
            for part in range(2):
                u = unit_c(a["w_up"][0], DFF * part + 256 * c, "h", [("norm_lo", 2 * KD)])
                product(u, ("up", c, part, u))
            if c == NF - 1:
                flush()
            if c in (1, 3):
                step("ple_load" if c == 1 else "ple_p")
        if c == NF - 1:
            held.append(("glu", c, downs.get(c - 2)))
        if c >= 1:
            downs[c - 1] = unit_d(a["w_down"][0], 256 * (c - 1), "a", 2 * ((c - 1) % 2), c == 1, c == NF,
                                  [("glu_lo", c)])
            if c < NF:
                product(downs[c - 1])
        if c < NF - 1:
            held.append(("glu", c, downs.get(c - 2)))
            if c == 0:
                flush()
    last_product(downs[NF - 1], "resid", 2)

    us = [unit_d(a["w_ple_gate"][0], 256 * i, "h", 2 * i, i == 0, i == 3, [("norm_lo", 3 * KD)]) for i in range(4)]
    for u in us:
        product(u)
    step("ple_gate", us[3])
    last_product(unit_d(a["w_ple"][0], 0, "a", 4, True, True, [("ple_lo", 1)]), "ple_x", 3)

    h_ready = [("norm_lo", 4 * KD)]
    w_ab = a["ab_w_in_2"][0]
    for e in range(4):
        u = unit_c(w_ab, 256 * e, "h", h_ready)
        product(u, ("ab_qk", e, u))
    step("lam")
    us = units_t(w_ab, 1024, "h", 0, h_ready)
    fill = [(us[0],), (us[1], ("ab_v", us[1]))]
    for e in range(2):
        u = unit_c(w_ab, 1536 + 256 * e, "h", h_ready)
        fill.append((u, ("pool_u", e, u)))
    mixed = list(attention(1))
    flush()
    weave(fill[:2], mixed[:7])
    weave(fill[2:], mixed[7:])
    for b in range(TT):
        step("ab_sum", b)
    step("ab_turn", 0)
    step("ab_turn", 1)
    us = [unit_d(a["ab_w_out_2"][0], 256 * i, "a", 2 * i, i == 0, i == 3, [("ab_lo", 2) if i < 2 else ("pool_lo", 1)])
          for i in range(4)]
    product(us[0])
    step("pool_mm")
    product(us[1])
    product(us[2])
    last_product(us[3], "resid", 4)

    def squared_relu_part(i, norm):
        n, rows_of = DFF2 // 256, {}
        for c in range(n + 1):
            if c < n:
                u = unit_c(a["ffn_w1_2"][i], 256 * c, "h", [("norm_lo", (norm + 1) * KD)])
                product(u, ("relu2", i * n + c, u))
                if c == n - 1:
                    flush()
            if c == n - 1:
                held.append(("relu2_split", i * n + c, c, rows_of.get(c - 2)))
            if c >= 1:
                rows_of[c - 1] = unit_d(a["ffn_w2_2"][i], 256 * (c - 1), "a", 2 * ((c - 1) % 2), c == 1,
                                        c == n, [("relu2_lo", i * n + c)])
                if c < n:
                    product(rows_of[c - 1])
            if c < n - 1:
                held.append(("relu2_split", i * n + c, c, rows_of.get(c - 2)))
                if c == 0:
                    flush()
        last_product(rows_of[n - 1], "resid", norm + 1)

    squared_relu_part(0, 4)

    h_ready = [("norm_lo", 6 * KD)]
    w_gla = a["gla_w_in_2"][0]
    fill = []
    for e in range(2 * GK // 256):
        u = unit_c(w_gla, 256 * e, "h", h_ready)
        fill.append((u, ("gla_qk", e, u)))
    weave(fill, [(1, ("gla_low",)), (3, ("gla_gate",)), (4, ("gla_cum",))])
    fill = []
    for i in range(4):
        u = unit_d(w_gla, 256 * i, "h", 2 * i, i == 0, i == 3, h_ready, c0=2 * GK)
        fill.append((u, ("gla_v", u)) if i == 3 else (u,))
    for e in range(2):
        u = unit_c(w_gla, 2 * GK + D + 256 * e, "h", h_ready)
        fill.append((u, ("gla_g", e, u)))
    mixed = [(2, ("gla_pairs", 0))]
    for l in range(6):
        mixed += [(0, ("gla_arg", l)), (2, ("gla_mask", l)), (0, ("gla_mul", l)), (1, ("gla_pairs", l + 1))]
    mixed += [(0, ("gla_decay",)), (1.5, ("gla_mask", 6)), (0, ("gla_k",)), (1, ("gla_ktok",))]
    weave(fill, mixed)
    fill = []
    for e in range(2, D // 256):
        u = unit_c(w_gla, 2 * GK + D + 256 * e, "h", h_ready)
        fill.append((u, ("gla_g", e, u)))
    weave(fill, [(0, ("gla_chunk", 0)), (1, ("gla_chunk", 1)), (0, ("gla_sum", 0)), (1.5, ("gla_chunk", 2)),
                 (1, ("gla_chunk", 3)), (0.5, ("gla_sum", 1))])
    us = [unit_d(a["gla_w_out_2"][0], 256 * i, "a", 2 * i, i == 0, i == 3, [("gla_lo", 1 + i // 2)])
          for i in range(4)]
    step("gla_turn", 0)
    step("gla_turn", 1)
    step("mm", us[0], 0)
    step("mm", us[0], 1)
    for i, u in enumerate(us):
        units[u]["needs_last"] = [("gla_lo", 3 + i // 2)]
        if 0 < i < 3:
            product(u)
    last_product(us[3], "resid", 6)
    squared_relu_part(1, 6)
    fresh = {}
    for s, nxt in ((i, order[i:]) for i, s in enumerate(order) if s[0] == "norm"):
        fresh[next(n[1] for n in nxt if n[0] == "mm")] = order[s][1]
    turn_banks = {i: (4, 5, 6, 7) if units[u]["kind"] in "TD" else (6, 7, 0, 1) for u, i in fresh.items()}
    NU = len(units)

    ctx = ExitStack()
    with ctx:
        def sb(name, shape, dt=F32):
            return ctx.enter_context(nc.sbuf_tensor(name, shape, dt))

        sems = {}

        def sem(name):
            if name not in sems:
                sems[name] = ctx.enter_context(nc.semaphore(name))
            return sems[name]

        raw = sb("raw", [P, RAW, UNIT])
        whi = sb("whi", [P, SPLIT, UNIT], F32R)
        wlo = sb("wlo", [P, SPLIT, UNIT], F32R)
        hhi = sb("hhi", [P, KD, T], F32R)
        hlo = sb("hlo", [P, KD, T], F32R)
        ahi = sb("ahi", [P, 3 * BT, T], F32R)
        alo = sb("alo", [P, 3 * BT, T], F32R)
        xs = sb("xs", [P, TT, D])
        x = sb("xres", [P, TT, D])
        ps = ctx.enter_context(nc.psum_tensor("ps", [P, 8, 512], F32))

        ident = sb("ident", [P, P])
        ones = sb("ones", [P, P])
        tri = sb("tri", [P, P])
        tri64 = sb("tri64", [P, P])
        blk64 = sb("blk64", [P, P])
        lev = sb("lev", [P, 6, P])
        cneg = sb("cneg", [P, P])
        dneg = sb("dneg", [P, P])
        inv = sb("inv", [P, 4, 16])
        colp = sb("colp", [P, 3, P])
        bias16 = sb("bias16", [P, NSM])
        alog = sb("alog", [P, DH])
        SMALL = KD * (NSM + GR)
        smhi = sb("smhi", [P, SMALL], F32R)
        smlo = sb("smlo", [P, SMALL], F32R)
        ss = sb("ss", [P, TT, 16])
        zz = sb("zz", [P, 4, TT, NSM])
        eps = sb("eps", [P, 1])
        warm = sb("warm", [P, 1])
        gcol0 = sb("gcol0", [P, KD])
        beta = sb("beta", [P, TT, DH])
        gg = sb("gg", [P, TT, DH])
        gx = sb("gx", [P, TT, 2, DH])
        gcol = sb("gcol", [P, TT, DH])
        gt = sb("gt", [P, TT, DH, 2])
        nmax = sb("nmax", [P, 2, 4])
        rsum = sb("rsum", [P, 2, 4])
        lamw = sb("lamw", [P, 8])
        conv = sb("conv", [P, 2, 2, PAD + T])
        cy = sb("cy", [P, 2, 2, T])
        diag = cy[:, 0, 0, :].rearrange("p (t n) -> p t n", t=TT)
        ARENA = nc.sbuf_bytes_remaining // 4 - 16
        arena = sb("arena", [P, ARENA])

        def view(base, n):
            assert base + n <= ARENA, (base, n, ARENA)
            return arena[:, base:base + n]

        def tiles(ap):
            return ap.rearrange("p (c t) -> p c t", t=T)

        def by(ap, n):
            return ap.rearrange("p (h i) -> p h i", h=n)

        rows = view(0, 3 * P).rearrange("p (b n) -> p b n", b=3)
        grow = view(3 * P, P)[0:KD, :]
        smT = view(12288, T)[0:NSM, :]
        smraw = view(4 * P, SMALL)
        wsm, wlow = [[m[:, at:at + KD * n].rearrange("p (k n) -> p k n", k=KD) for m in (smraw, smhi[:, :], smlo[:, :])]
                     for at, n in ((0, NSM), (KD * NSM, GR))]
        dnT = tiles(view(0, 3072))
        kcT = dnT[:, 2 * DH:3 * DH, :]
        gates = tiles(view(3072, 6144))
        fqkv = view(3072, 3072).rearrange("p (t n) -> p t n", t=TT)
        fT = tiles(view(6144, 2048))
        S2 = view(8192, 1024).rearrange("p (b n) -> p b n", b=2)
        PT2 = view(9216, 1024).rearrange("p (b n) -> p b n", b=2)
        fcum = view(10240, 2048).rearrange("p (t h j) -> p t h j", t=TT, h=FH)
        fbias = xs[:, :, :].rearrange("p t n -> p (t n)").rearrange("p (h j) -> p h j", h=FH)
        dsq = view(10240, 2048)
        kdec, rhsk, vb, qkT = [view(9216 + 1024 * i, 1024).rearrange("p (t h d) -> p t h d", t=TT, h=DH)
                               for i in range(4)]
        late_gates = [view(7168 + 512 * i, 512) for i in range(4)]
        own_ = [view(13312 + 512 * i, 512) for i in range(4)]
        DT = by(own_[3], DH)
        flat = [cy[:, i, :, :].rearrange("p a t -> p (a t)") for i in range(2)]
        X, XT, LT, Bl, Y = [[by(one, DH), by(two, DH)] for one, two in
                            zip(own_[0:3] + flat, late_gates + [own_[3]])]
        zT = xs[:, 0, :].rearrange("p (c t) -> p c t", t=T)
        S = by(xs[:, 1, 0:512], DH)
        EG = [by(xs[:, 1, 512:1024], DH), S]
        mg = gates[:, 0:KD, :]
        sg = view(0, 2048).rearrange("p (t n) -> p t n", t=TT)
        ptok = view(2048, 512).rearrange("p (t n) -> p t n", t=TT)
        qkf = tiles(view(0, 2048))
        vtok = view(2048, 1024).rearrange("p (t n) -> p t n", t=TT)
        S2b = view(3072, 1024).rearrange("p (b n) -> p b n", b=2)
        PT2b = view(4096, 1024).rearrange("p (b n) -> p b n", b=2)
        ob = view(5120, 1024).rearrange("p (t h d) -> p t h d", t=TT, h=4)
        oy = by(view(6144, 512), 4)
        W0 = 16
        pu, p1, p2, p3, p4 = [view(6656 + 1088 * i, 4 * (W0 + T)).rearrange("p (g t) -> p g t", g=4)
                              for i in range(5)]
        pr = tiles(view(12096, 1024))
        pw = by(view(13120, 512), 4)
        pfix = view(13632, 64).rearrange("p (g t) -> p g t", g=4)
        lamr = by(view(13696, 4 * FD), 4)
        gqT = tiles(view(0, 2048))
        gla = view(2048, 1024).rearrange("p (t n) -> p t n", t=TT)
        gmin = view(3072, 1024).rearrange("p (t n) -> p t n", t=TT)
        bcum = tiles(view(4096, 1024))
        E1 = tiles(view(2048, 1024))
        Cl = tiles(view(3072, 1024))
        attn = view(5120, 1024).rearrange("p (g i) -> p g i", g=TT * GH)
        atmp = view(6144, 1024).rearrange("p (g i) -> p g i", g=TT * GH)
        kdt = view(7168, 1024).rearrange("p (g i) -> p g i", g=TT * GH)
        EB = tiles(view(8192, 1024))
        vg = view(9216, 2048).rearrange("p (t n) -> p t n", t=TT)
        sgT = tiles(view(11264, 2048))
        GS = view(13312, 1024).rearrange("p (h d) -> p h d", h=GH)
        gkT = view(14336, 256)
        wgu = view(14592, GK)[0:GR, :]
        bgk = view(9216, GK)[0:1, :]
        og = [by(view(at, 1024), GH) for at in (2048, 4096)]
        gy = view(6144, 1024).rearrange("p (c t) -> p c t", c=KD)
        nfin = view(0, D)

        def as_rows(ap, s):
            return ap.rearrange(s, p=P)

        sources, place = [], {}

        def param(name, src, block, n):
            at = sum(k for b, _, k in sources if b == block)
            place[name] = (block, at)
            sources.append((block, src, n))

        param("g_ffn", as_rows(a["g_ffn"][0], "(k p) -> k p"), 0, KD)
        param("g_ple", as_rows(a["g_ple"][0], "(k p) -> k p"), 0, KD)
        param("norm_mix", as_rows(a["norm_mix_2"], "i (k p) -> (i k) p"), 0, 2 * KD)
        param("norm_ffn", as_rows(a["norm_ffn_2"], "i (k p) -> (i k) p"), 0, 2 * KD)
        param("gla_norm", as_rows(a["gla_norm_2"][0], "h (k p) -> (h k) p"), 0, KD)
        param("fox_gain", [a["fox_q_gain"], a["fox_k_gain"]], 0, 2)
        param("dn_gain", a["dn_norm_gain"], 0, 1)
        param("subln", a["ab_subln_2"], 0, 1)
        param("pool_scale", as_rows(a["pool_scale_2"][0], "(k p) -> k p"), 0, 4)
        param("sc_conv", as_rows(a["sc_conv_w"][0], "j (k p) -> (j k) p"), 0, 3 * BT)
        param("dn_conv", as_rows(a["dn_conv_w"][0], "j (k p) -> (j k) p"), 1, 4 * 3 * BT)
        for j in range(3):
            param(f"ffn_conv{j}", as_rows(a["ffn_conv_w"][0][j:j + 1], "j (k p) -> (j k) p"), (1, 2, 2)[j], 2 * UPT)

        def col(name, i):
            block, at = place[name]
            return colp[:, block, at + i:at + i + 1]

        def gain(i, k):
            return gcol0[:, k:k + 1] if i == 0 else col(gains[i][0], gains[i][1] + k)

        def cols(name, n, width):
            block, at = place[name]
            return colp[:, block, at:at + n].unsqueeze(2).to_broadcast([P, n, width])

        gains = [None, ("g_ffn", 0), ("g_ple", 0), ("norm_mix", 0), ("norm_ffn", 0),
                 ("norm_mix", KD), ("norm_ffn", KD)]
        n_rows, n_par = len(sources) + 3, 6
        groups = [(1, (2 * g, 2 * g + 1)) for g in range(4)] + [(0, tuple(range(4 * g, 4 * g + 4))) for g in range(2)]

        def turned(which, g):
            b, maps = groups[g]
            w = P * (b + 1)
            if which == 0:
                return [(i * w + kt * P, f, kt) for i, f in enumerate(maps) for kt in range(b + 1)]
            return [(i * w + kt * P, f // 2, kt) for i, f in enumerate(maps) if f % 2 == 0 for kt in range(b + 1)]

        att = [dict(q=fT[:, 0:4, :], k=fT[:, 4:8, :], S=S2, PT=PT2), dict(q=qkf[:, 0:4, :], k=qkf[:, 4:8, :], S=S2b, PT=PT2b)]

        def took(u):
            g, n = units[u]["free"][0]
            return sem(g), n + 1

        for name in ("params_in", "constants", "unit_done", "hi_done", "lo_done"):
            sem(name)
        block = ctx.enter_context(nc.Block())

        @block.sync
        def _(sp):
            for t in range(TT):
                sp.dma_start(x[:, t, :], a["x"][0][t * P:(t + 1) * P, :]).then_inc(sem(f"x_in{t}"), 16)
            for u in range(NU):
                if u >= RAW:
                    sp.wait_ge(sem("lo_done"), u - RAW + 1)
                src = units[u]["src"]
                dst = raw[:, u % RAW, :].rearrange("p (k n) -> p k n", k=src.shape[1])
                sp.dma_start(dst, src).then_inc(sem(f"raw_in{u % RAW}"), 16)
            for t in range(TT):
                sp.wait_ge(sem("final_x"), t + 1)
                sp.dma_start(a["out"][0][t * P:(t + 1) * P, :], xs[:, t, :]).then_inc(sem("stored"), 16)
            sp.wait_ge(sem("stored"), 16 * TT)

        made = {}

        @block.gpsimd
        def _(pool):
            n = [0]

            def then(ins):
                n[0] += 1
                ins.then_inc(sem("constants"), 1)
                pool.wait_ge(sem("constants"), n[0])

            then(pool.memset(ident[:, :], 0.0))
            then(pool.affine_select(out=ident[:, :], in_=ident[:, :], compare_op=ALU.not_equal, fill=1.0,
                                    base=0, pattern=[[-1, P]], channel_multiplier=1))
            then(pool.memset(warm[:, :], 0.0))
            then(pool.memset(eps[:, :], EPS))
            made["ident"] = n[0]
            then(pool.memset(rows[:, :, :], 0.0))
            at = {}
            for b, src, k in sources:
                r = at.get(b, 0)
                if isinstance(src, list):
                    for i, j in ((0, 0), (0, 1), (1, 0), (1, 1)):
                        pool.dma_start(rows[r + i:r + i + 1, b, FD * j:FD * (j + 1)], src[i])\
                           .then_inc(sem("rows_in"), 16)
                else:
                    pool.dma_start(rows[r:r + k, b, :], src).then_inc(sem("rows_in"), 16)
                at[b] = r + k
            for t_, v in ((ones, 1.0), (tri, 1.0), (blk64, 0.0), (cneg, 0.0), (dneg, 0.0)):
                then(pool.memset(t_[:, :], v))
            then(pool.memset(lev[:, :, :], 0.0))
            then(pool.memset(conv[:, :, :, :], 0.0))
            then(pool.affine_select(out=tri[:, :], in_=tri[:, :], compare_op=ALU.is_ge, fill=0.0,
                                    base=0, pattern=[[1, P]], channel_multiplier=-1))
            then(pool.affine_select(out=cneg[:, :], in_=cneg[:, :], compare_op=ALU.is_ge, fill=-BIG,
                                    base=0, pattern=[[-1, P]], channel_multiplier=1))
            then(pool.memset(dneg[0:CH, CH:P], -BIG))
            then(pool.memset(blk64[0:CH, 0:CH], 1.0))
            then(pool.memset(blk64[CH:P, CH:P], 1.0))
            then(pool.tensor_copy(tri64[:, :], tri[:, :]))
            then(pool.memset(tri64[0:CH, CH:P], 0.0))
            for l in range(6):
                s = 1 << l
                right = lev[:, l, :].rearrange("p (n two s) -> p n two s", two=2, s=s)[:, :, 1, :]
                then(pool.memset(right, 1.0))
                nb = P // (2 * s)
                then(pool.affine_select(out=right, in_=right, compare_op=ALU.is_ge, fill=0.0, base=0,
                                        pattern=[[-2 * s, nb], [0, s]], channel_multiplier=1))
                then(pool.affine_select(out=right, in_=right, compare_op=ALU.is_ge, fill=0.0, base=s - 1,
                                        pattern=[[2 * s, nb], [0, s]], channel_multiplier=-1))
            for g, w in enumerate(POOLS):
                then(pool.memset(inv[:, g, :], 1.0 / w))
                for i in range(w - 1):
                    then(pool.memset(inv[:, g, i:i + 1], 1.0 / (i + 1)))
            made["all"] = n[0]

            for ready in [took(s[2]) for s in order if s[0] == "pool_u"]:
                pool.wait_ge(*ready)
            E_ = W0 + T
            src, sums = pu, (p1, p2, p3, p4)

            def chained(ins):
                n[0] += 1
                ins.then_inc(sem("constants"), 1)
                pool.wait_ge(sem("constants"), n[0])

            chained(pool.memset(pu[:, :, 0:W0], 0.0))
            for l, dst in enumerate(sums):
                s = 1 << l
                at = 2 * s - 1
                chained(pool.tensor_tensor(dst[:, l:4, at:E_], src[:, l:4, at:E_], src[:, l:4, at - s:E_ - s], ALU.add))
                src = dst
            for g, w in enumerate(POOLS):
                pool.tensor_tensor(pfix[:, g, :], sums[g][:, g, W0:W0 + 16], inv[:, g, :], ALU.mult)
                chained(pool.tensor_scalar(pr[:, g, 16:T], sums[g][:, g, W0 + 16:E_], 1.0 / w, None, ALU.mult))
            pool.tensor_tensor(pr[:, :, 16:T], pr[:, :, 16:T], pu[:, :, W0 + 16:E_], ALU.subtract)
            pool.tensor_tensor(pr[:, :, 0:16], pfix, pu[:, :, W0:W0 + 16], ALU.subtract).then_inc(sem("pool_r"), 1)

        @block.scalar
        def _(act):
            n = [0]

            def link(ins):
                n[0] += 1
                ins.then_inc(sem("act_own"), 1)
                act.wait_ge(sem("act_own"), n[0])

            roots = [0]

            def root(ap, scale):
                roots[0] += 1
                act.wait_ge(sem("root_in"), roots[0])
                act.activation(ap, ap, ACT.Sqrt, scale=scale, bias=eps[:, :]).then_inc(sem("root_out"), 1)

            def square_sums(parts_):
                for junk, src, total in parts_:
                    ins = act.activation(junk, src, ACT.Square, accum_out=total)
                link(ins)

            def split_high(u):
                act.wait_ge(sem(f"raw_in{u % RAW}"), 16 * (u // RAW + 1))
                if u >= SPLIT:
                    act.wait_ge(sem("unit_done"), u - SPLIT + 1)
                act.activation(whi[:, u % SPLIT, :], raw[:, u % RAW, :], ACT.Copy).then_inc(sem("hi_done"), 1)

            def load_params():
                act.dma_start(bias16[:, 0:FH], a["b_fox_f"][0].partition_broadcast(P)).then_inc(sem("params_in"), 16)
                act.dma_start(bias16[:, FH + DH:NSM], a["dn_dt_bias"][0].partition_broadcast(P))\
                   .then_inc(sem("params_in"), 16)
                act.dma_start(alog[:, :], a["dn_a_log"][0].partition_broadcast(P)).then_inc(sem("params_in"), 16)
                act.dma_start(wlow[0], rows_by_tile(a["gla_w_in_2"][0], 0, D, 2 * GK + 2 * D, GR))\
                   .then_inc(sem("params_in"), 16)
                act.dma_start(wsm[0][:, :, 0:FH], rows_by_tile(w_in, 0, D, o_f, FH)).then_inc(sem("params_in"), 16)
                act.dma_start(wsm[0][:, :, FH:NSM], rows_by_tile(w_in, 0, D, o_b, 2 * DH)).then_inc(sem("params_in"), 16)

            def norm(i, waits):
                link(act.activation(warm[:, :], warm[:, :], ACT.Sqrt))
                for t in range(TT):
                    act.wait_ge(sem(waits[t][0]), waits[t][1])
                    square_sums([(xs[:, t, :], x[:, t, :], ss[:, t, 0:1])])
                    act.activation(ss[:, t, 0:1], ss[:, t, 0:1], ACT.Sqrt, scale=1.0 / D, bias=eps[:, :])\
                       .then_inc(sem("root_out"), 1)
                if i == 0:
                    split_high(0)
                for k in range(KD):
                    act.wait_ge(sem("norm_turned"), KD // 2 * i + k // 2 + 1)
                    if i == 0 and k == 0:
                        act.wait_ge(sem("gcol0_done"), 1)
                    act.activation(hhi[:, k, :], ps[:, turn_banks[i][k // 2], (k % 2) * T:(k % 2 + 1) * T], ACT.Copy,
                                   scale=gain(i, k)).then_inc(sem("norm_hi"), 1)
                if i == 0:
                    split_high(1)
                if i == 4:
                    act.dma_start(bgk, a["gla_b_gk_2"]).then_inc(sem("gla_par"), 16)
                    act.dma_start(wgu, a["gla_w_gk_up_2"][0]).then_inc(sem("gla_par"), 16)

            def params():
                act.wait_ge(sem("constants"), made["all"])
                act.wait_ge(sem("params_in"), 16 * n_par)
                act.activation(smhi[:, :], smraw, ACT.Copy).then_inc(sem("small_hi"), 1)
                act.wait_ge(sem("colp_done"), 3)

            def small():
                act.wait_ge(sem("small_done"), 1)
                act.activation(smT, ps[0:NSM, 6, 0:T], ACT.Copy).then_inc(sem("small_exp"), 1)

            def small_turn():
                act.wait_ge(sem("small_abs"), 1)
                act.activation(zz[:, 1], zz[:, 1], ACT.Exp, scale=-1.0).then_inc(sem("small_exp"), 1)
                act.activation(alog[:, :], alog[:, :], ACT.Exp).then_inc(sem("small_exp"), 1)
                act.wait_ge(sem("small_exp"), 3)
                act.activation(zz[:, 2], zz[:, 1], ACT.Ln, bias=1.0).then_inc(sem("small_exp"), 1)
                act.wait_ge(sem("small_lsg"), 1)
                act.activation(beta[:, :, :], zz[:, 3, :, FH:FH + DH], ACT.Exp).then_inc(sem("small_exp"), 1)

            def fox_qkv(j, u, freed):
                act.wait_ge(sem("unit_done"), u + 1)
                g = j % 2
                for t in range(TT):
                    ins = act.activation(fqkv[:, t, 512 * j:512 * (j + 1)], ps[:, 2 * g + t, :], ACT.Copy)
                ins.then_inc(sem(f"g{g}"), 1)

            def sc(e, part, j, u):
                act.wait_ge(sem("unit_done"), u + 1)
                out = cy[:, e % 2, :, :]
                if part == 1:
                    act.activation(out, tiles(ps[:, units[u]["bank"], :]), ACT.Copy).then_inc(took(u)[0], 1)
                if part == 0:
                    act.wait_ge(*took(u))
                    act.activation(ahi[:, BT + 2 * e:BT + 2 * e + 2, :], out, ACT.Copy).then_inc(sem("sc_hi"), 1)

            def conv_copy(j, u):
                act.wait_ge(sem("unit_done"), u + 1)
                if j >= 2:
                    act.wait_ge(sem("conv_read"), j - 1)
                act.activation(conv[:, j % 2, :, PAD:PAD + T], tiles(ps[:, units[u]["bank"], :]), ACT.Copy)\
                   .then_inc(took(u)[0], 1)

            def dn(e, j, u):
                conv_copy(j, u)

            def fox_turn(t):
                for b in range(2):
                    act.wait_ge(sem("fox_turned"), 2 * t + b + 1)
                    act.activation(fT[:, 4 * b:4 * b + 4, t * P:(t + 1) * P], by(ps[:, 2 * t + b, :], 4), ACT.Copy,
                                   scale=col("fox_gain", b)).then_inc(sem("fox_T"), 1)

            def fox_cum(t):
                for b in range(2):
                    act.wait_ge(sem("fox_cummed"), 2 * t + b + 1)
                    act.activation(fbias[:, 4 * b:4 * b + 4, t * P:(t + 1) * P], by(ps[:, 2 * t + b, :], 4), ACT.Copy,
                                   scale=-1.0).then_inc(sem("fox_bias"), 1)

            def att_scores(w, g):
                b, maps = groups[g]
                act.wait_ge(sem(f"att{w}_max"), g + 1)
                width = P * (b + 1)
                for i in range(len(maps)):
                    part = att[w]["S"][:, g % 2, i * width:(i + 1) * width]
                    ins = act.activation(part, part, ACT.Exp, bias=nmax[:, g % 2, i:i + 1],
                                         accum_out=rsum[:, g % 2, i:i + 1])
                    ins.then_inc(sem(f"att{w}_exp"), 1)

            def att_turn(w, g):
                act.wait_ge(sem(f"att{w}_turned"), g + 1)
                if g >= 2:
                    act.wait_ge(sem(f"att{w}_used"), g - 1)
                k = len(turned(w, g)) * P
                act.activation(att[w]["PT"][:, g % 2, 0:k], ps[:, 6 + g % 2, 0:k], ACT.Copy)\
                   .then_inc(sem(f"att{w}_PT"), 1)

            def fox_out():
                act.wait_ge(sem("att0_used"), 6)
                for b in range(2):
                    act.activation(ahi[:, 2 * b:2 * b + 2, :], tiles(ps[:, b, :]), ACT.Copy)\
                       .then_inc(sem("fox_hi"), 1)

            def z(e, u):
                act.wait_ge(sem("unit_done"), u + 1)
                act.activation(zT[:, 2 * e:2 * e + 2, :], tiles(ps[:, units[u]["bank"], :]), ACT.Silu)\
                   .then_inc(took(u)[0], 1)

            def gate(e, u):
                act.wait_ge(sem("unit_done"), u + 1)
                act.activation(gates[:, 2 * e:2 * e + 2, :], tiles(ps[:, units[u]["bank"], :]), ACT.Sigmoid)\
                   .then_inc(took(u)[0], 1)

            def dn_cum():
                act.wait_ge(sem("dn_gx"), 1)
                act.activation(gx[:, :, :, :], gx[:, :, :, :], ACT.Exp).then_inc(sem("dn_egx"), 1)

            def dn_decay(t):
                act.wait_ge(sem("dn_grow"), t + 1)
                act.activation(EG[t], by(ps[:, 6, :], DH), ACT.Exp).then_inc(sem("dn_eg"), 1)
                act.wait_ge(sem("dn_dt"), t + 1)
                act.activation(DT, DT, ACT.Exp).then_inc(sem("dn_edt"), 1)

            def dn_x0(t):
                act.wait_ge(sem("dn_x0_turned"), t + 1)
                act.activation(X[t], by(ps[:, 6, :], DH), ACT.Copy).then_inc(sem("dn_X"), 1)

            def dn_y(t, l):
                act.wait_ge(sem("dn_BX"), 2 * (l - 1) + t + 1)
                act.activation(Y[t], by(ps[:, 7 - t, :], DH), ACT.Copy).then_inc(sem("dn_Y"), 1)

            def dn_sol(t):
                act.wait_ge(sem("dn_solved"), 2 * t + 2)
                act.activation(kcT[:, :, t * P:(t + 1) * P], by(ps[:, 7, :], DH), ACT.Copy)\
                   .then_inc(sem("dn_kcT"), 1)

            def head_sums(t, src, width, junk):
                n_h = src.shape[1]
                square_sums([(junk[:, h, :], src[:, h, :], ss[:, t, h:h + 1]) for h in range(n_h)])
                r_ = ss[:, t, 0:n_h]
                act.activation(r_, r_, ACT.Sqrt, scale=1.0 / width, bias=eps[:, :]).then_inc(sem("root_out"), 1)

            def dn_sum(t):
                act.wait_ge(sem("dn_o"), 2 * t + 2)
                head_sums(t, by(ps[:, 2 + t, :], DH), DV, Y[0])

            def dn_out(t):
                act.wait_ge(sem("dn_y2"), t + 1)
                act.activation(ahi[:, 2 * BT:3 * BT, t * P:(t + 1) * P], XT[0], ACT.Copy).then_inc(sem("dn_hi"), 1)

            def merge(n_, g, b, u):
                if n_ == NB - 1:
                    s = slice(4 * g + 2 * b, 4 * g + 2 * b + 2)
                    act.wait_ge(sem("merged"), 2 * g + b + 1)
                    act.activation(hhi[:, s, :], mg[:, s, :], ACT.Copy).then_inc(sem("merged_hi"), 1)

            def up(c, part, u):
                conv_copy(len(convs) + 2 * c + part, u)

            def glu(c, down):
                act.wait_ge(sem("conv_read"), len(convs) + 2 * c + 1)
                act.activation(cy[:, 0, :, :], cy[:, 0, :, :], ACT.Silu).then_inc(sem("glu_silu"), 1)
                act.wait_ge(sem("glu_prod"), c + 1)
                if down is not None:
                    act.wait_ge(sem("unit_done"), down + 1)
                s = 2 * (c % 2)
                act.activation(ahi[:, s:s + 2, :], cy[:, 1, :, :], ACT.Copy).then_inc(sem("glu_hi"), 1)

            def ple_gate(u):
                for t in range(TT):
                    act.wait_ge(sem("half_done") if t == 0 else sem("unit_done"), u + 1)
                    act.activation(sg[:, t, :].rearrange("p (b n) -> p b n", b=2), ps[:, 2 * t:2 * t + 2, :],
                                   ACT.Sigmoid).then_inc(sem(f"g{t}"), 1)

            def ple_load():
                act.dma_start(ptok, a["p"][0][0].rearrange("(t p) d -> p t d", p=P)).then_inc(sem("p_in"), 16)

            def ple_p():
                act.wait_ge(sem("p_turned"), 1)
                act.activation(ahi[:, 4:6, :], tiles(ps[:, 6, :]), ACT.Copy).then_inc(sem("ple_hi"), 1)

            def ab_qk(e, u):
                act.wait_ge(sem("unit_done"), u + 1)
                act.wait_ge(sem("ple_added"), TT)
                act.activation(qkf[:, 2 * e:2 * e + 2, :], tiles(ps[:, units[u]["bank"], :]), ACT.Copy,
                               scale=FD ** -0.5 if e < 2 else 1.0).then_inc(took(u)[0], 1)
                if e == 0:
                    act.dma_start(pw, a["pool_w_2"][0].rearrange("g c d -> c g d")).then_inc(sem("pw_in"), 16)
                    act.dma_start(lamr, a["ab_lambda_2"][0].partition_broadcast(P)).then_inc(sem("pw_in"), 16)

            def ab_v(u):
                act.wait_ge(sem("unit_done"), u + 1)
                for t in range(TT):
                    ins = act.activation(vtok[:, t, :], ps[:, t, :], ACT.Copy)
                ins.then_inc(sem("g0"), 1)

            def pool_u(e, u):
                act.wait_ge(sem("unit_done"), u + 1)
                act.activation(pu[:, 2 * e:2 * e + 2, W0:W0 + T], tiles(ps[:, units[u]["bank"], :]), ACT.Copy)\
                   .then_inc(took(u)[0], 1)

            def lam():
                act.wait_ge(sem("lam_sum"), 1)
                act.activation(lamw[:, 0:2], lamw[:, 0:2], ACT.Exp).then_inc(sem("lam_exp"), 1)

            def pool_mm():
                act.wait_ge(sem("pool_y"), 1)
                act.activation(ahi[:, 4:8, :], pr, ACT.Copy).then_inc(sem("pool_hi"), 1)

            def ab_sum(b):
                act.wait_ge(sem("att1_used"), 6)
                head_sums(b, by(ps[:, b, :], 4), P, oy)

            def ab_turn(b):
                act.wait_ge(sem("ab_oturned"), b + 1)
                act.activation(ahi[:, 0:4, b * P:(b + 1) * P], by(ps[:, 6 + b, :], 4), ACT.Copy,
                               scale=col("subln", 0)).then_inc(sem("ab_hi"), 1)

            def relu2(i, u):
                act.wait_ge(sem("unit_done"), u + 1)
                if i >= 2:
                    act.wait_ge(sem("relu2_lo"), i - 1)
                act.activation(cy[:, i % 2, :, :], tiles(ps[:, units[u]["bank"], :]), ACT.Relu)\
                   .then_inc(took(u)[0], 1)

            def relu2_split(i, c, down):
                act.wait_ge(sem("relu2_sq"), i + 1)
                if down is not None:
                    act.wait_ge(sem("unit_done"), down + 1)
                s = 2 * (c % 2)
                act.activation(ahi[:, s:s + 2, :], cy[:, i % 2, :, :], ACT.Copy).then_inc(sem("relu2_hi"), 1)

            def gla_low():
                act.wait_ge(sem("gla_lowed"), 1)
                act.activation(gkT[0:GR, :], ps[0:GR, 6, 0:T], ACT.Copy).then_inc(sem("gla_gkT"), 1)

            def gla_gate():
                act.wait_ge(sem("gla_abs"), 1)
                act.activation(gla[:, :, :], gla[:, :, :], ACT.Exp, scale=-1.0).then_inc(sem("gla_ln"), 1)
                act.wait_ge(sem("gla_ln"), 1)
                act.activation(gla[:, :, :], gla[:, :, :], ACT.Ln, bias=1.0).then_inc(sem("gla_ln"), 1)

            def gla_qk(e, u):
                act.wait_ge(sem("unit_done"), u + 1)
                act.activation(gqT[:, 2 * e:2 * e + 2, :], tiles(ps[:, units[u]["bank"], :]), ACT.Copy,
                               scale=(GK // GH) ** -0.5 if e < GK // 256 else 1.0).then_inc(took(u)[0], 1)

            def gla_cum():
                for b in range(2):
                    act.wait_ge(sem("gla_cummed"), b + 1)
                    act.activation(bcum[:, 2 * b:2 * b + 2, :], tiles(ps[:, 6 + b, :]), ACT.Copy,
                                   scale=1.0 / 16.0).then_inc(sem("gla_b"), 1)

            def gla_arg(l):
                act.wait_ge(sem("gla_arg"), l + 1)
                act.activation(E1[:, :, :], E1[:, :, :], ACT.Exp).then_inc(sem("gla_E"), 1)

            def gla_decay():
                act.activation(EB[:, :, :], bcum[:, :, :], ACT.Exp).then_inc(sem("gla_EB"), 1)
                act.wait_ge(sem("gla_arg"), 7)
                act.activation(E1[:, :, :], E1[:, :, :], ACT.Exp).then_inc(sem("gla_E"), 1)

            def gla_ktok():
                for b in range(2):
                    act.wait_ge(sem("gla_kturned"), b + 1)
                    act.activation(kdt[:, 4 * b:4 * b + 4, :], by(ps[:, 6 + b, :], 4), ACT.Copy)\
                       .then_inc(sem("gla_kdt"), 1)

            def gla_v(u):
                for t in range(TT):
                    act.wait_ge(sem("half_done") if t == 0 else sem("unit_done"), u + 1)
                    act.activation(vg[:, t, :].rearrange("p (b n) -> p b n", b=2), ps[:, 2 * t:2 * t + 2, :],
                                   ACT.Copy).then_inc(sem(f"g{t}"), 1)

            def gla_g(e, u):
                act.wait_ge(sem("unit_done"), u + 1)
                act.activation(sgT[:, 2 * e:2 * e + 2, :], tiles(ps[:, units[u]["bank"], :]), ACT.Silu)\
                   .then_inc(took(u)[0], 1)

            def gla_sum(t):
                act.wait_ge(sem("gla_o"), 2 * t + 2)
                src = ps[:, 2 * t:2 * t + 2, :].rearrange("p b (h d) -> p (b h) d", d=GV)
                head_sums(t, src, GV, gy.rearrange("p (h c) t -> p h (c t)", h=GH))

            def gla_turn(t):
                for b in range(2):
                    act.wait_ge(sem("gla_y"), 2 * t + b + 1)
                    act.activation(ahi[:, 4 * b:4 * b + 4, t * P:(t + 1) * P], gy[:, 4 * b:4 * b + 4, :],
                                   ACT.Copy).then_inc(sem("gla_hi"), 1)

            def final(waits):
                act.dma_start(nfin, a["norm_final_2"].partition_broadcast(P)).then_inc(sem("nfin_in"), 16)
                link(act.activation(warm[:, :], warm[:, :], ACT.Sqrt))
                for t in range(TT):
                    act.wait_ge(sem(waits[t][0]), waits[t][1])
                    square_sums([(xs[:, t, :], x[:, t, :], ss[:, t, 0:1])])
                    act.activation(ss[:, t, 0:1], ss[:, t, 0:1], ACT.Sqrt, scale=1.0 / D, bias=eps[:, :])\
                       .then_inc(sem("root_out"), 1)

            def fox_norm():
                for g, v in fox_taken:
                    act.wait_ge(sem(g), v)
                act.activation(xs[:, :, 0:2 * FW], fqkv[:, :, 0:2 * FW], ACT.Square).then_inc(sem("fox_sq"), 1)
                root(ss[:, :, :], 1.0 / FD)

            def dn_silu():
                act.wait_ge(sem("conv_read"), 3 * DW // 256)
                for i in range(3):
                    part = dnT[:, DH * i:DH * (i + 1), :]
                    act.activation(part, part, ACT.Silu).then_inc(sem("dn_silu"), 1)
                for i in range(2):
                    act.wait_ge(sem("dn_silu"), i + 1)
                    act.activation(tiles(dsq[:, 1024 * i:1024 * (i + 1)]), dnT[:, DH * i:DH * (i + 1), :], ACT.Square)\
                       .then_inc(sem("dn_sq"), 1)

            def dn_unit():
                act.wait_ge(sem("dn_ss"), 1)
                act.activation(ss[:, 0, :], ps[:, 0, 0:16], ACT.Sqrt, bias=eps[:, :]).then_inc(sem("root_out"), 1)

            fox_taken = [s[3] for s in order if s[0] == "fox_qkv"]

            parts = dict(norm=norm, params=params, small=small, small_turn=small_turn, fox_qkv=fox_qkv, sc=sc, dn=dn, fox_turn=fox_turn,
                         load_params=load_params, glu=glu, relu2_split=relu2_split, ple_load=ple_load,
                         fox_cum=fox_cum, att_scores=att_scores, att_turn=att_turn, fox_out=fox_out, z=z,
                         gate=gate, dn_cum=dn_cum, dn_decay=dn_decay, dn_x0=dn_x0, dn_y=dn_y,
                         dn_sol=dn_sol, dn_out=dn_out, merge=merge, up=up, ple_gate=ple_gate, ple_p=ple_p,
                         ab_qk=ab_qk, ab_v=ab_v, pool_u=pool_u, lam=lam, pool_mm=pool_mm,
                         relu2=relu2, gla_low=gla_low, gla_gate=gla_gate, gla_qk=gla_qk, gla_cum=gla_cum,
                         gla_arg=gla_arg, gla_decay=gla_decay, gla_ktok=gla_ktok, gla_v=gla_v,
                         gla_g=gla_g, gla_sum=gla_sum, gla_turn=gla_turn, final=final, fox_norm=fox_norm,
                         dn_silu=dn_silu, dn_unit=dn_unit, dn_sum=dn_sum, ab_sum=ab_sum, ab_turn=ab_turn)
            parts["mm"] = lambda u, part: split_high(u + LEAD) if part == 0 and u + LEAD < NU else None
            act.dma_start(grow[:, :], a["g_mix"][0].rearrange("(k p) -> k p", p=P)).then_inc(sem("gmix_in"), 16)
            act.wait_ge(sem("constants"), made["ident"])
            for s in order:
                if s[0] in parts:
                    parts[s[0]](*s[1:])

        @block.vector
        def _(dve):
            n = [0]

            def link(ins):
                n[0] += 1
                ins.then_inc(sem("dve_own"), 1)
                dve.wait_ge(sem("dve_own"), n[0])

            def own(ins, name, value):
                ins.then_inc(sem(name), 1)
                dve.wait_ge(sem(name), value)

            def wide(ap, shape):
                return ap.to_broadcast([P] + shape)

            def split_low(u):
                dve.wait_ge(sem("hi_done"), u + 1)
                dve.tensor_tensor(wlo[:, u % SPLIT, :], raw[:, u % RAW, :], whi[:, u % SPLIT, :].bitcast(F32),
                                  ALU.subtract).then_inc(sem("lo_done"), 1)

            roots = [0]

            def root(ap, ins=None):
                roots[0] += 1
                if ins is not None:
                    ins.then_inc(sem("root_in"), 1)
                dve.wait_ge(sem("root_out"), roots[0])
                link(dve.reciprocal(ap, ap))

            def norm_root(i, t):
                root(ss[:, t, 0:1])
                if i < 7:
                    dve.tensor_scalar(diag[:, t, :], ident[:, :], ss[:, t, 0:1], None, ALU.mult)\
                       .then_inc(sem("norm_diag"), 1)
                    return
                if t == 0:
                    dve.wait_ge(sem("nfin_in"), 16)
                dve.scalar_tensor_tensor(out=xs[:, t, :], in0=x[:, t, :], scalar=ss[:, t, 0:1], in1=nfin,
                                         op0=ALU.mult, op1=ALU.mult).then_inc(sem("final_x"), 1)

            def split_late(u):
                if u + LEAD < NU:
                    split_low(u + LEAD)

            def norm(i, waits):
                if i == 0:
                    dve.wait_ge(sem("gmix_turned"), 1)
                    dve.tensor_copy(gcol0[:, :], ps[:, 0, 0:KD]).then_inc(sem("gcol0_done"), 1)
                    dve.wait_ge(sem("gcol0_done"), 1)
                    split_low(0)
                for k in range(KD):
                    dve.wait_ge(sem("norm_hi"), KD * i + (k | 1) + 1)
                    dve.scalar_tensor_tensor(out=hlo[:, k, :], in0=ps[:, turn_banks[i][k // 2], (k % 2) * T:(k % 2 + 1) * T],
                                             scalar=gain(i, k), in1=hhi[:, k, :].bitcast(F32),
                                             op0=ALU.mult, op1=ALU.subtract).then_inc(sem("norm_lo"), 1)
                if i == 0:
                    split_low(1)

            def params():
                dve.wait_ge(sem("constants"), made["all"])
                dve.wait_ge(sem("small_hi"), 1)
                dve.tensor_tensor(smlo[:, :], smraw, smhi[:, :].bitcast(F32), ALU.subtract).then_inc(sem("small_lo"), 1)
                dve.wait_ge(sem("colp_turned"), 1)
                own(dve.tensor_copy(colp[:, :, :].rearrange("p b n -> p (b n)"), ps[:, 7, 0:3 * P]), "colp_done", 1)
                own(dve.tensor_scalar(col("fox_gain", 0), col("fox_gain", 0), FD ** -0.5, None, ALU.mult),
                    "colp_done", 2)
                own(dve.tensor_scalar(col("subln", 0), col("subln", 0), 1.0 - LI, None, ALU.mult), "colp_done", 3)

            def small_turn():
                dve.wait_ge(sem("params_in"), 16 * n_par)
                link(dve.memset(bias16[:, FH:FH + DH], 0.0))
                dve.wait_ge(sem("small_done"), 2)
                link(dve.tensor_tensor(zz[:, 0], ps[:, 6, 0:TT * NSM].rearrange("p (t n) -> p t n", t=TT),
                                       wide(bias16[:, :].unsqueeze(1), [TT, NSM]), ALU.add))
                dve.scalar_tensor_tensor(out=zz[:, 1], in0=zz[:, 0], scalar=-1.0, in1=zz[:, 0], op0=ALU.mult,
                                         op1=ALU.max).then_inc(sem("small_abs"), 1)
                dve.wait_ge(sem("small_exp"), 4)
                link(dve.tensor_scalar(zz[:, 3], zz[:, 1], 1.0, None, ALU.add))
                link(dve.scalar_tensor_tensor(out=zz[:, 1], in0=zz[:, 3], scalar=-1.0, in1=zz[:, 1],
                                              op0=ALU.add, op1=ALU.subtract))
                link(dve.reciprocal(zz[:, 3], zz[:, 3]))
                link(dve.tensor_tensor(zz[:, 1], zz[:, 1], zz[:, 3], ALU.mult))
                link(dve.tensor_tensor(zz[:, 2], zz[:, 2], zz[:, 1], ALU.subtract))
                link(dve.scalar_tensor_tensor(out=gg[:, :, :], in0=zz[:, 0, :, FH + DH:NSM], scalar=0.0,
                                              in1=zz[:, 2, :, FH + DH:NSM], op0=ALU.max, op1=ALU.add))
                link(dve.scalar_tensor_tensor(out=gg[:, :, :], in0=gg[:, :, :], scalar=-1.0,
                                              in1=wide(alog[:, :].unsqueeze(1), [TT, DH]),
                                              op0=ALU.mult, op1=ALU.mult))
                own(dve.scalar_tensor_tensor(out=zz[:, 3], in0=zz[:, 0], scalar=0.0, in1=zz[:, 2],
                                             op0=ALU.min, op1=ALU.subtract), "small_lsg", 1)
                for t in range(TT):
                    dve.tensor_tensor(fcum[:, t], wide(tri[:, :].unsqueeze(1), [FH, P]),
                                      wide(zz[:, 3, t, 0:FH].unsqueeze(2), [FH, P]), ALU.mult)\
                       .then_inc(sem("fox_f"), 1)

            def sc(e, part, j, u):
                out = cy[:, e % 2, :, :]
                if part == 2:
                    dve.wait_ge(sem("unit_done"), u + 1)
                    dve.wait_ge(*took(u - 1))
                    own(dve.tensor_tensor(conv[:, j % 2, :, PAD:PAD + T], tiles(ps[:, units[u]["bank"], :]), out,
                                          ALU.mult), *took_name(u))
                    taps("sc_conv", 3, BT, 2 * e, j, out)
                if part == 0:
                    dve.wait_ge(sem("unit_done"), u + 1)
                    own(dve.tensor_tensor(out, tiles(ps[:, units[u]["bank"], :]), out, ALU.mult), *took_name(u))
                    dve.wait_ge(sem("sc_hi"), e + 1)
                    s = slice(BT + 2 * e, BT + 2 * e + 2)
                    dve.tensor_tensor(alo[:, s, :], out, ahi[:, s, :].bitcast(F32), ALU.subtract)\
                       .then_inc(sem("sc_lo"), 1)

            def took_name(u):
                g, k = units[u]["free"][0]
                return g, k + 1

            def taps(name, width, per_tap, tile0, j, out):
                for i in range(width - 1, -1, -1):
                    lag = width - 1 - i
                    for q in range(2):
                        src = conv[:, j % 2, q, PAD - lag:PAD - lag + T]
                        w = col(name, i * per_tap + tile0 + q)
                        if lag == 0:
                            ins = dve.tensor_scalar(out[:, q, :], src, w, None, ALU.mult)
                        else:
                            ins = dve.scalar_tensor_tensor(out=out[:, q, :], in0=src, scalar=w,
                                                           in1=out[:, q, :], op0=ALU.mult, op1=ALU.add)
                    if i > 0:
                        link(ins)
                own(ins, "conv_read", j + 1)

            def taps_ffn(tile0, j, out):
                for i in range(2, -1, -1):
                    for q in range(2):
                        src = conv[:, j % 2, q, PAD - 2 + i:PAD - 2 + i + T]
                        w = col(f"ffn_conv{i}", tile0 + q)
                        if i == 2:
                            ins = dve.tensor_scalar(out[:, q, :], src, w, None, ALU.mult)
                        else:
                            ins = dve.scalar_tensor_tensor(out=out[:, q, :], in0=src, scalar=w,
                                                           in1=out[:, q, :], op0=ALU.mult, op1=ALU.add)
                    if i > 0:
                        link(ins)
                own(ins, "conv_read", j + 1)

            def dn(e, j, u):
                dve.wait_ge(*took(u))
                taps("dn_conv", 4, 3 * BT, 2 * e, j, dnT[:, 2 * e:2 * e + 2, :])

            def fox_norm():
                dve.wait_ge(sem("fox_sq"), 1)
                nh = 2 * FH
                qk = fqkv[:, :, 0:2 * FW].rearrange("p t (h d) -> p t h d", d=FD)
                sq = xs[:, :, 0:2 * FW].rearrange("p t (h d) -> p t h d", d=FD)
                root(ss[:, :, :], dve.tensor_reduce(ss[:, :, :], sq, AX.X, ALU.add))
                for t in range(TT):
                    dve.tensor_tensor(qk[:, t], qk[:, t], wide(ss[:, t, :].unsqueeze(2), [nh, FD]), ALU.mult)\
                       .then_inc(sem("fox_qk"), 1)

            def att_scores(w, g):
                b, maps = groups[g]
                k, width = len(maps), P * (b + 1)
                Sg = att[w]["S"][:, g % 2, :].rearrange("p (m j) -> p m j", m=k)
                halves_ = [(Sg[:, odd:k:2, :], by(ps[:, bank, 0:k // 2 * width], k // 2))
                           for odd, bank in ((0, 6 + g % 2), (1, 2 + g % 2))]
                dve.wait_ge(sem(f"att{w}_scored"), g + 1)
                if g >= 2:
                    dve.wait_ge(sem(f"att{w}_turned"), g - 1)
                diag = slice(b * P, width)
                if w == 0:
                    dve.wait_ge(sem("fox_bias"), 4)
                    for odd, (dst, src) in enumerate(halves_):
                        link(dve.tensor_tensor(dst, src, fbias[:, maps[0] + odd:maps[0] + k:2, 0:width], ALU.add))
                    link(dve.tensor_tensor(Sg[:, :, diag], Sg[:, :, diag], wide(cneg[:, :].unsqueeze(1), [k, P]),
                                           ALU.add))
                else:
                    for dst, src in halves_:
                        if b:
                            link(dve.tensor_copy(dst[:, :, 0:P], src[:, :, 0:P]))
                        link(dve.tensor_tensor(dst[:, :, diag], src[:, :, diag],
                                               wide(dneg[:, :].unsqueeze(1), [k // 2, P]), ALU.add))
                dve.tensor_reduce(nmax[:, g % 2, 0:k], Sg, AX.X, ALU.max, negate=True)\
                   .then_inc(sem(f"att{w}_max"), 1)

            def att_norm(w, g):
                b, maps = groups[g]
                k, width = len(maps), P * (b + 1)
                Sg = att[w]["S"][:, g % 2, :].rearrange("p (m j) -> p m j", m=k)
                exps = sum(len(m) for _, m in groups[:g + 1])
                dve.wait_ge(sem(f"att{w}_exp"), exps)
                r = rsum[:, g % 2, 0:k]
                link(dve.reciprocal(r, r))
                if w == 0:
                    dve.tensor_tensor(Sg, Sg, wide(r.unsqueeze(2), [k, width]), ALU.mult)\
                       .then_inc(sem("att0_p"), 1)
                    return
                r2 = rsum[:, g % 2, 0:k].rearrange("p (h m) -> p h m", m=2)[:, :, 1]
                link(dve.tensor_scalar(r2, r2, lamw[:, 2:3], None, ALU.mult))
                for i in range(0, k, 2):
                    link(dve.tensor_scalar(Sg[:, i, :], Sg[:, i, :], rsum[:, g % 2, i:i + 1], None, ALU.mult))
                    ins = dve.scalar_tensor_tensor(out=Sg[:, i, :], in0=Sg[:, i + 1, :],
                                                   scalar=rsum[:, g % 2, i + 1:i + 2], in1=Sg[:, i, :],
                                                   op0=ALU.mult, op1=ALU.add)
                ins.then_inc(sem("att1_p"), 1)

            def fox_out():
                for b in range(2):
                    dve.wait_ge(sem("fox_hi"), b + 1)
                    s = slice(2 * b, 2 * b + 2)
                    dve.tensor_tensor(alo[:, s, :], tiles(ps[:, b, :]), ahi[:, s, :].bitcast(F32), ALU.subtract)\
                       .then_inc(sem("fox_lo"), 1)

            def dn_unit():
                root(ss[:, 0, :])
                for i in range(2):
                    dve.tensor_tensor(by(dsq[:, 1024 * i:1024 * (i + 1)], 8), wide(ident[:, :].unsqueeze(1), [8, P]),
                                      wide(ss[:, 0, 8 * i:8 * i + 8].unsqueeze(2), [8, P]), ALU.mult)\
                       .then_inc(sem("dn_dd"), 1)

            def dn_scale():
                q, k = dnT[:, 0:DH, :], dnT[:, DH:2 * DH, :]
                for i, (part, s) in enumerate(((q, DV ** -0.5), (k, 1.0))):
                    dve.wait_ge(sem("dn_bc"), 2 * i + 2)
                    two = ps[:, 2 * i:2 * i + 2, :].rearrange("p b (c t) -> p (b c) t", t=T)
                    own(dve.scalar_tensor_tensor(out=part, in0=part, scalar=s, in1=two, op0=ALU.mult,
                                                 op1=ALU.mult), "dn_qk", i + 1)

            def dn_cum():
                dve.wait_ge(sem("dn_gc"), 1)
                pg = ps[:, 6, 0:TT * 2 * DH].rearrange("p (t a h) -> p t a h", t=TT, a=2)
                link(dve.tensor_copy(gcol[:, :, :], pg[:, :, 0, :]))
                link(dve.tensor_copy(gx[:, :, 0, :], pg[:, :, 0, :]))
                dve.tensor_tensor(gx[:, :, 1, :], pg[:, :, 1, :], gcol[:, :, :], ALU.subtract)\
                   .then_inc(sem("dn_gx"), 1)
                dve.wait_ge(sem("dn_egx"), 1)
                link(dve.tensor_tensor(gx[:, :, 0, :], gx[:, :, 0, :], beta[:, :, :], ALU.mult))

            def dn_tok(t):
                dve.wait_ge(sem("dn_tokened"), 2 * t + 2)
                k, v = by(ps[:, 2 * t, :], DH), by(ps[:, 2 * t + 1, :], DH)
                dve.tensor_tensor(rhsk[:, t], k, wide(gx[:, t, 0, :].unsqueeze(2), [DH, P]), ALU.mult)\
                   .then_inc(sem("dn_tok"), 1)
                dve.tensor_tensor(kdec[:, t], k, wide(gx[:, t, 1, :].unsqueeze(2), [DH, P]), ALU.mult)\
                   .then_inc(sem("dn_tok"), 1)
                dve.tensor_tensor(vb[:, t], v, wide(beta[:, t, :].unsqueeze(2), [DH, P]), ALU.mult)\
                   .then_inc(sem("dn_tok"), 1)

            def dn_decay(t):
                dve.tensor_tensor(X[t], wide(tri64[:, :].unsqueeze(1), [DH, P]),
                                  wide(gg[:, t, :].unsqueeze(2), [DH, P]), ALU.mult).then_inc(sem("dn_gb"), 1)
                dve.tensor_tensor(XT[t], wide(ident[:, :].unsqueeze(1), [DH, P]),
                                  wide(beta[:, t, :].unsqueeze(2), [DH, P]), ALU.mult).then_inc(sem("dn_gb"), 1)
                dve.wait_ge(sem("dn_eg"), t + 1)
                link(dve.tensor_tensor(DT, by(ps[:, 6, :], DH), wide(gcol[:, t, :].unsqueeze(2), [DH, P]),
                                       ALU.subtract))
                dve.tensor_scalar(DT, DT, 0.0, None, ALU.min).then_inc(sem("dn_dt"), 1)
                dve.tensor_copy(gt[:, t], EG[t][:, :, CH - 1:P:CH]).then_inc(sem("dn_gt"), 1)
                dve.wait_ge(sem("dn_edt"), t + 1)
                link(dve.tensor_tensor(DT, DT, wide(tri64[:, :].unsqueeze(1), [DH, P]), ALU.mult))

            def dn_kk(t):
                dve.wait_ge(sem("dn_kked"), 2 * t + 2)
                link(dve.tensor_tensor(LT[t], by(ps[:, 2 * t, :], DH), DT, ALU.mult))
                link(dve.tensor_tensor(LT[t], by(ps[:, 7, :], DH), LT[t], ALU.mult))
                link(dve.tensor_tensor(qkT[:, t], by(ps[:, 2 * t + 1, :], DH), DT, ALU.mult))
                q = dnT[:, 0:DH, t * P:(t + 1) * P]
                dve.tensor_tensor(q, q, EG[t], ALU.mult).then_inc(sem("dn_lt"), 1)

            def dn_x0(t):
                link(dve.tensor_tensor(Bl[t], LT[t], wide(lev[:, 0, :].unsqueeze(1), [DH, P]), ALU.mult))
                dve.tensor_tensor(XT[t], wide(ident[:, :].unsqueeze(1), [DH, P]), Bl[t], ALU.subtract)\
                   .then_inc(sem("dn_x0"), 1)
                dve.wait_ge(sem("dn_x0"), t + 1)

            def dn_y(t, l):
                dve.tensor_tensor(Bl[t], LT[t], wide(lev[:, l, :].unsqueeze(1), [DH, P]), ALU.mult)\
                   .then_inc(sem("dn_B"), 1)

            def dn_z(t, l):
                n_ = 2 * (l - 1) + t + 1
                dve.wait_ge(sem("dn_XBX"), 2 * n_)
                own(dve.tensor_tensor(XT[t], XT[t], by(ps[:, 2 * t, :], DH), ALU.subtract), "dn_X2", 2 * n_ - 1)
                own(dve.tensor_tensor(X[t], X[t], by(ps[:, 2 * t + 1, :], DH), ALU.subtract), "dn_X2", 2 * n_)

            def dn_sol(t):
                dve.wait_ge(sem("dn_solved"), 2 * t + 1)
                own(dve.tensor_copy(vb[:, t], by(ps[:, 6, :], DH)), "dn_u", t + 1)

            def dn_new(c):
                t, p0 = c // 2, CH * (c % 2)
                if c == 0:
                    return
                dve.wait_ge(sem("dn_kS"), c)
                part = vb[p0:p0 + CH, t]
                own(dve.tensor_tensor(part, part, by(ps[p0:p0 + CH, 0, :], DH), ALU.subtract), "dn_vnew", c)

            def dn_state(c):
                if c == NCH - 1:
                    return
                t = c // 2
                dve.wait_ge(sem("dn_supd"), c + 1)
                pS = by(ps[:, 1, :], DH)
                if c == 0:
                    own(dve.tensor_copy(S, pS), "dn_S", 1)
                    return
                for h in range(DH):
                    ins = dve.scalar_tensor_tensor(out=S[:, h, :], in0=S[:, h, :], scalar=gt[:, t, h, c % 2:c % 2 + 1],
                                                   in1=pS[:, h, :], op0=ALU.mult, op1=ALU.add)
                own(ins, "dn_S", c + 1)

            def head_scale(t, out, src, width):
                heads = src.shape[1]
                r_ = ss[:, t, 0:heads]
                root(r_)
                return dve.tensor_tensor(out, src, wide(r_.unsqueeze(2), [heads, width]), ALU.mult)

            def dn_sum(t):
                head_scale(t, rhsk[:, t], by(ps[:, 2 + t, :], DH), DV).then_inc(sem("dn_onorm"), 1)

            def dn_out(t):
                dve.wait_ge(sem("dn_oturned"), t + 1)
                if t >= 1:
                    dve.wait_ge(sem("dn_hi"), t)
                own(dve.scalar_tensor_tensor(out=XT[0], in0=by(ps[:, 6, :], DH), scalar=col("dn_gain", 0),
                                             in1=zT[:, :, t * P:(t + 1) * P], op0=ALU.mult, op1=ALU.mult),
                    "dn_y2", t + 1)
                dve.wait_ge(sem("dn_hi"), t + 1)
                s = (slice(None), slice(2 * BT, 3 * BT), slice(t * P, (t + 1) * P))
                own(dve.tensor_tensor(alo[s], XT[0], ahi[s].bitcast(F32), ALU.subtract), "dn_lo", t + 1)

            def merge(n_, g, b, u):
                done = sem("half_done") if b == 0 else sem("unit_done")
                dve.wait_ge(done, u + 1)
                s = 4 * g + 2 * b
                merged = mg[:, s:s + 2, :]
                gate_ = gates[:, KD * n_ + s:KD * n_ + s + 2, :]
                ins = dve.tensor_tensor(gate_, tiles(ps[:, units[u]["bank"] + b, :]), gate_, ALU.mult)
                if n_ < NB - 1:
                    own(ins, f"c{4 + b}", units[u]["free"][b][1] + 1)
                elif b == 1:
                    own(ins, f"g{g}", units[u]["free"][0][1] + 1)
                else:
                    link(ins)
                if n_ == 0:
                    return
                ins = dve.tensor_tensor(merged, merged, gate_, ALU.add)
                if n_ < NB - 1:
                    link(ins)
                else:
                    own(ins, "merged", 2 * g + b + 1)

            def merge_lo(i):
                dve.wait_ge(sem("merged_hi"), i + 1)
                s = slice(2 * i, 2 * i + 2)
                dve.tensor_tensor(hlo[:, s, :], mg[:, s, :], hhi[:, s, :].bitcast(F32), ALU.subtract)\
                   .then_inc(sem("merged_lo"), 1)

            def resid(u, t):
                dve.wait_ge(sem("half_done") if t == 0 else sem("unit_done"), u + 1)
                xt = x[:, t, :].rearrange("p (b n) -> p b n", b=2)
                dve.tensor_tensor(xt, xt, ps[:, 2 * t:2 * t + 2, :], ALU.add).then_inc(sem(f"g{t}"), 1)

            def up(c, part, u):
                dve.wait_ge(*took(u))
                taps_ffn(UPT * part + 2 * c, len(convs) + 2 * c + part, cy[:, part, :, :])

            def glu(c, down):
                dve.wait_ge(sem("glu_silu"), c + 1)
                own(dve.tensor_tensor(cy[:, 1, :, :], cy[:, 0, :, :], cy[:, 1, :, :], ALU.mult), "glu_prod", c + 1)
                dve.wait_ge(sem("glu_hi"), c + 1)
                s = slice(2 * (c % 2), 2 * (c % 2) + 2)
                own(dve.tensor_tensor(alo[:, s, :], cy[:, 1, :, :], ahi[:, s, :].bitcast(F32), ALU.subtract),
                    "glu_lo", c + 1)

            def ple_p():
                dve.wait_ge(sem("ple_hi"), 1)
                dve.tensor_tensor(alo[:, 4:6, :], tiles(ps[:, 6, :]), ahi[:, 4:6, :].bitcast(F32), ALU.subtract)\
                   .then_inc(sem("ple_lo"), 1)

            def ple_x(u, t):
                dve.wait_ge(sem("half_done") if t == 0 else sem("unit_done"), u + 1)
                st_ = sg[:, t, :].rearrange("p (b n) -> p b n", b=2)
                own(dve.tensor_tensor(st_, ps[:, 2 * t:2 * t + 2, :], st_, ALU.mult), f"g{t}",
                    units[u]["free"][t][1] + 1)
                dve.tensor_tensor(x[:, t, :], x[:, t, :], sg[:, t, :], ALU.add).then_inc(sem("ple_added"), 1)

            def lam():
                dve.wait_ge(sem("pw_in"), 32)
                w4 = lamr[:, :, :].rearrange("p (a b) d -> p a b d", b=2)
                link(dve.tensor_tensor(w4[:, :, 0, :], w4[:, :, 0, :], w4[:, :, 1, :], ALU.mult))
                dve.tensor_reduce(lamw[:, 0:2], w4[:, :, 0, :], AX.X, ALU.add).then_inc(sem("lam_sum"), 1)
                dve.wait_ge(sem("lam_exp"), 1)
                link(dve.tensor_tensor(lamw[:, 2:3], lamw[:, 1:2], lamw[:, 0:1], ALU.subtract))
                link(dve.tensor_scalar(lamw[:, 2:3], lamw[:, 2:3], -LI, None, ALU.add))

            def pool_mm():
                dve.wait_ge(sem("pool_mmed"), 1)
                for g in range(4):
                    ins = dve.tensor_scalar(pr[:, g, :], tiles(ps[:, 4 + g // 2, :])[:, g % 2, :],
                                            col("pool_scale", g), None, ALU.mult)
                own(ins, "pool_y", 1)
                dve.wait_ge(sem("pool_hi"), 1)
                dve.tensor_tensor(alo[:, 4:8, :], pr, ahi[:, 4:8, :].bitcast(F32), ALU.subtract)\
                   .then_inc(sem("pool_lo"), 1)

            def ab_sum(b):
                head_scale(b, ob[:, b], by(ps[:, b, :], 4), P).then_inc(sem("ab_onorm"), 1)

            def ab_turn(b):
                dve.wait_ge(sem("ab_hi"), b + 1)
                s = (slice(None), slice(0, 4), slice(b * P, (b + 1) * P))
                dve.scalar_tensor_tensor(out=alo[s], in0=by(ps[:, 6 + b, :], 4), scalar=col("subln", 0),
                                         in1=ahi[s].bitcast(F32), op0=ALU.mult, op1=ALU.subtract)\
                   .then_inc(sem("ab_lo"), 1)

            def relu2(i, u):
                dve.wait_ge(*took(u))
                y = cy[:, i % 2, :, :]
                own(dve.tensor_tensor(y, y, y, ALU.mult), "relu2_sq", i + 1)

            def relu2_split(i, c, down):
                dve.wait_ge(sem("relu2_hi"), i + 1)
                s = slice(2 * (c % 2), 2 * (c % 2) + 2)
                dve.tensor_tensor(alo[:, s, :], cy[:, i % 2, :, :], ahi[:, s, :].bitcast(F32), ALU.subtract)\
                   .then_inc(sem("relu2_lo"), 1)

            def gla_gate():
                dve.wait_ge(sem("gla_gated"), 2)
                two = ps[:, 0:2, :]
                link(dve.tensor_scalar(gmin, two, 0.0, None, ALU.min))
                dve.scalar_tensor_tensor(out=gla, in0=gmin, scalar=-2.0, in1=two, op0=ALU.mult, op1=ALU.add).then_inc(sem("gla_abs"), 1)
                dve.wait_ge(sem("gla_ln"), 2)
                own(dve.tensor_tensor(gla, gmin, gla, ALU.subtract), "gla_la", 1)

            def gla_mask(l):
                dve.wait_ge(sem("gla_paired"), 2 * l + 2)
                two = ps[:, 6:8, :].rearrange("p b (g i) -> p (b g) i", i=P)
                mask = ident[:, :] if l == 0 else lev[:, l - 1, :]
                dst = attn if l == 0 else atmp
                own(dve.tensor_tensor(dst, two, wide(mask.unsqueeze(1), [TT * GH, P]), ALU.mult), "gla_took", l + 1)
                if l:
                    link(dve.tensor_tensor(attn, attn, atmp, ALU.add))

            def halves(ap, l):
                return ap.rearrange("p h t -> p (h t)").rearrange("p (m two s) -> p m two s", two=2, s=1 << l)

            def gla_arg(l):
                s = 1 << l
                if l == 0:
                    dve.wait_ge(sem("gla_b"), 2)
                    dve.wait_ge(*gla_qk_ready[0])
                    dve.wait_ge(*gla_qk_ready[1])
                b_, e_ = halves(bcum, l), halves(E1, l)
                m = GH * T // (2 * s)
                ref = wide(b_[:, :, 0, s - 1:s], [m, s])
                dve.tensor_tensor(e_[:, :, 1, :], b_[:, :, 1, :], ref, ALU.subtract)
                own(dve.tensor_tensor(e_[:, :, 0, :], ref, b_[:, :, 0, :], ALU.subtract), "gla_arg", l + 1)

            def gla_mul(l):
                e_, c_ = halves(E1, l), halves(Cl, l)
                q_, k_ = halves(gqT[:, 0:GH, :], l), halves(gqT[:, GH:2 * GH, :], l)
                dve.wait_ge(sem("gla_E"), l + 1)
                dve.tensor_tensor(c_[:, :, 1, :], e_[:, :, 1, :], q_[:, :, 1, :], ALU.mult)
                own(dve.tensor_tensor(c_[:, :, 0, :], e_[:, :, 0, :], k_[:, :, 0, :], ALU.mult), "gla_C", l + 1)

            def gla_decay():
                b_ = bcum.rearrange("p h (c s) -> p (h c) s", s=CH)
                e_ = E1.rearrange("p h (c s) -> p (h c) s", s=CH)
                own(dve.tensor_tensor(e_, wide(b_[:, :, CH - 1:CH], [GH * NCH, CH]), b_, ALU.subtract), "gla_arg", 7)
                dve.wait_ge(sem("gla_EB"), 1)
                q = gqT[:, 0:GH, :]
                link(dve.tensor_tensor(q, q, EB, ALU.mult))

            def gla_k():
                dve.wait_ge(sem("gla_E"), 7)
                own(dve.tensor_tensor(Cl, E1, gqT[:, GH:2 * GH, :], ALU.mult), "gla_C", 7)

            def gla_chunk(c):
                if c == NCH - 1:
                    return
                dve.wait_ge(sem("gla_supd"), 2 * c + 2)
                pS = ps[:, 6:8, :].rearrange("p b (h d) -> p (b h) d", d=GV)
                if c == 0:
                    own(dve.tensor_copy(GS, pS), "gla_S", 1)
                    return
                for h in range(GH):
                    ins = dve.scalar_tensor_tensor(out=GS[:, h, :], in0=GS[:, h, :],
                                                   scalar=EB[:, h, CH * c + CH - 1:CH * c + CH],
                                                   in1=pS[:, h, :], op0=ALU.mult, op1=ALU.add)
                own(ins, "gla_S", c + 1)

            def gla_sum(t):
                head_scale(t, og[t], ps[:, 2 * t:2 * t + 2, :].rearrange("p b (h d) -> p (b h) d", d=GV), GV)\
                    .then_inc(sem("gla_onorm"), 1)

            def gla_turn(t):
                if t == 0:
                    for ready in gla_g_ready:
                        dve.wait_ge(*ready)
                for b in range(2):
                    dve.wait_ge(sem("gla_oturned"), 2 * t + b + 1)
                    for i in range(4 * b, 4 * b + 4):
                        ins = dve.scalar_tensor_tensor(out=gy[:, i, :], in0=by(ps[:, 6 - 2 * t + b, :], 4)[:, i % 4, :],
                                                       scalar=col("gla_norm", i),
                                                       in1=sgT[:, i, t * P:(t + 1) * P],
                                                       op0=ALU.mult, op1=ALU.mult)
                    own(ins, "gla_y", 2 * t + b + 1)
                for b in range(2):
                    dve.wait_ge(sem("gla_hi"), 2 * t + b + 1)
                    s = (slice(None), slice(4 * b, 4 * b + 4), slice(t * P, (t + 1) * P))
                    own(dve.tensor_tensor(alo[s], gy[:, 4 * b:4 * b + 4, :], ahi[s].bitcast(F32), ALU.subtract),
                        "gla_lo", 2 * t + b + 1)

            gla_g_ready = [took(s[2]) for s in order if s[0] == "gla_g"][-2:]
            gla_qk_ready = [took(s[2]) for s in order if s[0] == "gla_qk"][2:]
            parts = dict(norm=norm, params=params, small_turn=small_turn, sc=sc, dn=dn, fox_norm=fox_norm, dn_scale=dn_scale,
                         dn_sum=dn_sum, ab_sum=ab_sum, ab_turn=ab_turn, gla_sum=gla_sum, gla_turn=gla_turn,
                         att_scores=att_scores, att_norm=att_norm, glu=glu, relu2_split=relu2_split,
                         fox_out=fox_out, dn_unit=dn_unit, dn_cum=dn_cum, dn_tok=dn_tok,
                         dn_decay=dn_decay, dn_kk=dn_kk, dn_x0=dn_x0, dn_y=dn_y, dn_z=dn_z, dn_sol=dn_sol,
                         dn_new=dn_new, dn_state=dn_state, dn_out=dn_out, merge=merge, merge_lo=merge_lo, resid=resid, up=up,
                         ple_p=ple_p, ple_x=ple_x, lam=lam, pool_mm=pool_mm,
                         relu2=relu2, gla_gate=gla_gate, gla_mask=gla_mask, gla_mul=gla_mul,
                         gla_k=gla_k, gla_arg=gla_arg, gla_decay=gla_decay, gla_chunk=gla_chunk,
                         norm_root=norm_root, split_late=split_late)
            parts["mm"] = lambda u, part: split_low(u + LEAD) if part == 1 and u not in late and u + LEAD < NU else None
            dve.wait_ge(sem("constants"), made["ident"])
            for s in order:
                if s[0] in parts:
                    parts[s[0]](*s[1:])

        @block.tensor
        def _(pe):
            def mm(u, part):
                w = units[u]
                s = u % SPLIT
                if part == 0:
                    pe.wait_ge(sem("lo_done"), u + 1)
                    if u not in fresh:
                        for name, v in w["needs"]:
                            pe.wait_ge(sem(name), v)
                else:
                    for name, v in w.get("needs_last", ()):
                        pe.wait_ge(sem(name), v)
                first = part == 0
                free = w["free"] if w["kind"] == "T" else w["free"][part:part + 1]
                for name, v in free:
                    if v:
                        pe.wait_ge(sem(name), v)
                hi, lo = (hhi, hlo) if w["act"] == "h" else (ahi, alo)
                k0 = w.get("k0", 0)

                def normed(k):
                    if first and u in fresh:
                        pe.wait_ge(sem("norm_lo"), KD * fresh[u] + k + 1)

                if w["kind"] in "CB":
                    nk, width = (KD, 256) if w["kind"] == "C" else (4, 512)
                    n = width // P // 2
                    for ct in range(part * n, part * n + n):
                        out = ps[:, w["bank"] + ct // 2, (ct % 2) * T:(ct % 2 + 1) * T]
                        for k in range(nk):
                            at = k * width + ct * P
                            wh, wl = whi[:, s, at:at + P], wlo[:, s, at:at + P]
                            normed(k)
                            pe.matmul(out, wh, hi[:, k0 + k, :], start=k == 0, stop=False)
                            pe.matmul(out, wh, lo[:, k0 + k, :], start=False, stop=False)
                            ins = pe.matmul(out, wl, hi[:, k0 + k, :], start=False, stop=k == nk - 1)
                else:
                    nk, banks = (4, [(w.get("bank", 0) + part, 0)]) if w["kind"] == "T" else \
                        (2, [(2 * part + b, b) for b in range(2)])
                    width = 512 if w["kind"] == "T" else D
                    for bank, b in banks:
                        out = ps[:, bank, :]
                        for k in range(nk):
                            at = k * width + 512 * b
                            wh, wl = whi[:, s, at:at + 512], wlo[:, s, at:at + 512]
                            xh = hi[:, k0 + k, part * P:(part + 1) * P]
                            xl = lo[:, k0 + k, part * P:(part + 1) * P]
                            start, stop = w["first"] and k == 0, w["last"] and k == nk - 1
                            if b == 0:
                                normed(k0 + k)
                            pe.matmul(out, xh, wh, start=start, stop=False)
                            pe.matmul(out, xh, wl, start=False, stop=False)
                            ins = pe.matmul(out, xl, wh, start=False, stop=stop)
                ins.then_inc(sem("half_done") if part == 0 else sem("unit_done"), 1)

            def norm(i, waits):
                if i == 0:
                    pe.wait_ge(sem("gmix_in"), 16)
                    pe.transpose(ps[:, 0, 0:KD], grow[:, :], ident[0:KD, 0:KD]).then_inc(sem("gmix_turned"), 1)
                for t in range(TT):
                    pe.wait_ge(sem("norm_diag"), TT * i + t + 1)
                    for k in range(KD):
                        at = (k % 2) * T + t * P
                        ins = pe.matmul(ps[:, turn_banks[i][k // 2], at:at + P], x[:, t, k * P:(k + 1) * P], diag[:, t, :],
                                        start=True, stop=True)
                        if t == TT - 1 and k % 2:
                            ins.then_inc(sem("norm_turned"), 1)

            def params():
                pe.wait_ge(sem("rows_in"), 16 * n_rows)
                for b in range(3):
                    ins = pe.transpose(ps[:, 7, b * P:(b + 1) * P], rows[:, b, :], ident[:, :])
                ins.then_inc(sem("colp_turned"), 1)

            def small():
                pe.wait_ge(sem("norm_lo"), KD)
                pe.wait_ge(sem("small_lo"), 1)
                out = ps[0:NSM, 6, 0:T]
                for k in range(KD):
                    pe.matmul(out, wsm[1][:, k, :], hhi[:, k, :], start=k == 0, stop=False)
                    pe.matmul(out, wsm[1][:, k, :], hlo[:, k, :], start=False, stop=False)
                    ins = pe.matmul(out, wsm[2][:, k, :], hhi[:, k, :], start=False, stop=k == KD - 1)
                ins.then_inc(sem("small_done"), 1)

            def small_turn():
                pe.wait_ge(sem("small_exp"), 1)
                for t in range(TT):
                    ins = pe.transpose(ps[:, 6, t * NSM:(t + 1) * NSM], smT[:, t * P:(t + 1) * P], ident[0:NSM, 0:NSM])
                ins.then_inc(sem("small_done"), 1)

            def fox_turn(t):
                pe.wait_ge(sem("fox_qk"), t + 1)
                for b in range(2):
                    for c in range(4):
                        at = FW * b + c * P
                        ins = pe.transpose(ps[:, 2 * t + b, c * P:(c + 1) * P], fqkv[:, t, at:at + P], ident[:, :])
                    ins.then_inc(sem("fox_turned"), 1)

            def fox_cum(t):
                pe.wait_ge(sem("fox_f"), TT)
                pe.wait_ge(sem("fox_T"), 4)
                for b in range(2):
                    out = by(ps[:, 2 * t + b, :], 4)
                    if t:
                        lf = zz[:, 3, 0, 4 * b:4 * b + 4].unsqueeze(2).to_broadcast([P, 4, P])
                        pe.matmul(out, ones[:, :], lf, start=True, stop=False)
                    pe.matmul(out, ones[:, :], fcum[:, t, 4 * b:4 * b + 4, :], start=t == 0, stop=True)\
                      .then_inc(sem("fox_cummed"), 1)

            def att_scores(w, g):
                b, maps = groups[g]
                width = P * (b + 1)
                q, k = att[w]["q"], att[w]["k"]
                if g == 0:
                    if w == 0:
                        pe.wait_ge(sem("fox_T"), 4)
                        pe.wait_ge(sem("fox_bias"), 4)
                    else:
                        for r in ab_qk_ready:
                            pe.wait_ge(*r)
                if g >= 2:
                    pe.wait_ge(sem(f"att{w}_PT"), g - 1)
                for i, f in enumerate(maps):
                    half = slice(FD * (f % 2), FD * (f % 2) + FD)
                    bank, at = (6 if f % 2 == 0 else 2) + g % 2, (i // 2) * width
                    ins = pe.matmul(ps[:, bank, at:at + width], q[half, f // 2, b * P:(b + 1) * P],
                                    k[half, f // 2, 0:width], start=True, stop=True)
                ins.then_inc(sem(f"att{w}_scored"), 1)

            def att_turn(w, g):
                pe.wait_ge(sem(f"att{w}_p"), g + 1)
                for i, (at, _, _) in enumerate(turned(w, g)):
                    ins = pe.transpose(ps[:, 6 + g % 2, i * P:(i + 1) * P], att[w]["S"][:, g % 2, at:at + P],
                                       ident[:, :])
                ins.then_inc(sem(f"att{w}_turned"), 1)

            def att_values(w, g):
                b, _ = groups[g]
                pe.wait_ge(sem(f"att{w}_PT"), g + 1)
                if g == 0:
                    if w == 0:
                        pe.wait_ge(sem("fox_bias"), 4)
                    else:
                        pe.wait_ge(*ab_v_ready)
                for i, (_, f, kt) in enumerate(turned(w, g)):
                    pT = att[w]["PT"][:, g % 2, i * P:(i + 1) * P]
                    if w == 0:
                        at = (f // 2 % 2) * T + b * P
                        ins = pe.matmul(ps[FD * (f % 2):FD * (f % 2) + FD, f // 4, at:at + P],
                                        fqkv[:, kt, 2 * FW + f * FD:2 * FW + (f + 1) * FD], pT,
                                        start=kt == 0, stop=kt == b)
                    else:
                        ins = pe.matmul(ps[:, b, f * P:(f + 1) * P], pT, vtok[:, kt, f * P:(f + 1) * P],
                                        start=kt == 0, stop=kt == b)
                ins.then_inc(sem(f"att{w}_used"), 1)

            def dn_square():
                pe.wait_ge(sem("dn_sq"), 2)
                pe.wait_ge(sem("fox_lo"), 2)
                for i in range(16):
                    ins = pe.matmul(ps[:, 0, i:i + 1], dsq[:, P * i:P * (i + 1)], ones[:, 0:1], start=True, stop=True)
                ins.then_inc(sem("dn_ss"), 1)

            def dn_unit():
                for b in range(4):
                    pe.wait_ge(sem("dn_dd"), b // 2 + 1)
                    pe.matmul(ps[:, b, :], ones[:, :], dsq[:, 512 * b:512 * (b + 1)], start=True, stop=True)\
                      .then_inc(sem("dn_bc"), 1)

            def dn_cum():
                pe.wait_ge(sem("att0_PT"), 6)
                for t in range(TT):
                    for j, m in enumerate((tri64, blk64)):
                        at = (2 * t + j) * DH
                        ins = pe.matmul(ps[:, 6, at:at + DH], m[:, :], gg[:, t, :], start=True, stop=True)
                ins.then_inc(sem("dn_gc"), 1)

            def dn_tok(t):
                pe.wait_ge(sem("dn_qk"), 2)
                for j, c0 in enumerate((DH, 2 * DH)):
                    for h in range(DH):
                        ins = pe.transpose(ps[:, 2 * t + j, h * P:(h + 1) * P], dnT[:, c0 + h, t * P:(t + 1) * P],
                                           ident[:, :])
                    ins.then_inc(sem("dn_tokened"), 1)

            def dn_decay(t):
                pe.wait_ge(sem("dn_gb"), 2 * t + 2)
                if t == 0:
                    pe.wait_ge(sem("dn_gx"), 1)
                else:
                    pe.wait_ge(sem("dn_X"), t)
                    pe.wait_ge(sem("dn_lt"), t)
                pe.matmul(by(ps[:, 7, :], DH), ones[:, :], XT[t], start=True, stop=True)
                pe.matmul(by(ps[:, 6, :], DH), ones[:, :], X[t], start=True, stop=True).then_inc(sem("dn_grow"), 1)

            def dn_kk(t):
                pe.wait_ge(sem("dn_tok"), 3 * t + 3)
                for j in range(2):
                    for h in range(DH):
                        cols_ = slice(t * P, (t + 1) * P)
                        ins = pe.matmul(ps[:, 2 * t + j, h * P:(h + 1) * P], dnT[:, DH + h, cols_],
                                        dnT[:, (DH if j == 0 else 0) + h, cols_], start=True, stop=True)
                    ins.then_inc(sem("dn_kked"), 1)

            def dn_x0(t):
                pe.wait_ge(sem("dn_x0"), t + 1)
                pe.wait_ge(sem("dn_edt"), t + 1)
                for h in range(DH):
                    ins = pe.transpose(ps[:, 6, h * P:(h + 1) * P], XT[t][:, h, :], ident[:, :])
                ins.then_inc(sem("dn_x0_turned"), 1)

            def dn_y(t, l):
                n_ = 2 * (l - 1) + t + 1
                pe.wait_ge(sem("dn_B"), n_)
                pe.wait_ge(sem("dn_X"), t + 1)
                if l > 1:
                    pe.wait_ge(sem("dn_X2"), 2 * (n_ - 2))
                for h in range(DH):
                    ins = pe.matmul(ps[:, 7 - t, h * P:(h + 1) * P], Bl[t][:, h, :], X[t][:, h, :], start=True, stop=True)
                ins.then_inc(sem("dn_BX"), 1)

            def dn_z(t, l):
                pe.wait_ge(sem("dn_Y"), 2 * (l - 1) + t + 1)
                for h in range(DH):
                    ins = pe.matmul(ps[:, 2 * t, h * P:(h + 1) * P], Y[t][:, h, :], XT[t][:, h, :], start=True, stop=True)
                ins.then_inc(sem("dn_XBX"), 1)
                for h in range(DH):
                    ins = pe.matmul(ps[:, 2 * t + 1, h * P:(h + 1) * P], XT[t][:, h, :], Y[t][:, h, :], start=True, stop=True)
                ins.then_inc(sem("dn_XBX"), 1)

            def dn_sol(t):
                pe.wait_ge(sem("dn_X2"), 2 * (8 + t + 1))
                if t:
                    pe.wait_ge(sem("dn_u"), t)
                    pe.wait_ge(sem("dn_kcT"), t)
                for h in range(DH):
                    ins = pe.matmul(ps[:, 6, h * P:(h + 1) * P], XT[t][:, h, :], vb[:, t, h, :], start=True, stop=True)
                ins.then_inc(sem("dn_solved"), 1)
                for h in range(DH):
                    ins = pe.matmul(ps[:, 7, h * P:(h + 1) * P], rhsk[:, t, h, :], XT[t][:, h, :], start=True, stop=True)
                ins.then_inc(sem("dn_solved"), 1)

            def dn_new(c):
                if c == 0:
                    return
                t, p0 = c // 2, CH * (c % 2)
                pe.wait_ge(sem("dn_S"), c)
                pe.wait_ge(sem("dn_kcT"), t + 1)
                for h in range(DH):
                    ins = pe.matmul(ps[p0:p0 + CH, 0, h * P:(h + 1) * P], kcT[:, h, c * CH:(c + 1) * CH], S[:, h, :],
                                    start=True, stop=True)
                ins.then_inc(sem("dn_kS"), 1)

            def dn_state(c):
                t, p0 = c // 2, CH * (c % 2)
                own_ = slice(p0, p0 + CH)
                pe.wait_ge(sem("dn_u"), t + 1)
                if c:
                    pe.wait_ge(sem("dn_vnew"), c)
                for h in range(DH):
                    out = ps[own_, 2 + t, h * P:(h + 1) * P]
                    if c:
                        pe.matmul(out, dnT[:, h, c * CH:(c + 1) * CH], S[:, h, :], start=True, stop=False)
                    ins = pe.matmul(out, qkT[own_, t, h, own_], vb[own_, t, h, :], start=c == 0, stop=True)
                ins.then_inc(sem("dn_o"), 1)
                if c < NCH - 1:
                    for h in range(DH):
                        ins = pe.matmul(ps[:, 1, h * P:(h + 1) * P], kdec[own_, t, h, :], vb[own_, t, h, :],
                                        start=True, stop=True)
                    ins.then_inc(sem("dn_supd"), 1)

            def dn_out(t):
                pe.wait_ge(sem("dn_onorm"), t + 1)
                pe.wait_ge(sem("dn_u"), TT)
                if t:
                    pe.wait_ge(sem("dn_y2"), t)
                for h in range(DH):
                    ins = pe.transpose(ps[:, 6, h * P:(h + 1) * P], rhsk[:, t, h, :], ident[:, :])
                ins.then_inc(sem("dn_oturned"), 1)

            def ple_p():
                pe.wait_ge(sem("p_in"), 16)
                for k in range(2):
                    for t in range(TT):
                        at = k * T + t * P
                        ins = pe.transpose(ps[:, 6, at:at + P], ptok[:, t, k * P:(k + 1) * P], ident[:, :])
                ins.then_inc(sem("p_turned"), 1)

            def pool_mm():
                pe.wait_ge(sem("pool_r"), 1)
                pe.wait_ge(sem("pw_in"), 32)
                for g in range(4):
                    ins = pe.matmul(ps[:, 4 + g // 2, (g % 2) * T:(g % 2 + 1) * T], pw[:, g, :], pr[:, g, :],
                                    start=True, stop=True)
                ins.then_inc(sem("pool_mmed"), 1)

            def ab_turn(b):
                pe.wait_ge(sem("ab_onorm"), b + 1)
                pe.wait_ge(sem("att1_PT"), 6)
                for h in range(4):
                    ins = pe.transpose(ps[:, 6 + b, h * P:(h + 1) * P], ob[:, b, h, :], ident[:, :])
                ins.then_inc(sem("ab_oturned"), 1)

            def gla_low():
                pe.wait_ge(sem("norm_lo"), 6 * KD)
                out = ps[0:GR, 6, 0:T]
                for k in range(KD):
                    pe.matmul(out, wlow[1][:, k, :], hhi[:, k, :], start=k == 0, stop=False)
                    pe.matmul(out, wlow[1][:, k, :], hlo[:, k, :], start=False, stop=False)
                    ins = pe.matmul(out, wlow[2][:, k, :], hhi[:, k, :], start=False, stop=k == KD - 1)
                ins.then_inc(sem("gla_lowed"), 1)

            def gla_gate():
                pe.wait_ge(sem("gla_gkT"), 1)
                pe.wait_ge(sem("gla_par"), 32)
                for t in range(TT):
                    pe.matmul(ps[:, t, :], ones[0:1, :], bgk[:, :], start=True, stop=False)
                    pe.matmul(ps[:, t, :], gkT[0:GR, t * P:(t + 1) * P], wgu[:, :], start=False, stop=True)\
                      .then_inc(sem("gla_gated"), 1)

            def gla_cum():
                pe.wait_ge(sem("gla_la"), 1)
                for b in range(2):
                    for h in (2 * b, 2 * b + 1):
                        for t in range(TT):
                            at = (h % 2) * T + t * P
                            ins = pe.matmul(ps[:, 6 + b, at:at + P], gla[:, t, h * P:(h + 1) * P], tri64[:, :],
                                            start=True, stop=True)
                    ins.then_inc(sem("gla_cummed"), 1)

            def gla_pairs(l):
                if l == 0:
                    pe.wait_ge(sem("gla_b"), 2)
                    for r in gla_qk_ready:
                        pe.wait_ge(*r)
                else:
                    pe.wait_ge(sem("gla_C"), l)
                    pe.wait_ge(sem("gla_took"), l)
                for t in range(TT):
                    for h in range(GH):
                        c_ = slice(t * P, (t + 1) * P)
                        lhs = Cl[:, h, c_] if l else gqT[:, GH + h, c_]
                        rhs = Cl[:, h, c_] if l else gqT[:, h, c_]
                        ins = pe.matmul(ps[:, 6 + t, h * P:(h + 1) * P], lhs, rhs, start=True, stop=True)
                    ins.then_inc(sem("gla_paired"), 1)

            def gla_ktok():
                pe.wait_ge(sem("gla_C"), 7)
                pe.wait_ge(sem("gla_took"), 7)
                for t in range(TT):
                    for h in range(GH):
                        ins = pe.transpose(ps[:, 6 + t, h * P:(h + 1) * P], Cl[:, h, t * P:(t + 1) * P], ident[:, :])
                    ins.then_inc(sem("gla_kturned"), 1)

            def gla_chunk(c):
                t, p0 = c // 2, CH * (c % 2)
                own_ = slice(p0, p0 + CH)
                if c == 0:
                    pe.wait_ge(*gla_v_ready[0])
                    pe.wait_ge(*gla_v_ready[1])
                    pe.wait_ge(sem("gla_kdt"), 2)
                else:
                    pe.wait_ge(sem("gla_S"), min(c, NCH - 1))
                for h in range(GH):
                    out = ps[own_, 2 * t + h // 2, (h % 2) * GV:(h % 2 + 1) * GV]
                    if c:
                        pe.matmul(out, gqT[:, h, c * CH:(c + 1) * CH], GS[:, h, :], start=True, stop=False)
                    ins = pe.matmul(out, attn[own_, t * GH + h, own_], vg[own_, t, h * GV:(h + 1) * GV],
                                    start=c == 0, stop=True)
                ins.then_inc(sem("gla_o"), 1)
                if c < NCH - 1:
                    for b in range(2):
                        for h in (2 * b, 2 * b + 1):
                            ins = pe.matmul(ps[:, 6 + b, (h % 2) * GV:(h % 2 + 1) * GV], kdt[own_, t * GH + h, :],
                                            vg[own_, t, h * GV:(h + 1) * GV], start=True, stop=True)
                        ins.then_inc(sem("gla_supd"), 1)

            def gla_turn(t):
                pe.wait_ge(sem("gla_onorm"), t + 1)
                if t:
                    for ready in gla_g_ready:
                        pe.wait_ge(*ready)
                else:
                    pe.wait_ge(sem("gla_S"), NCH - 1)
                for b in range(2):
                    for i in range(4):
                        at = (4 * b + i) * P
                        h, d0 = at // GV, at % GV
                        ins = pe.transpose(ps[:, 6 - 2 * t + b, i * P:(i + 1) * P], og[t][:, h, d0:d0 + P], ident[:, :])
                    ins.then_inc(sem("gla_oturned"), 1)

            gla_g_ready = [took(s[2]) for s in order if s[0] == "gla_g"][-2:]
            ab_qk_ready = [took(s[2]) for s in order if s[0] == "ab_qk"][2:]
            ab_v_ready = [took(s[1] - 1) for s in order if s[0] == "ab_v"][0]
            gla_qk_ready = [took(s[2]) for s in order if s[0] == "gla_qk"][2:]
            v0 = [s[1] for s in order if s[0] == "gla_v"][0] - 3
            gla_v_ready = [(sem(g), v + 1) for g, v in units[v0]["free"]]
            parts = dict(mm=mm, norm=norm, params=params, small=small, small_turn=small_turn, fox_turn=fox_turn, fox_cum=fox_cum,
                         att_scores=att_scores, att_turn=att_turn, att_values=att_values,
                         dn_square=dn_square, dn_cum=dn_cum, dn_tok=dn_tok, dn_decay=dn_decay, dn_kk=dn_kk,
                         dn_x0=dn_x0, dn_y=dn_y, dn_z=dn_z, dn_sol=dn_sol, dn_new=dn_new, dn_state=dn_state,
                         dn_out=dn_out, dn_unit=dn_unit, ple_p=ple_p, pool_mm=pool_mm, ab_turn=ab_turn, gla_low=gla_low,
                         gla_gate=gla_gate, gla_cum=gla_cum, gla_pairs=gla_pairs, gla_ktok=gla_ktok,
                         gla_chunk=gla_chunk, gla_turn=gla_turn)
            pe.wait_ge(sem("constants"), made["ident"])
            for s in order:
                if s[0] == "params":
                    pe.wait_ge(sem("constants"), made["all"])
                if s[0] in parts:
                    parts[s[0]](*s[1:])


_INS = ["x", "p", "g_mix", "w_in", "b_fox_f", "fox_q_gain", "fox_k_gain", "sc_conv_w", "dn_conv_w", "dn_a_log",
        "dn_dt_bias", "dn_norm_gain", "w_branch", "w_o", "g_ffn", "w_up", "ffn_conv_w", "w_down", "g_ple",
        "w_ple_gate", "w_ple", "norm_mix_2", "norm_ffn_2", "norm_final_2", "ab_w_in_2", "ab_lambda_2",
        "ab_subln_2", "pool_w_2", "pool_scale_2", "ab_w_out_2", "gla_w_in_2", "gla_w_gk_up_2", "gla_b_gk_2",
        "gla_norm_2", "gla_w_out_2", "ffn_w1_2", "ffn_w2_2"]


def kernel(**inputs):
    import numpy as _np
    import concourse.bacc as _bacc
    from concourse import mybir as _mybir
    from concourse.bass_utils import run_bass_kernel_spmd as _run

    nc = _bacc.Bacc("TRN2", target_bir_lowering=False, num_devices=1)
    arrays, args = {}, {}
    for name in _INS:
        v = _np.ascontiguousarray(inputs[name])
        arrays[f"in_{name}"] = v
        args[name] = nc.dram_tensor(f"in_{name}", v.shape, _mybir.dt.from_np(v.dtype), kind="ExternalInput").ap()
    shape = inputs["x"].shape
    args["out"] = nc.dram_tensor("out_0", shape, _mybir.dt.from_np(_np.dtype("float32")), kind="ExternalOutput").ap()
    build(nc, args)
    r = _run(nc, [arrays], core_ids=[0])
    return r.results[0]["out_0"]
```
